# Optimizing a Trainium2 kernel written in Bass

```python
import jax
import jax.numpy as jnp
from jax import lax
import numpy as np

D_MODEL = 1024
BATCH = 1
SEQ = 512
DEPTH = 1
DEC_BATCH = 1
DEC_SEQ = 32
PAST_LEN = 1024

CHUNK = 64
LEFT_CHUNKS = 8
ATT_WINDOW = LEFT_CHUNKS * CHUNK
A_HEADS = 8
A_HEAD_DIM = 64
A_WIDTH = A_HEADS * A_HEAD_DIM
REL_CLIP = 128
R_HEADS = 4
R_KEY_DIM = 128
R_VAL_DIM = 128
R_WIDTH = R_HEADS * R_VAL_DIM
ROPE_BASE = 10000.0
D_FF = 4 * D_MODEL
NORM_EPS = 1e-6
GN_EPS = 1e-6

IN_SPLITS = (A_WIDTH, A_WIDTH, A_WIDTH, R_HEADS * R_KEY_DIM, R_HEADS * R_KEY_DIM, R_WIDTH, R_WIDTH, D_MODEL, D_MODEL)
IN_COLS = sum(IN_SPLITS)
IN_OFFSETS = tuple(int(o) for o in np.cumsum(IN_SPLITS)[:-1])

kernel_name = 'chunkband_relbias_attn_retention_hybrid_step'

def rms_norm(x, g):
    xf = x.astype(jnp.float32)
    y = xf * lax.rsqrt(jnp.mean(xf * xf, axis=-1, keepdims=True) + NORM_EPS)
    return (y * g.astype(jnp.float32)).astype(x.dtype)

def rotary(x, pos):
    half = x.shape[-1] // 2
    inv = ROPE_BASE ** (-jnp.arange(half, dtype=jnp.float32) / half)
    ang = pos[:, None] * inv[None, :]
    cos = jnp.cos(ang)[:, None, :]
    sin = jnp.sin(ang)[:, None, :]
    xf = x.astype(jnp.float32)
    x1, x2 = xf[..., :half], xf[..., half:]
    return jnp.concatenate([x1 * cos - x2 * sin, x1 * sin + x2 * cos], axis=-1).astype(x.dtype)

def retention_log_decay():
    return jnp.log1p(-jnp.exp2(-5.0 - jnp.arange(R_HEADS, dtype=jnp.float32)))

def mixer_inputs(h, pos, w_in):
    B, T, _ = h.shape
    z = h @ w_in
    qa, ka, va, qr, kr, vr, gr, ga, gb = jnp.split(z, IN_OFFSETS, axis=-1)
    qa = qa.reshape(B, T, A_HEADS, A_HEAD_DIM)
    ka = ka.reshape(B, T, A_HEADS, A_HEAD_DIM)
    va = va.reshape(B, T, A_HEADS, A_HEAD_DIM)
    qr = rotary(qr.reshape(B, T, R_HEADS, R_KEY_DIM), pos)
    kr = rotary(kr.reshape(B, T, R_HEADS, R_KEY_DIM), pos) * (R_KEY_DIM ** -0.5)
    vr = vr.reshape(B, T, R_HEADS, R_VAL_DIM)
    return qa, ka, va, qr, kr, vr, gr, ga, gb

def chunk_attention_prompt(q, k, v, table):
    B, S, H, dh = q.shape
    nc = S // CHUNK
    band = LEFT_CHUNKS + 1
    pad = ((0, 0), (ATT_WINDOW, 0), (0, 0), (0, 0))
    kc = jnp.pad(k, pad).reshape(B, nc + LEFT_CHUNKS, CHUNK, H, dh)
    vc = jnp.pad(v, pad).reshape(B, nc + LEFT_CHUNKS, CHUNK, H, dh)
    kb = jnp.concatenate([kc[:, i:i + nc] for i in range(band)], axis=2)
    vb = jnp.concatenate([vc[:, i:i + nc] for i in range(band)], axis=2)
    qc = q.reshape(B, nc, CHUNK, H, dh)
    s = jnp.einsum('bnqhd,bnkhd->bnhqk', qc, kb, preferred_element_type=jnp.float32) * (dh ** -0.5)
    r = jnp.arange(band * CHUNK)
    dist = jnp.arange(CHUNK)[:, None] - r[None, :] + ATT_WINDOW
    bias = table[:, jnp.clip(dist, -REL_CLIP, REL_CLIP) + REL_CLIP].astype(jnp.float32)
    valid = (jnp.arange(nc)[:, None] * CHUNK - ATT_WINDOW + r[None, :]) >= 0
    s = jnp.where(valid[None, :, None, None, :], s + bias[None, None], -jnp.inf)
    p = jax.nn.softmax(s, axis=-1).astype(v.dtype)
    o = jnp.einsum('bnhqk,bnkhd->bnqhd', p, vb)
    return o.reshape(B, S, H, dh)

def chunk_attention_sample(q, k_new, v_new, k_cache, v_cache, table):
    L = k_cache.shape[1]
    T = q.shape[1]
    k = jnp.concatenate([k_cache.astype(k_new.dtype), k_new], axis=1)
    v = jnp.concatenate([v_cache.astype(v_new.dtype), v_new], axis=1)
    s = jnp.einsum('bqhd,bkhd->bhqk', q, k, preferred_element_type=jnp.float32) * (A_HEAD_DIM ** -0.5)
    dist = jnp.arange(T)[:, None] - (jnp.arange(L + T)[None, :] - L)
    bias = table[:, jnp.clip(dist, -REL_CLIP, REL_CLIP) + REL_CLIP].astype(jnp.float32)
    p = jax.nn.softmax(s + bias[None], axis=-1).astype(v.dtype)
    return jnp.einsum('bhqk,bkhd->bqhd', p, v)

def retention_block(q, k, v, state, lg):
    T = q.shape[1]
    qf = q.astype(jnp.float32)
    kf = k.astype(jnp.float32)
    vf = v.astype(jnp.float32)
    idx = jnp.arange(T, dtype=jnp.float32)
    diff = idx[:, None] - idx[None, :]
    decay = jnp.where(diff[None] >= 0, jnp.exp(jnp.maximum(diff, 0.0)[None] * lg[:, None, None]), 0.0)
    s = jnp.einsum('bthd,bshd->bhts', qf, kf) * decay[None]
    intra = jnp.einsum('bhts,bshe->bthe', s, vf)
    cross = jnp.einsum('bthd,bhde->bthe', qf, state) * jnp.exp((idx + 1.0)[:, None] * lg[None, :])[None, :, :, None]
    kdec = kf * jnp.exp((T - 1.0 - idx)[:, None] * lg[None, :])[None, :, :, None]
    new_state = state * jnp.exp(T * lg)[None, :, None, None] + jnp.einsum('bthd,bthe->bhde', kdec, vf)
    return intra + cross, new_state

def retention_prompt(q, k, v, lg):
    B, S, H, dk = q.shape
    nc = S // CHUNK

    def to_chunks(t):
        return jnp.moveaxis(t.reshape(B, nc, CHUNK, H, t.shape[-1]), 1, 0)

    def step(state, qkv):
        o, state = retention_block(qkv[0], qkv[1], qkv[2], state, lg)
        return state, o

    s0 = jnp.zeros((B, H, dk, R_VAL_DIM), jnp.float32)
    s_fin, o = lax.scan(step, s0, (to_chunks(q), to_chunks(k), to_chunks(v)))
    return jnp.moveaxis(o, 0, 1).reshape(B, S, H, R_VAL_DIM), s_fin

def head_group_norm(o):
    mu = jnp.mean(o, axis=-1, keepdims=True)
    var = jnp.mean(jnp.square(o - mu), axis=-1, keepdims=True)
    return (o - mu) * lax.rsqrt(var + GN_EPS)

def mixer_output(att, ret, gr, ga, gb, w_attn_out, w_ret_out, w_o):
    B, T = att.shape[:2]
    dt = att.dtype
    ya = att.reshape(B, T, A_WIDTH) @ w_attn_out
    rn = head_group_norm(ret) * jax.nn.silu(gr.astype(jnp.float32)).reshape(B, T, R_HEADS, R_VAL_DIM)
    yr = rn.astype(dt).reshape(B, T, R_WIDTH) @ w_ret_out
    m = jax.nn.sigmoid(ga) * ya + jax.nn.sigmoid(gb) * yr
    return m @ w_o

def block_tail(x, mix, g_mix_post, g_ffn_pre, g_ffn_post, w_up, w_down):
    x = x + rms_norm(mix, g_mix_post)
    h = rms_norm(x, g_ffn_pre)
    f = jnp.square(jax.nn.relu(h @ w_up)) @ w_down
    return x + rms_norm(f, g_ffn_post)

def setup_inputs(seed: int = 0) -> dict:
    key = jax.random.key(seed)
    ks = jax.random.split(key, 18)

    def nrm(k, shape, scale):
        return scale * jax.random.normal(k, shape, jnp.float32)

    cache_len = min(ATT_WINDOW, PAST_LEN)
    return {
        'x_prompt': nrm(ks[0], (BATCH, SEQ, D_MODEL), 1.0),
        'x_sample': nrm(ks[1], (DEC_BATCH, DEC_SEQ, D_MODEL), 1.0),
        'cache_attn_k': nrm(ks[2], (DEPTH, DEC_BATCH, cache_len, A_HEADS, A_HEAD_DIM), 1.0),
        'cache_attn_v': nrm(ks[3], (DEPTH, DEC_BATCH, cache_len, A_HEADS, A_HEAD_DIM), 1.0),
        'state_retention': nrm(ks[4], (DEPTH, DEC_BATCH, R_HEADS, R_KEY_DIM, R_VAL_DIM), 1.0),
        'norm_mix_pre': 1.0 + nrm(ks[5], (DEPTH, D_MODEL), 0.05),
        'w_in': nrm(ks[6], (DEPTH, D_MODEL, IN_COLS), D_MODEL ** -0.5),
        'rel_bias_table': nrm(ks[7], (DEPTH, A_HEADS, 2 * REL_CLIP + 1), 0.5),
        'w_attn_out': nrm(ks[8], (DEPTH, A_WIDTH, D_MODEL), A_WIDTH ** -0.5),
        'w_ret_out': nrm(ks[9], (DEPTH, R_WIDTH, D_MODEL), R_WIDTH ** -0.5),
        'w_o': nrm(ks[10], (DEPTH, D_MODEL, D_MODEL), D_MODEL ** -0.5),
        'norm_mix_post': 1.0 + nrm(ks[11], (DEPTH, D_MODEL), 0.05),
        'norm_ffn_pre': 1.0 + nrm(ks[12], (DEPTH, D_MODEL), 0.05),
        'w_ff_up': nrm(ks[13], (DEPTH, D_MODEL, D_FF), D_MODEL ** -0.5),
        'w_ff_down': nrm(ks[14], (DEPTH, D_FF, D_MODEL), D_FF ** -0.5),
        'norm_ffn_post': 1.0 + nrm(ks[15], (DEPTH, D_MODEL), 0.05),
    }

def reference(x_prompt, x_sample, cache_attn_k, cache_attn_v, state_retention,
              norm_mix_pre, w_in, rel_bias_table, w_attn_out, w_ret_out, w_o,
              norm_mix_post, norm_ffn_pre, w_ff_up, w_ff_down, norm_ffn_post):
    xp = x_prompt
    xs = x_sample
    S = xp.shape[1]
    T = xs.shape[1]
    pos_p = jnp.arange(S, dtype=jnp.float32)
    pos_s = PAST_LEN + jnp.arange(T, dtype=jnp.float32)
    lg = retention_log_decay()
    kp_l, vp_l, sp_l, ks_l, vs_l, ss_l = [], [], [], [], [], []
    for l in range(DEPTH):
        h = rms_norm(xp, norm_mix_pre[l])
        qa, ka, va, qr, kr, vr, gr, ga, gb = mixer_inputs(h, pos_p, w_in[l])
        att = chunk_attention_prompt(qa, ka, va, rel_bias_table[l])
        ret, s_p = retention_prompt(qr, kr, vr, lg)
        mix = mixer_output(att, ret, gr, ga, gb, w_attn_out[l], w_ret_out[l], w_o[l])
        xp = block_tail(xp, mix, norm_mix_post[l], norm_ffn_pre[l], norm_ffn_post[l], w_ff_up[l], w_ff_down[l])
        kp_l.append(ka[:, -ATT_WINDOW:])
        vp_l.append(va[:, -ATT_WINDOW:])
        sp_l.append(s_p)
        h = rms_norm(xs, norm_mix_pre[l])
        qa, ka, va, qr, kr, vr, gr, ga, gb = mixer_inputs(h, pos_s, w_in[l])
        att = chunk_attention_sample(qa, ka, va, cache_attn_k[l], cache_attn_v[l], rel_bias_table[l])
        ret, s_s = retention_block(qr, kr, vr, state_retention[l].astype(jnp.float32), lg)
        mix = mixer_output(att, ret, gr, ga, gb, w_attn_out[l], w_ret_out[l], w_o[l])
        xs = block_tail(xs, mix, norm_mix_post[l], norm_ffn_pre[l], norm_ffn_post[l], w_ff_up[l], w_ff_down[l])
        ks_l.append(ka.astype(cache_attn_k.dtype))
        vs_l.append(va.astype(cache_attn_v.dtype))
        ss_l.append(s_s.astype(state_retention.dtype))
    return (xp, xs, jnp.stack(kp_l), jnp.stack(vp_l), jnp.stack(sp_l), jnp.stack(ks_l), jnp.stack(vs_l), jnp.stack(ss_l))


_drawn_inputs = setup_inputs


def setup_inputs(seed=0):
    import zlib

    import numpy as np

    out = dict(_drawn_inputs(seed))
    spreads = {}
    factors = {}
    for name, (base, spread) in spreads.items():
        noise = np.random.default_rng([zlib.crc32(name.encode()), seed]).standard_normal(out[name].shape)
        drawn = base * np.exp(spread * noise) if base else spread * noise
        out[name] = jnp.asarray(drawn.astype(out[name].dtype))
    for name, factor in factors.items():
        out[name] = (out[name] * factor).astype(out[name].dtype)
    return out
```

```python
from contextlib import ExitStack

import concourse.bass as bass
import numpy as np
from concourse import mybir

D = 1024
P = 128
KT = D // P
SEQ, DEC = 512, 32
T = SEQ + DEC
HALF = T // 2
TILES = [(0, P), (P, P), (2 * P, P), (3 * P, P), (SEQ, DEC)]
AH, AD = 8, 64
PAIRS = AH // 2
CACHE = 512
RH, RD = 4, 128
CLIP = 128
TABLE = 2 * CLIP + 1
PAST = 1024
EPS = 1e-6
IN_COLS = 5632
D_FF = 4 * D
STAGE = 2 * P
RC = 136
NEG = -1.0e30
Z_AQ, Z_AK, Z_AV, Z_GATE, Z_SPARE, Z_RQ, Z_RK, Z_RV, Z_RG, Z_SLOTS = 0, 4, 8, 4, 12, 20, 24, 28, 32, 36


def shape_constants():
    f = np.float32
    ident = np.eye(P, dtype=f)
    flip = np.ascontiguousarray(ident[::-1])
    half = RD // 2
    inv = (f(10000.0) ** (-np.arange(half, dtype=f) / f(half))).astype(f)
    pos = np.concatenate([np.arange(SEQ), PAST + np.arange(DEC)]).astype(f)
    ang = (inv[:, None] * pos[None, :]).astype(f)
    cos = np.cos(ang.astype(np.float64)).astype(f)
    sin = np.sin(ang.astype(np.float64)).astype(f)
    rope = np.zeros((P, 2, T), f)
    rope[:half, 0] = rope[half:, 0] = cos
    rope[half:, 1] = -sin
    rope[:half, 1] = sin
    decay = np.zeros((P, RH, RC), f)
    t = np.arange(P)
    for h in range(RH):
        lg = np.log1p(-np.exp2(-5.0 - h))
        key = RD ** -0.5
        decay[:, h, :P] = np.where(t[None, :] >= t[:, None], key * np.exp(-(t[:, None] + 1.0) * lg), 0.0)
        decay[:, h, P] = np.exp((t + 1.0) * lg)
        decay[:, h, P + 1] = key * np.exp((P - 1.0 - t) * lg)
        decay[:DEC, h, P + 2] = key * np.exp((DEC - 1.0 - t[:DEC]) * lg)
        decay[:, h, P + 3] = np.exp(P * lg)
        decay[:, h, P + 4] = np.exp(DEC * lg)
    return {"ident": ident, "flip": flip, "ones": np.ones((P, P), f), "rope": rope, "decay": decay}


class Order:

    def __init__(self, eng, sem):
        self.eng, self.sem, self.base, self.n = eng, sem, 0, 0

    def after(self, ins):
        ins.then_inc(self.sem, 1)
        self.n += 1
        self.eng.wait_ge(self.sem, self.base + self.n)

    def flatten(self):
        self.base, self.n = self.base + self.n, 0

    def body(self, i, per):
        self.start = self.base
        self.base, self.n, self.per = self.start + i * per, 0, per

    def leave(self, count):
        assert self.n == self.per, (self.n, self.per)
        self.base, self.n = self.start + count * self.per, 0


def build(nc, a, outs):
    fp, fr = mybir.dt.float32, mybir.dt.float32r
    ALU, ACT, AX = mybir.AluOpType, mybir.ActivationFunctionType, mybir.AxisListType
    ctx = ExitStack()

    with ctx:
        def sem(name):
            return ctx.enter_context(nc.semaphore(name))

        arena_bytes = 212 * 1000
        arena = ctx.enter_context(nc.sbuf_tensor("arena", [P, arena_bytes // 4], fp))
        first = nc.sbuf_base - arena_bytes
        top = [first]

        def place(name, shape, dtype=fp, at=None):
            size = 4 * int(np.prod(shape[1:]))
            size += -size % 32
            where = top[0] if at is None else at
            if at is None:
                top[0] += size
                assert top[0] <= first + arena_bytes, (name, top[0] - first - arena_bytes)
            ends[name] = where + size
            return nc.alloc_sbuf_tensor_at(name, shape, dtype, offset=where)

        ends = {}
        xT = place("xT", [P, KT, T])
        act_hi = place("act_hi", [P, KT, T], fr)
        act_lo = place("act_lo", [P, KT, T], fr)
        w_raw = place("w_raw", [P, 2, KT, STAGE])
        w_hi = place("w_hi", [P, 2, KT, P], fr)
        w_lo = place("w_lo", [P, 2, KT, P], fr)
        rstd = place("rstd", [P, T])
        sqsum = place("sqsum", [P, T])
        ident = place("ident_sb", [P, P])
        ones = place("ones_sb", [P, P])
        gains = place("gains_sb", [P, 4, KT])
        tok_var = place("tok_var", [P, 8])
        tok_rstd = place("tok_rstd", [P, 8])
        rope = place("rope_sb", [P, 2, T])
        decay = place("decay_sb", [P, RH, RC])
        state_in = place("state_in", [P, RH, RD])
        z_at = top[0]
        z = place("z", [P, Z_SLOTS, T])
        work_at = top[0]

        mid_hi = place("mid_hi", [P, KT, T], fr, at=z_at + 4 * T * Z_RQ)
        mid_lo = place("mid_lo", [P, KT, T], fr, at=z_at + 4 * T * (Z_RQ + KT))
        y_mix = place("y_mix", [P, KT, T], at=z_at + 4 * T * Z_GATE)
        y_ffn = place("y_ffn", [P, KT, T], at=z_at + 4 * T * (Z_GATE + KT))
        y_out = place("y_out", [P, 5, D], at=z_at + 4 * T * Z_RQ)
        x_nat = place("x_nat", [P, 5, D], at=z_at)
        hankel = place("hankel", [P, AH, 2 * P], at=z_at + 4 * T * Z_RQ)
        k_cache = place("k_cache", [P, 4, AH * AD], at=ends["hankel"])
        table_row = place("table_row", [AH, 3 * P], at=ends["k_cache"])
        flip = place("flip_sb", [P, P], at=ends["table_row"])
        xg = place("xg", [P, 2, KT, P], at=ends["flip_sb"])
        x_waste = place("x_waste", [P, 2, D], at=ends["xg"])
        assert ends["x_nat"] <= z_at + 4 * T * Z_SPARE and ends["x_waste"] <= work_at
        bias = place("bias", [P, AH, 2 * P], at=z_at + 4 * T * Z_SPARE)
        kcT = place("kcT", [P, PAIRS, CACHE], at=ends["bias"])
        assert ends["kcT"] <= z_at + 4 * T * Z_RQ

        v_cache = place("v_cache", [P, 4, P])
        q_pad = place("q_pad", [P, 2, T])
        k_pair = place("k_pair", [P, T])
        v_pair = place("v_pair", [P, T])
        probs = place("probs", [P, 4 * P + 3 * P + 2 * P + P + CACHE + DEC])
        probsT = place("probsT", [P, 1440])
        k_nat = place("k_nat", [P, 5, P])
        v_nat = place("v_nat", [P, 5, P])
        att_nat = place("att_nat", [P, 5, P])
        neg_max = place("neg_max", [P, 8])
        row_sum = place("row_sum", [P, 8])
        row_inv = place("row_inv", [P, 8])
        att_end = top[0]

        top[0] = work_at
        head_c = place("head_c", [P, RC])
        gate_sig = place("gate_sig", [P, T])
        rq = place("rq", [P, T])
        rk = place("rk", [P, T])
        rv = place("rv", [P, T])
        rope_q = place("rope_q", [P, T])
        rope_k = place("rope_k", [P, T])
        gate_row = place("gate_row", [P, T])
        rk_nat = place("rk_nat", [P, 5, P])
        rv_nat = place("rv_nat", [P, 5, P])
        ret_a = place("ret_a", [P, 4 * P + DEC])
        states = place("states", [P, 4, RD])
        state_new = place("state_new", [P, RD])
        ret_o = place("ret_o", [P, 5, RD])
        ret_n = place("ret_n", [P, 5, RD])
        gn_stats = place("gn_stats", [P, 5, 6])
        gn_mv = place("gn_mv", [P, 5, 2])
        gn_std = place("gn_std", [P, 5])
        gn_rstd = place("gn_rstd", [P, 5])

        top[0] = work_at
        part_a = place("part_a", [P, T])
        part_b = place("part_b", [P, T])
        merged = place("merged", [P, 2, T])
        sq = place("sq", [P, 2, T])
        scaled = place("scaled", [P, 2, T])
        relu = place("relu", [P, 2, T])
        relu2 = place("relu2", [P, 2, T])

        acc = [ctx.enter_context(nc.psum_tensor(f"acc{i}", [P, 2, 512], fp)) for i in range(2)]
        wk = ctx.enter_context(nc.psum_tensor("wk", [P, 2048], fp))
        wk_halves = [wk[:, 1024 * i:1024 * i + 1024].rearrange("p (n c) -> p n c", n=2) for i in range(2)]

        table_ext = nc.dram_tensor("table_ext", (AH, 3 * P), fp, kind="Internal").ap()

        ident_in, const_in = sem("ident_in"), sem("const_in")
        x_in = [sem(f"x_in{t}") for t in range(5)]
        w_in_sem = [sem("w_loaded0"), sem("w_loaded1")]
        cache_k_in, table_in, table_filled, table_out, hankel_in = (
            sem("cache_k_in"), sem("table_in"), sem("table_filled"), sem("table_out"), sem("hankel_in"))
        x_tr, x_copied, xg_ready, x_hi, x_lo, x_sum_act, x_sum_dve, var_clear = (
            sem("x_tr"), sem("x_copied"), sem("xg_ready"), sem("x_hi"), sem("x_lo"), sem("x_sum_act"), sem("x_sum_dve"), sem("var_clear"))
        kc_tr, kc_ready, bias_mm, bias_ready = sem("kc_tr"), sem("kc_ready"), sem("bias_mm"), sem("bias_ready")
        sum_mm, var_ready, std_ready, tok_rstd_ready, spread_mm, rstd_ready = (
            sem("sum_mm"), sem("var_ready"), sem("std_ready"), sem("tok_rstd_ready"), sem("spread_mm"), sem("rstd_ready"))
        hi_ready, lo_ready, mm_done, acc_free = sem("hi_ready"), sem("lo_ready"), sem("mm_done"), sem("acc_free")
        dve_order, act_order, pool_order = sem("dve_order"), sem("act_order"), sem("pool_order")
        pair_ready, kv_tr, k_nat_ready, v_nat_ready = sem("pair_ready"), sem("kv_tr"), sem("k_nat_ready"), sem("v_nat_ready")
        scores_mm, max_ready, probs_ready = sem("scores_mm"), sem("max_ready"), sem("probs_ready")
        pT_mm, pT_a, pT_b, pT_c = sem("pT_mm"), sem("pT_a"), sem("pT_b"), sem("pT_c")
        pv_mm, att_nat_ready, att_tr, attT_ready = sem("pv_mm"), sem("att_nat_ready"), sem("att_tr"), sem("attT_ready")
        k_out, v_out, v_cache_in = sem("k_out"), sem("v_out"), sem("v_cache_in")
        ret_const_in, gate_sig_ready, swish_ready, q_rotated = sem("ret_const_in"), sem("gate_sig_ready"), sem("swish_ready"), sem("q_rotated")
        q_copied, gate_copied = sem("q_copied"), sem("gate_copied")
        ret_ready, rkv_tr, rk_nat_ready, rv_nat_ready = sem("ret_ready"), sem("rkv_tr"), sem("rk_nat_ready"), sem("rv_nat_ready")
        ret_s_mm, ret_a_ready, ret_o_mm, gn_var, gn_root = (
            sem("ret_s_mm"), sem("ret_a_ready"), sem("ret_o_mm"), sem("gn_var"), sem("gn_root"))
        ret_n_ready, ret_tr, retT_ready, state_out = sem("ret_n_ready"), sem("ret_tr"), sem("retT_ready"), sem("state_out")
        in_hi, in_lo, gates_ready, merge_ready, mid_hi_r, mid_lo_r = (
            sem("in_hi"), sem("in_lo"), sem("gates_ready"), sem("merge_ready"), sem("mid_hi_ready"), sem("mid_lo_ready"))
        sq_ready, sq_added = sem("sq_ready"), sem("sq_added")
        scaled_ready, x1_ready, h2_hi, h2_lo = sem("scaled_ready"), sem("x1_ready"), sem("h2_hi"), sem("h2_lo")
        relu2_ready, f_hi, f_lo = sem("relu2_ready"), sem("f_hi"), sem("f_lo")
        outT_ready, out_tr, y_stored, y_zero = sem("outT_ready"), sem("out_tr"), sem("y_stored"), sem("y_zero")
        out_nat = [sem("out_nat_even"), sem("out_nat_odd")]

        block = ctx.enter_context(nc.Block())

        CREDITS = {k_out: 32, v_out: 32, state_out: 32, attT_ready: 1, retT_ready: 1, sq_added: 2, f_lo: 2, acc_free: 2}

        G_RET, G_GATE, G_MERGE, G_WO, G_FFN = 3, 7, 11, 13, 15

        def halves(ap):
            return ap.rearrange("p (n c) -> p n c", n=2)

        def evacuated(eng, g, j):
            eng.wait_ge(acc_free, 4 * g + j + 3)

        w_in_v = a["w_in"].rearrange("(k p) n -> p k n", p=P)
        w_ao_v = a["w_attn_out"].rearrange("(k p) n -> p k n", p=P)
        w_ro_v = a["w_ret_out"].rearrange("(k p) n -> p k n", p=P)
        w_o_v = a["w_o"].rearrange("(k p) n -> p k n", p=P)
        w_up_v = a["w_ff_up"].rearrange("(k p) n -> p k n", p=P)
        w_dn_v = a["w_ff_down"].rearrange("(k p) n -> p k n", p=P)

        S_COL = {3: 0, 2: 512, 0: 896, 1: 1024, 4: 1504}
        P_COL = {0: 0, 1: P, 2: 3 * P, 3: 6 * P, 4: 10 * P}
        WIDTH = {0: P, 1: 2 * P, 2: 3 * P, 3: 4 * P, 4: CACHE + DEC}
        NEAR = {0: (0, P), 1: (0, 2 * P), 2: (P, 2 * P), 3: (2 * P, 2 * P), 4: (3 * P, P + DEC)}
        PT_COL = {3: 0, 2: 512, 0: 896, 1: 1024, 4: 1280}
        ORDER = (3, 2, 0, 1, 4)

        def x_psum(t):
            n = TILES[t][1]
            if t in (0, 1):
                return acc[t][:].rearrange("p n (k c) -> p (n k) c", k=4)
            if t in (2, 3):
                return wk[:, 1024 * (t - 2):1024 * (t - 1)].rearrange("p (k c) -> p k c", k=KT)
            return acc[0][:, 0, 0:KT * n].rearrange("p (k c) -> p k c", k=KT)

        def out_psum(m):
            return wk[:, 1024 * (m % 2):1024 * (m % 2) + 5 * P]

        @block.sync
        def _(sp):
            for t, (s, n) in enumerate(TILES):
                src = a["x_prompt"][0, s:s + n, :] if t < 4 else a["x_sample"][0]
                sp.dma_start(x_nat[0:n, t, :], src).then_inc(x_in[t], 16)

            def load(buf, src_a, src_b, col):
                sp.dma_start(w_raw[:, buf, 0:4, :], src_a[:, :, bass.ds(col, STAGE)]).then_inc(w_in_sem[buf], 16)
                sp.dma_start(w_raw[:, buf, 4:8, :], src_b[:, :, bass.ds(col, STAGE)]).then_inc(w_in_sem[buf], 16)

            def load_body(g, src_a, src_b, col):
                for buf in range(2):
                    sp.wait_ge(lo_ready, 4 * g - 2 + 2 * buf)
                    load(buf, src_a, src_b, col + STAGE * buf)

            load(0, w_in_v[:, 0:4], w_in_v[:, 4:8], 0)
            sp.dma_start(k_cache[:], a["cache_attn_k"].rearrange("(t p) c -> p t c", p=P)).then_inc(cache_k_in, 16)
            load(1, w_in_v[:, 0:4], w_in_v[:, 4:8], STAGE)
            sp.dma_start(rope[:], a["rope"]).then_inc(ret_const_in, 16)
            sp.dma_start(decay[:], a["decay"]).then_inc(ret_const_in, 16)
            sp.dma_start(state_in[:], a["state_retention"].rearrange("h d e -> d h e")).then_inc(ret_const_in, 16)
            with sp.Fori(1, G_MERGE) as g:
                load_body(g, w_in_v[:, 0:4], w_in_v[:, 4:8], 512 * g)
            with sp.Fori(0, 2) as i:
                load_body(i + G_MERGE, w_ao_v, w_ro_v, 512 * i)
            with sp.Fori(0, 2) as i:
                load_body(i + G_WO, w_o_v[:, 0:4], w_o_v[:, 4:8], 512 * i)
            with sp.Fori(0, 4) as c:
                with sp.Fori(0, 2) as i:
                    load_body(G_FFN + 4 * c + i, w_up_v[:, 0:4], w_up_v[:, 4:8], 1024 * c + 512 * i)
                with sp.Fori(0, 2) as i:
                    load_body(G_FFN + 2 + 4 * c + i, w_dn_v[:, bass.ds(8 * c, 4)],
                              w_dn_v[:, bass.ds(8 * c + 4, 4)], 512 * i)
            for m in range(KT):
                sp.wait_ge(out_nat[m % 2], m // 2 + 1)
                cols = slice(P * m, P * m + P)
                sp.dma_start(outs["y_prompt"][0].rearrange("(t p) c -> p t c", p=P)[:, :, cols], y_out[:, 0:4, cols]).then_inc(y_stored, 16)
                sp.dma_start(outs["y_sample"][0][:, cols], y_out[0:DEC, 4, cols]).then_inc(y_stored, 16)
            sp.wait_ge(y_stored, 32 * KT)

        @block.gpsimd
        def _(pool):
            order = Order(pool, pool_order)
            pool.dma_start(table_row[:, 0:TABLE], a["rel_bias_table"]).then_inc(table_in, 16)
            pool.wait_ge(table_in, 16)
            pool.tensor_copy(table_row[:, TABLE:3 * P],
                             table_row[:, TABLE - 1:TABLE].to_broadcast([AH, 3 * P - TABLE])).then_inc(table_filled, 1)
            pool.wait_ge(table_filled, 1)
            pool.dma_start(table_ext, table_row[:]).then_inc(table_out, 16)
            pool.wait_ge(table_out, 16)
            pool.dma_start(hankel[:], bass.AP(table_ext.tensor, 1, [[1, P], [3 * P, AH], [1, 2 * P]])).then_inc(hankel_in, 16)
            pool.wait_ge(ret_const_in, 48)
            pool.wait_ge(acc_free, 2 + 4 * G_GATE)
            pool.wait_ge(attT_ready, PAIRS + 1)
            pool.wait_ge(k_out, 32 * PAIRS + 32)
            pool.wait_ge(v_out, 32 * PAIRS + 32)

            with pool.Fori(0, RH) as i:
                order.body(i, 3)
                pool.wait_ge(q_copied, i + 1)
                for to, frm in ((0, RD // 2), (RD // 2, 0)):
                    order.after(pool.tensor_tensor(rope_q[to:to + RD // 2, :], rq[frm:frm + RD // 2, :], rope[frm:frm + RD // 2, 1, :], ALU.mult))
                order.after(pool.tensor_tensor(rq[:], rq[:], rope[:, 0, :], ALU.mult))
                pool.tensor_tensor(rq[:], rq[:], rope_q[:], ALU.add).then_inc(q_rotated, 1)
                pool.wait_ge(gate_sig_ready, i + 1)
                pool.tensor_tensor(gate_row[:], gate_row[:], gate_sig[:], ALU.mult).then_inc(swish_ready, 1)
            order.leave(RH)
            pool.wait_ge(state_out, 32 * RH + 32)

            def add_squares(norm):
                if norm > 1:
                    pool.wait_ge(sum_mm, norm - 1)
                order.after(pool.memset(sqsum[:], 0.0))
                for m in range(KT):
                    k = KT * (norm - 1) + m
                    pool.wait_ge(sq_ready, k + 1)
                    ins = pool.tensor_tensor(sqsum[:], sqsum[:], sq[:, m % 2, :], ALU.add)
                    ins.then_inc(sq_added, 1)
                    pool.wait_ge(sq_added, k + 3)

            pool.wait_ge(mid_lo_r, KT)
            pool.memset(y_ffn[:], 0.0).then_inc(y_zero, 1)
            add_squares(1)
            pool.wait_ge(sum_mm, 1)
            order.after(pool.memset(sqsum[:], 0.0))
            for m in range(KT):
                pool.wait_ge(scaled_ready, m + 1)
                pool.tensor_tensor(xT[:, m, :], xT[:, m, :], scaled[:, m % 2, :], ALU.add).then_inc(x1_ready, 1)
                pool.wait_ge(sq_ready, KT + m + 1)
                pool.tensor_tensor(sqsum[:], sqsum[:], sq[:, m % 2, :], ALU.add).then_inc(sq_added, 1)
                pool.wait_ge(sq_added, KT + m + 3)
            add_squares(3)
            for m in range(KT):
                pool.wait_ge(scaled_ready, KT + m + 1)
                pool.tensor_tensor(y_ffn[:, m, :], xT[:, m, :], scaled[:, m % 2, :], ALU.add).then_inc(outT_ready, 1)

        @block.scalar
        def _(act):
            order = Order(act, act_order)

            def split_hi(u, v, wait_load=None):
                if wait_load is not None:
                    act.wait_ge(w_in_sem[v // 2], wait_load)
                act.activation(w_hi[:, v % 2], w_raw[:, v // 2, :, P * (v % 2):P * (v % 2) + P], ACT.Copy).then_inc(hi_ready, 1)

            def split_ahead(g, j):
                act.wait_ge(mm_done, 4 * g + j + 1)
                v = (j + 2) % 4
                split_hi(4 * g + j + 2, v, {0: 32 * (g + 1), 2: 32 * (g + 2)}.get(j))

            act.dma_start(ident[:], a["ident"]).then_inc(ident_in, 16)
            act.dma_start(gains[:], a["gains"]).then_inc(const_in, 16)
            act.dma_start(ones[:], a["ones"]).then_inc(const_in, 16)
            act.dma_start(flip[:], a["flip"]).then_inc(const_in, 16)
            for counter, n in CREDITS.items():
                act.sem_inc(counter, n)
            for t, (s, n) in enumerate(TILES):
                if t == 0:
                    act.wait_ge(var_clear, 1)
                if t < 2:
                    act.wait_ge(x_in[t], 16)
                    act.activation(x_waste[0:n, 0, :], x_nat[0:n, t, :], ACT.Square, accum_out=tok_var[0:n, t:t + 1]).then_inc(x_sum_act, 1)
                act.wait_ge(x_tr, t + 1)
                act.activation(xT[:, :, s:s + n], x_psum(t), ACT.Copy).then_inc(x_copied, 1)
                act.wait_ge(xg_ready, t + 1)
                act.activation(act_hi[:, :, s:s + n], xg[:, t % 2, :, 0:n], ACT.Copy).then_inc(x_hi, 1)
                if t == 3:
                    split_hi(0, 0, 32)
            split_hi(1, 1)

            def root(norm):
                act.wait_ge(var_ready, norm + 1)
                act.activation(tok_rstd[:, 0:5], tok_var[:, 0:5], ACT.Sqrt).then_inc(std_ready, 1)

            root(0)
            act.wait_ge(kc_tr, 1)
            act.activation(kcT[:], wk[:].rearrange("p (a b) -> p a b", a=PAIRS), ACT.Copy).then_inc(kc_ready, 1)

            with act.Fori(0, G_RET) as g:
                for j in range(4):
                    split_ahead(g, j)

            def exps(i, e):
                for k, t in enumerate(ORDER):
                    n = TILES[t][1]
                    if k in (0, 1, 3):
                        act.wait_ge(max_ready, 6 * i + 3 * e + (1, 2, 2, 3, 3)[k])
                    act.activation(probs[0:n, P_COL[t]:P_COL[t] + WIDTH[t]], wk[0:n, S_COL[t]:S_COL[t] + WIDTH[t]],
                                   ACT.Exp, bias=neg_max[0:n, t:t + 1], accum_out=row_sum[0:n, t:t + 1]).then_inc(probs_ready, 1)

            def probsT_copy(i, e):
                act.wait_ge(pT_mm, 6 * i + 3 * e + 2)
                act.activation(probsT[:, 512:1024], wk[:, 512:1024], ACT.Copy).then_inc(pT_b, 1)

            def store_kv(i):
                for nat, ready, stored, name in ((k_nat, k_nat_ready, k_out, "new_k"), (v_nat, v_nat_ready, v_out, "new_v")):
                    act.wait_ge(ready, i + 1)
                    act.dma_start(outs[name + "_prompt"].rearrange("(t p) c -> p t c", p=P)[:, :, bass.ds(P * i, P)],
                                  nat[:, 0:4, :]).then_inc(stored, 16)
                    act.dma_start(outs[name + "_sample"][:, bass.ds(P * i, P)], nat[0:DEC, 4, :]).then_inc(stored, 16)

            with act.Fori(0, PAIRS) as i:
                g = i + G_RET
                act.wait_ge(attT_ready, i + 1)
                act.dma_start(v_cache[:], a["cache_attn_v"].rearrange("(t p) c -> p t c", p=P)[:, :, bass.ds(P * i, P)])\
                    .then_inc(v_cache_in, 16)
                split_ahead(g, 0)
                act.wait_ge(kv_tr, i + 1)
                act.wait_ge(v_out, 32 * i + 32)
                act.activation(v_nat[:, 0:4, :], wk[:, 1024:1536].rearrange("p (t c) -> p t c", t=4), ACT.Copy)
                act.activation(v_nat[0:DEC, 4, :], wk[0:DEC, 1536:1664], ACT.Copy).then_inc(v_nat_ready, 1)
                split_ahead(g, 1)
                store_kv(i)
                exps(i, 0)
                probsT_copy(i, 0)
                split_ahead(g, 2)
                exps(i, 1)
                probsT_copy(i, 1)
                split_ahead(g, 3)

            with act.Fori(0, RH) as i:
                g = i + G_GATE
                split_ahead(g, 0)
                act.wait_ge(gate_copied, i + 1)
                act.activation(gate_sig[:], gate_row[:], ACT.Sigmoid).then_inc(gate_sig_ready, 1)
                act.wait_ge(rkv_tr, i + 1)
                act.activation(rv_nat[:, 0:4, :], wk[:, 1024:1536].rearrange("p (t c) -> p t c", t=4), ACT.Copy)
                act.activation(rv_nat[0:DEC, 4, :], wk[0:DEC, 1536:1664], ACT.Copy).then_inc(rv_nat_ready, 1)
                split_ahead(g, 1)
                act.wait_ge(ret_a_ready, i + 1)
                act.dma_start(outs["new_state_prompt"][bass.ds(i, 1)].rearrange("h d e -> (h d) e"), states[:, 3, :]).then_inc(state_out, 16)
                act.dma_start(outs["new_state_sample"][bass.ds(i, 1)].rearrange("h d e -> (h d) e"), state_new[:]).then_inc(state_out, 16)
                split_ahead(g, 2)
                act.wait_ge(gn_var, i + 1)
                act.activation(gn_std[:, 0:4], gn_std[:, 0:4], ACT.Sqrt)
                act.activation(gn_std[0:DEC, 4:5], gn_std[0:DEC, 4:5], ACT.Sqrt).then_inc(gn_root, 1)
                split_ahead(g, 3)

            act.wait_ge(mm_done, 4 * G_MERGE)
            for k in range(KT):
                if k == 4:
                    act.wait_ge(retT_ready, RH + 1)
                if k == 0:
                    act.wait_ge(attT_ready, PAIRS + 1)
                act.activation(act_hi[:, k, :], z[:, k if k < 4 else Z_RQ + k - 4, :], ACT.Copy).then_inc(in_hi, 1)
            act.wait_ge(acc_free, 2 + 4 * G_MERGE)
            with act.Fori(0, 2) as i:
                for j in range(4):
                    m = 4 * i + j
                    act.activation(z[:, bass.ds(Z_GATE + m, 1), :], z[:, bass.ds(Z_GATE + m, 1), :], ACT.Sigmoid)
                    act.activation(z[:, bass.ds(Z_GATE + KT + m, 1), :], z[:, bass.ds(Z_GATE + KT + m, 1), :], ACT.Sigmoid)\
                        .then_inc(gates_ready, 1)
                    split_ahead(i + G_MERGE, j)
                    act.wait_ge(merge_ready, m + 1)
                    act.activation(mid_hi[:, m, :], merged[:, j % 2, :], ACT.Copy).then_inc(mid_hi_r, 1)

            with act.Fori(0, 2) as i:
                for j in range(4):
                    split_ahead(i + G_WO, j)
                    evacuated(act, i + G_WO, j)
                    act.wait_ge(sq_added, 4 * i + j + 1)
                    act.activation(sq[:, j % 2, :], y_mix[:, 4 * i + j, :], ACT.Square).then_inc(sq_ready, 1)
            root(1)
            for m in range(KT):
                act.wait_ge(x1_ready, m + 1)
                act.activation(act_hi[:, m, :], xT[:, m, :], ACT.Copy, scale=gains[:, 2, m:m + 1]).then_inc(h2_hi, 1)
                act.wait_ge(sq_added, KT + m + 1)
                act.activation(sq[:, m % 2, :], xT[:, m, :], ACT.Square).then_inc(sq_ready, 1)
            root(2)

            def up(c, i):
                for j in range(4):
                    g = G_FFN + 4 * c + i
                    split_ahead(g, j)
                    k = 8 * c + 4 * i + j
                    evacuated(act, g, j)
                    act.wait_ge(f_lo, k + 1)
                    ins = act.activation(relu2[:, j % 2, :], relu[:, j % 2, :], ACT.Square)
                    ins.then_inc(relu2_ready, 1)
                    act.wait_ge(relu2_ready, k + 1)
                    act.activation(mid_hi[:, 4 * i + j, :], relu2[:, j % 2, :], ACT.Copy).then_inc(f_hi, 1)

            with act.Fori(0, 3) as c:
                with act.Fori(0, 2) as i:
                    up(c, i)
                with act.Fori(0, 2) as i:
                    for j in range(4):
                        split_ahead(G_FFN + 2 + 4 * c + i, j)
            with act.Fori(0, 2) as i:
                up(3, i)
            for m in range(KT):
                if m < KT - 2:
                    split_ahead(G_FFN + 14 + m // 4, m % 4)
                evacuated(act, G_FFN + 14 + m // 4, m % 4)
                act.wait_ge(sq_added, 2 * KT + m + 1)
                act.activation(sq[:, m % 2, :], y_ffn[:, m, :], ACT.Square).then_inc(sq_ready, 1)
            root(3)
            for m in range(1, KT, 2):
                act.wait_ge(out_tr, m + 1)
                act.activation(y_out[:, 0:4, P * m:P * m + P], out_psum(m)[:, 0:SEQ].rearrange("p (t c) -> p t c", t=4), ACT.Copy)
                act.activation(y_out[0:DEC, 4, P * m:P * m + P], out_psum(m)[0:DEC, SEQ:5 * P], ACT.Copy).then_inc(out_nat[1], 1)

        @block.tensor
        def _(pe):
            def column_tile(g, j, hi, lo, kt=range(KT), dst=None, first_=True, last=True, before=None):
                dst = acc[j % 2] if dst is None else dst
                if first_:
                    pe.wait_ge(lo_ready, 4 * g + j + 1)
                    pe.wait_ge(acc_free, 4 * g + j + 1)
                ks = list(kt)
                for k in ks:
                    if before:
                        before(k)
                    for n in range(2):
                        cols = slice(HALF * n, HALF * n + HALF)
                        pe.matmul(dst[:, n, 0:HALF], w_hi[:, j % 2, k, :], hi[:, k, cols], start=(k == ks[0]), stop=False)
                    for n in range(2):
                        cols = slice(HALF * n, HALF * n + HALF)
                        pe.matmul(dst[:, n, 0:HALF], w_hi[:, j % 2, k, :], lo[:, k, cols], start=False, stop=False)
                    for n in range(2):
                        cols = slice(HALF * n, HALF * n + HALF)
                        ins = pe.matmul(dst[:, n, 0:HALF], w_lo[:, j % 2, k, :], hi[:, k, cols], start=False, stop=(k == ks[-1]))
                if last:
                    ins.then_inc(mm_done, 1)

            def tr(out, in_):
                n = in_.shape[0]
                return pe.transpose(out, in_, ident[0:n, 0:n])

            pe.wait_ge(ident_in, 16)
            for t, (s, n) in enumerate(TILES):
                pe.wait_ge(x_in[t], 16)
                if t == 4:
                    pe.wait_ge(x_copied, 1)
                ps = x_psum(t)
                for k in range(KT):
                    ins = tr(ps[:, k, :], x_nat[0:n, t, P * k:P * k + P])
                ins.then_inc(x_tr, 1)
            pe.wait_ge(cache_k_in, 16)
            pe.wait_ge(x_copied, 4)
            for p in range(PAIRS):
                for t in range(4):
                    ins = tr(wk[:, 512 * p + P * t:512 * p + P * t + P], k_cache[:, t, P * p:P * p + P])
            ins.then_inc(kc_tr, 1)
            def feature_sum(norm):
                for t, (s, n) in enumerate(TILES):
                    ins = pe.matmul(wk[0:n, 1024 + t:1025 + t], sqsum[:, s:s + n], ones[:, 0:1], start=True, stop=True)
                ins.then_inc(sum_mm, 1)

            def spread(norm):
                pe.wait_ge(tok_rstd_ready, norm + 1)
                for t, (s, n) in enumerate(TILES):
                    ins = pe.matmul(wk[:, s:s + n], tok_rstd[0:n, t:t + 1].to_broadcast([n, P]), ident[0:n, 0:n], start=True, stop=True)
                ins.then_inc(spread_mm, 1)

            pe.wait_ge(kc_ready, 1)
            spread(0)
            pe.wait_ge(x_copied, 5)
            pe.wait_ge(x_lo, 5)
            with pe.Fori(0, G_RET) as g:
                for j in range(4):
                    column_tile(g, j, act_hi, act_lo)

            pe.wait_ge(hankel_in, 16)
            pe.wait_ge(const_in, 48)
            pe.wait_ge(rstd_ready, 1)
            for h in range(AH):
                for b in range(2):
                    ins = pe.matmul(wk[:, 256 * h + P * b:256 * h + P * b + P], hankel[:, h, P * (1 - b):P * (1 - b) + P], flip[:],
                                    start=True, stop=True)
            ins.then_inc(bias_mm, 1)

            def scores(i, e):
                for t in ORDER:
                    s, n = TILES[t]
                    q = q_pad[:, e, s:s + n]
                    if t < 4:
                        ins = pe.matmul(wk[:, S_COL[t]:S_COL[t] + WIDTH[t]], q, k_pair[:, 0:WIDTH[t]], start=True, stop=True)
                    else:
                        pe.matmul(wk[0:n, 1504:1536], q, kcT[:, bass.ds(i, 1), 0:32].rearrange("p a c -> p (a c)"), start=True, stop=True)
                        pe.matmul(wk[0:n, 1536:2016], q, kcT[:, bass.ds(i, 1), 32:CACHE].rearrange("p a c -> p (a c)"), start=True, stop=True)
                        ins = pe.matmul(wk[0:n, 2016:2048], q, k_pair[:, SEQ:T], start=True, stop=True)
                ins.then_inc(scores_mm, 1)

            def probs_times_v(i, e):
                done = 0
                for k, t in enumerate(ORDER):
                    n = TILES[t][1]
                    if k in (0, 1, 3):
                        pe.wait_ge(probs_ready, 10 * i + 5 * e + (1, 3, 3, 5, 5)[k])
                    blocks = WIDTH[t] // P
                    for b in range(blocks):
                        ins = tr(wk[:, PT_COL[t] + n * b:PT_COL[t] + n * b + n], probs[0:n, P_COL[t] + P * b:P_COL[t] + P * b + P])
                    if t == 4:
                        ins = tr(wk[0:DEC, 1408:1440], probs[0:n, P_COL[t] + CACHE:P_COL[t] + CACHE + DEC])
                    if k in (0, 2, 4):
                        ins.then_inc(pT_mm, 1)
                for k, t in enumerate(ORDER):
                    n = TILES[t][1]
                    if k in (0, 1, 3):
                        pe.wait_ge((pT_a, pT_b, None, pT_c)[k], 2 * i + e + 1)
                    out = wk[0:n, 1536 + AD * t:1536 + AD * t + AD]
                    blocks = WIDTH[t] // P
                    for b in range(blocks):
                        v = v_nat[:, b, AD * e:AD * e + AD] if t < 4 else v_cache[:, b, AD * e:AD * e + AD]
                        ins = pe.matmul(out, probsT[:, PT_COL[t] + n * b:PT_COL[t] + n * b + n], v,
                                        start=(b == 0), stop=(t < 4 and b == blocks - 1))
                    if t == 4:
                        ins = pe.matmul(out, probsT[0:DEC, 1408:1440], v_nat[0:DEC, 4, AD * e:AD * e + AD], start=False, stop=True)
                ins.then_inc(pv_mm, 1)

            def to_natural(src, col):
                for t, (s, n) in enumerate(TILES):
                    ins = tr(wk[0:n, col + P * t:col + P * t + P], src[:, s:s + n])
                return ins

            with pe.Fori(0, PAIRS) as i:
                g = i + G_RET
                column_tile(g, 0, act_hi, act_lo)
                pe.wait_ge(pair_ready, i + 1)
                pe.wait_ge(bias_ready, 1)
                pe.wait_ge(attT_ready, i + 1)
                to_natural(k_pair, 0)
                to_natural(v_pair, 1024).then_inc(kv_tr, 1)
                column_tile(g, 1, act_hi, act_lo)
                pe.wait_ge(k_nat_ready, i + 1)
                pe.wait_ge(v_nat_ready, i + 1)
                scores(i, 0)
                column_tile(g, 2, act_hi, act_lo)
                pe.wait_ge(v_cache_in, 16 * i + 16)
                probs_times_v(i, 0)
                pe.wait_ge(att_nat_ready, 2 * i + 1)
                scores(i, 1)
                column_tile(g, 3, act_hi, act_lo)
                probs_times_v(i, 1)
                pe.wait_ge(att_nat_ready, 2 * i + 2)
                for t, (s, n) in enumerate(TILES):
                    ins = tr(wk[:, s:s + n], att_nat[0:n, t, :])
                ins.then_inc(att_tr, 1)

            with pe.Fori(0, RH) as i:
                g = i + G_GATE
                column_tile(g, 0, act_hi, act_lo)
                pe.wait_ge(ret_ready, i + 1)
                pe.wait_ge(retT_ready, i + 1)
                pe.wait_ge(attT_ready, PAIRS + 1)
                to_natural(rk, 0)
                to_natural(rv, 1024).then_inc(rkv_tr, 1)
                column_tile(g, 1, act_hi, act_lo)
                pe.wait_ge(q_rotated, i + 1)
                pe.wait_ge(rk_nat_ready, i + 1)
                pe.wait_ge(rv_nat_ready, i + 1)
                for t, (s, n) in enumerate(TILES):
                    pe.matmul(wk[0:n, s:s + n], rk[:, s:s + n], rq[:, s:s + n], start=True, stop=True)
                for t, (s, n) in enumerate(TILES):
                    ins = pe.matmul(wk[:, 1024 + RD * t:1024 + RD * t + RD], rk_nat[0:n, t, :], rv_nat[0:n, t, :], start=True, stop=True)
                ins.then_inc(ret_s_mm, 1)
                column_tile(g, 2, act_hi, act_lo)
                pe.wait_ge(ret_a_ready, i + 1)
                for t, (s, n) in enumerate(TILES):
                    out = wk[0:n, RD * t:RD * t + RD]
                    alone = t == 0
                    ins = pe.matmul(out, ret_a[0:n, s:s + n], rv_nat[0:n, t, :], start=True, stop=alone)
                    if t == 4:
                        ins = pe.matmul(out, rq[:, s:s + n], state_in[:, bass.ds(i, 1), :].rearrange("p a c -> p (a c)"), start=False, stop=True)
                    elif t:
                        ins = pe.matmul(out, rq[:, s:s + n], states[:, t - 1, :], start=False, stop=True)
                ins.then_inc(ret_o_mm, 1)
                column_tile(g, 3, act_hi, act_lo)
                pe.wait_ge(ret_n_ready, i + 1)
                for t, (s, n) in enumerate(TILES):
                    ins = tr(wk[:, 1024 + s:1024 + s + n], ret_n[0:n, t, :])
                ins.then_inc(ret_tr, 1)

            pe.wait_ge(retT_ready, RH + 1)
            with pe.Fori(0, 2) as i:
                for j in range(4):
                    def branch_ready(k):
                        pe.wait_ge(in_lo, k + 1)
                    column_tile(i + G_MERGE, j, act_hi, act_lo, range(4), last=False, before=branch_ready)
                    column_tile(i + G_MERGE, j, act_hi, act_lo, range(4, 8), dst=wk_halves[j % 2], first_=False, before=branch_ready)

            with pe.Fori(0, 2) as i:
                for j in range(4):
                    def merge_split(k):
                        pe.wait_ge(mid_lo_r, k + 1)
                    column_tile(i + G_WO, j, mid_hi, mid_lo, before=merge_split if j == 0 else None)
            pe.wait_ge(sq_added, KT + 2)
            feature_sum(1)
            spread(1)
            pe.wait_ge(sq_added, 2 * KT + 2)
            feature_sum(2)
            spread(2)

            def ffn(c, last):
                def h2_split(k):
                    pe.wait_ge(h2_lo, k + 1)
                with pe.Fori(0, 2) as i:
                    for j in range(4):
                        column_tile(G_FFN + 4 * c + i, j, act_hi, act_lo, before=h2_split if j == 0 else None)

                def hidden_split(k):
                    pe.wait_ge(f_lo, 8 * c + k + 3)
                with pe.Fori(0, 2) as i:
                    for j in range(4):
                        column_tile(G_FFN + 2 + 4 * c + i, j, mid_hi, mid_lo, before=hidden_split if j == 0 else None)

            with pe.Fori(0, 3) as c:
                ffn(c, False)
            ffn(3, True)
            pe.wait_ge(sq_added, 3 * KT + 2)
            feature_sum(3)
            spread(3)
            for m in range(KT):
                pe.wait_ge(outT_ready, m + 1)
                if m < 2:
                    pe.wait_ge(rstd_ready, 4)
                else:
                    pe.wait_ge(out_nat[m % 2], m // 2)
                for t, (s, n) in enumerate(TILES):
                    ins = tr(out_psum(m)[0:n, P * t:P * t + P], y_ffn[:, m, s:s + n])
                ins.then_inc(out_tr, 1)

        @block.vector
        def _(dve):
            order = Order(dve, dve_order)

            def copy(out, in_):
                return dve.tensor_scalar(out, in_, 1.0, None, ALU.mult)

            def split_lo(u, v):
                dve.wait_ge(hi_ready, u + 1)
                dve.tensor_tensor(w_lo[:, v % 2], w_raw[:, v // 2, :, P * (v % 2):P * (v % 2) + P],
                                  w_hi[:, v % 2].bitcast(fp), ALU.subtract).then_inc(lo_ready, 1)

            def split_ahead(g, j):
                split_lo(4 * g + j + 2, (j + 2) % 4)

            def to_z(g, j, slot):
                dve.wait_ge(mm_done, 4 * g + j + 1)
                dve.tensor_tensor(z[:, bass.ds(slot, 1), :].rearrange("p a (n c) -> p (a n) c", n=2),
                                  acc[j % 2][:, :, 0:HALF], halves(rstd[:]), ALU.mult).then_inc(acc_free, 1)

            dve.memset(tok_var[:], 1.0).then_inc(var_clear, 1)
            dve.memset(q_pad[:], 0.0)
            dve.wait_ge(const_in, 48)
            dve.wait_ge(var_clear, 1)
            for t, (s, n) in enumerate(TILES):
                if t >= 2:
                    dve.wait_ge(x_in[t], 16)
                    dve.scalar_tensor_tensor(x_waste[0:n, 1, :], x_nat[0:n, t, :], 1.0, x_nat[0:n, t, :], ALU.mult, ALU.mult,
                                             accum_out=tok_var[0:n, t:t + 1]).then_inc(x_sum_dve, 1)
                dve.wait_ge(x_copied, t + 1)
                dve.tensor_tensor(xg[:, t % 2, :, 0:n], xT[:, :, s:s + n],
                                  gains[:, 0, :].unsqueeze(2).to_broadcast([P, KT, n]), ALU.mult).then_inc(xg_ready, 1)
                dve.wait_ge(x_hi, t + 1)
                dve.tensor_tensor(act_lo[:, :, s:s + n], xg[:, t % 2, :, 0:n], act_hi[:, :, s:s + n].bitcast(fp), ALU.subtract)\
                    .then_inc(x_lo, 1)
                if t == 3:
                    split_lo(0, 0)
            split_lo(1, 1)

            def norm(n):
                if n:
                    dve.wait_ge(sum_mm, n)
                    dve.tensor_scalar(tok_var[:, 0:4], wk[:, 1024:1028], 1.0 / D, EPS, ALU.mult, ALU.add)
                    dve.tensor_scalar(tok_var[0:DEC, 4:5], wk[0:DEC, 1028:1029], 1.0 / D, EPS, ALU.mult, ALU.add).then_inc(var_ready, 1)
                else:
                    dve.wait_ge(x_sum_act, 2)
                    dve.wait_ge(x_sum_dve, 3)
                    dve.tensor_scalar(tok_var[:, 0:5], tok_var[:, 0:5], 1.0 / D, EPS, ALU.mult, ALU.add).then_inc(var_ready, 1)
                dve.wait_ge(std_ready, n + 1)
                dve.reciprocal(tok_rstd[:, 0:5], tok_rstd[:, 0:5]).then_inc(tok_rstd_ready, 1)
                dve.wait_ge(spread_mm, n + 1)
                dve.tensor_copy(rstd[:], wk[:, 0:T]).then_inc(rstd_ready, 1)
                dve.wait_ge(rstd_ready, n + 1)

            norm(0)
            order.flatten()

            with dve.Fori(0, G_RET) as g:
                for j in range(4):
                    to_z(g, j, 4 * g + j)
                    split_ahead(g, j)

            dve.wait_ge(bias_mm, 1)
            order.after(dve.tensor_tensor(bias[:], wk[:].rearrange("p (h c) -> p h c", h=AH),
                                          hankel[:, :, 2 * P - 1:2 * P].to_broadcast([P, AH, 2 * P]), ALU.subtract))
            dve.memset(bias[0:AD, :, P + AD:2 * P], NEG).then_inc(bias_ready, 1)
            order.flatten()

            def masked_max(i, e):
                h = 2 * i + e
                dve.wait_ge(scores_mm, h + 1)
                for group, tiles in enumerate(((3,), (2, 0), (1, 4))):
                    for t in tiles:
                        n = TILES[t][1]
                        c, w = NEAR[t]
                        near = wk[0:n, S_COL[t] + c:S_COL[t] + c + w]
                        b = P if t == 0 else 0
                        ins = dve.tensor_tensor(near, near, bias[0:n, bass.ds(h, 1), b:b + w].rearrange("p a c -> p (a c)"), ALU.add)
                    order.after(ins)
                    for t in tiles:
                        n = TILES[t][1]
                        ins = dve.tensor_reduce(neg_max[0:n, t:t + 1], wk[0:n, S_COL[t]:S_COL[t] + WIDTH[t]], AX.X, ALU.max, negate=True)
                    ins.then_inc(max_ready, 1)

            def probsT_copies(i, e):
                dve.wait_ge(pT_mm, 6 * i + 3 * e + 1)
                dve.tensor_copy(probsT[:, 0:512], wk[:, 0:512]).then_inc(pT_a, 1)
                dve.wait_ge(pT_mm, 6 * i + 3 * e + 3)
                dve.tensor_copy(probsT[:, 1024:1408], wk[:, 1024:1408])
                dve.tensor_copy(probsT[0:DEC, 1408:1440], wk[0:DEC, 1408:1440]).then_inc(pT_c, 1)

            def att_to_natural(i, e):
                dve.wait_ge(probs_ready, 10 * i + 5 * e + 5)
                dve.reciprocal(row_inv[:, 0:4], row_sum[:, 0:4])
                order.after(dve.reciprocal(row_inv[0:DEC, 4:5], row_sum[0:DEC, 4:5]))
                dve.wait_ge(pv_mm, 2 * i + e + 1)
                dve.tensor_tensor(att_nat[:, 0:4, AD * e:AD * e + AD], wk[:, 1536:1792].rearrange("p (t c) -> p t c", t=4),
                                  row_inv[:, 0:4].unsqueeze(2).to_broadcast([P, 4, AD]), ALU.mult)
                dve.tensor_scalar(att_nat[0:DEC, 4, AD * e:AD * e + AD], wk[0:DEC, 1792:1856], row_inv[0:DEC, 4:5], None, ALU.mult)\
                    .then_inc(att_nat_ready, 1)

            with dve.Fori(0, PAIRS) as i:
                g = i + G_RET
                order.body(i, 8)
                for e in range(2):
                    rows = slice(AD * e, AD * e + AD)
                    dve.tensor_scalar(q_pad[rows, e, :], z[rows, bass.ds(i, 1), :].rearrange("p a c -> p (a c)"), AD ** -0.5, None, ALU.mult)
                copy(k_pair[:], z[:, bass.ds(Z_AK + i, 1), :].rearrange("p a c -> p (a c)"))
                copy(v_pair[:], z[:, bass.ds(Z_AV + i, 1), :].rearrange("p a c -> p (a c)")).then_inc(pair_ready, 1)
                to_z(g, 0, Z_RQ + 4 * i)
                split_ahead(g, 0)
                dve.wait_ge(kv_tr, i + 1)
                dve.wait_ge(k_out, 32 * i + 32)
                dve.tensor_copy(k_nat[:, 0:4, :], wk[:, 0:512].rearrange("p (t c) -> p t c", t=4))
                dve.tensor_copy(k_nat[0:DEC, 4, :], wk[0:DEC, 512:640]).then_inc(k_nat_ready, 1)
                to_z(g, 1, Z_RQ + 4 * i + 1)
                split_ahead(g, 1)
                masked_max(i, 0)
                probsT_copies(i, 0)
                att_to_natural(i, 0)
                to_z(g, 2, Z_RQ + 4 * i + 2)
                split_ahead(g, 2)
                masked_max(i, 1)
                probsT_copies(i, 1)
                att_to_natural(i, 1)
                dve.wait_ge(att_tr, i + 1)
                copy(z[:, bass.ds(i, 1), :].rearrange("p a c -> p (a c)"), wk[:, 0:T]).then_inc(attT_ready, 1)
                to_z(g, 3, Z_RQ + 4 * i + 3)
                split_ahead(g, 3)
            order.leave(PAIRS)

            dve.wait_ge(ret_const_in, 48)
            dve.wait_ge(k_out, 32 * PAIRS + 32)
            dve.wait_ge(v_out, 32 * PAIRS + 32)
            with dve.Fori(0, RH) as i:
                g = i + G_GATE
                order.body(i, 9)
                def row(slot, frm=0, to=P):
                    return z[frm:to, bass.ds(slot, 1), :].rearrange("p a c -> p (a c)")

                copy(rq[:], row(Z_RQ + i)).then_inc(q_copied, 1)
                copy(head_c[:], decay[:, bass.ds(i, 1), :].rearrange("p a c -> p (a c)"))
                for to, frm in ((0, RD // 2), (RD // 2, 0)):
                    dve.tensor_tensor(rope_k[to:to + RD // 2, :], row(Z_RK + i, frm, frm + RD // 2), rope[frm:frm + RD // 2, 1, :], ALU.mult)
                order.after(dve.tensor_tensor(rk[:], row(Z_RK + i), rope[:, 0, :], ALU.mult))
                dve.tensor_tensor(rk[:], rk[:], rope_k[:], ALU.add)
                copy(rv[:], row(Z_RV + i)).then_inc(ret_ready, 1)
                copy(gate_row[:], row(Z_RG + i)).then_inc(gate_copied, 1)
                to_z(g, 0, Z_GATE + 4 * i)
                split_ahead(g, 0)
                dve.wait_ge(rkv_tr, i + 1)
                dve.tensor_scalar(rk_nat[:, 0:4, :], wk[:, 0:512].rearrange("p (t c) -> p t c", t=4), head_c[:, P + 1:P + 2], None, ALU.mult)
                dve.tensor_scalar(rk_nat[0:DEC, 4, :], wk[0:DEC, 512:640], head_c[0:DEC, P + 2:P + 3], None, ALU.mult).then_inc(rk_nat_ready, 1)
                to_z(g, 1, Z_GATE + 4 * i + 1)
                split_ahead(g, 1)
                dve.wait_ge(ret_s_mm, i + 1)
                dve.wait_ge(state_out, 32 * i + 32)
                dve.tensor_tensor(ret_a[:, 0:SEQ].rearrange("p (t c) -> p t c", t=4), wk[:, 0:SEQ].rearrange("p (t c) -> p t c", t=4),
                                  head_c[:, 0:P].unsqueeze(1).to_broadcast([P, 4, P]), ALU.mult)
                dve.tensor_tensor(ret_a[0:DEC, SEQ:T], wk[0:DEC, SEQ:T], head_c[0:DEC, 0:DEC], ALU.mult)
                order.after(dve.tensor_copy(states[:, 0, :], wk[:, 1024:1024 + RD]))
                for t in range(1, 4):
                    order.after(dve.scalar_tensor_tensor(states[:, t, :], states[:, t - 1, :], head_c[:, P + 3:P + 4],
                                                         wk[:, 1024 + RD * t:1024 + RD * t + RD], ALU.mult, ALU.add))
                dve.scalar_tensor_tensor(state_new[:], state_in[:, bass.ds(i, 1), :].rearrange("p a c -> p (a c)"), head_c[:, P + 4:P + 5],
                                         wk[:, 1536:1536 + RD], ALU.mult, ALU.add).then_inc(ret_a_ready, 1)
                to_z(g, 2, Z_GATE + 4 * i + 2)
                dve.wait_ge(ret_o_mm, i + 1)
                dve.tensor_scalar(ret_o[:, 0:4, :], wk[:, 0:SEQ].rearrange("p (t c) -> p t c", t=4), head_c[:, P:P + 1], None, ALU.mult)
                order.after(dve.tensor_scalar(ret_o[0:DEC, 4, :], wk[0:DEC, SEQ:SEQ + RD], head_c[0:DEC, P:P + 1], None, ALU.mult))
                for t, (s, n) in enumerate(TILES):
                    ins = dve.bn_stats(gn_stats[0:n, t, :], ret_o[0:n, t, :])
                order.after(ins)
                split_ahead(g, 2)
                for t, (s, n) in enumerate(TILES):
                    ins = dve.bn_aggr(gn_mv[0:n, t, :], gn_stats[0:n, t, :])
                order.after(ins)
                dve.tensor_scalar(gn_std[:, 0:4], gn_mv[:, 0:4, 1], EPS, None, ALU.add)
                dve.tensor_scalar(gn_std[0:DEC, 4:5], gn_mv[0:DEC, 4, 1:2], EPS, None, ALU.add).then_inc(gn_var, 1)
                dve.wait_ge(gn_root, i + 1)
                dve.reciprocal(gn_rstd[:, 0:4], gn_std[:, 0:4])
                order.after(dve.reciprocal(gn_rstd[0:DEC, 4:5], gn_std[0:DEC, 4:5]))
                for t, (s, n) in enumerate(TILES):
                    ins = dve.tensor_scalar(ret_n[0:n, t, :], ret_o[0:n, t, :], gn_mv[0:n, t, 0:1], gn_rstd[0:n, t:t + 1],
                                            ALU.subtract, ALU.mult)
                ins.then_inc(ret_n_ready, 1)
                to_z(g, 3, Z_GATE + 4 * i + 3)
                split_ahead(g, 3)
                dve.wait_ge(ret_tr, i + 1)
                dve.wait_ge(swish_ready, i + 1)
                dve.tensor_tensor(z[:, bass.ds(Z_RQ + i, 1), :].rearrange("p a c -> p (a c)"), wk[:, 1024:1024 + T],
                                  gate_row[:], ALU.mult).then_inc(retT_ready, 1)
            order.leave(RH)

            for k in range(KT):
                dve.wait_ge(in_hi, k + 1)
                dve.tensor_tensor(act_lo[:, k, :], z[:, k if k < 4 else Z_RQ + k - 4, :], act_hi[:, k, :].bitcast(fp), ALU.subtract)\
                    .then_inc(in_lo, 1)
            with dve.Fori(0, 2) as i:
                for j in range(4):
                    m = 4 * i + j
                    dve.wait_ge(gates_ready, m + 1)
                    dve.wait_ge(mm_done, 4 * G_MERGE + m + 1)
                    dve.tensor_tensor(halves(part_a[:]), acc[j % 2][:, :, 0:HALF],
                                      z[:, bass.ds(Z_GATE + m, 1), :].rearrange("p a (n c) -> p (a n) c", n=2), ALU.mult)
                    ins = dve.tensor_tensor(halves(part_b[:]), wk_halves[j % 2][:, :, 0:HALF],
                                            z[:, bass.ds(Z_GATE + KT + m, 1), :].rearrange("p a (n c) -> p (a n) c", n=2), ALU.mult)
                    ins.then_inc(acc_free, 1)
                    evacuated(dve, i + G_MERGE, j)
                    dve.tensor_tensor(merged[:, j % 2, :], part_a[:], part_b[:], ALU.add).then_inc(merge_ready, 1)
                    split_ahead(i + G_MERGE, j)
                    dve.wait_ge(mid_hi_r, m + 1)
                    dve.tensor_tensor(mid_lo[:, bass.ds(m, 1), :].rearrange("p a c -> p (a c)"), merged[:, j % 2, :],
                                      mid_hi[:, bass.ds(m, 1), :].rearrange("p a c -> p (a c)").bitcast(fp), ALU.subtract).then_inc(mid_lo_r, 1)

            with dve.Fori(0, 2) as i:
                for j in range(4):
                    dve.wait_ge(mm_done, 4 * (i + G_WO) + j + 1)
                    copy(y_mix[:, bass.ds(4 * i + j, 1), :].rearrange("p a (n c) -> p (a n) c", n=2),
                                    acc[j % 2][:, :, 0:HALF]).then_inc(acc_free, 1)
                    split_ahead(i + G_WO, j)
            norm(1)

            def h2_low(m):
                dve.wait_ge(h2_hi, m + 1)
                dve.scalar_tensor_tensor(act_lo[:, m, :], xT[:, m, :], gains[:, 2, m:m + 1], act_hi[:, m, :].bitcast(fp),
                                         ALU.mult, ALU.subtract).then_inc(h2_lo, 1)

            for m in range(KT):
                if m >= 2:
                    dve.wait_ge(x1_ready, m - 1)
                dve.scalar_tensor_tensor(scaled[:, m % 2, :], y_mix[:, m, :], gains[:, 1, m:m + 1], rstd[:], ALU.mult, ALU.mult)\
                    .then_inc(scaled_ready, 1)
                if m >= 1:
                    h2_low(m - 1)
            h2_low(KT - 1)
            norm(2)

            def up(c, i):
                for j in range(4):
                    g = G_FFN + 4 * c + i
                    k = 8 * c + 4 * i + j
                    dve.wait_ge(mm_done, 4 * g + j + 1)
                    dve.scalar_tensor_tensor(halves(relu[:, j % 2, :]), acc[j % 2][:, :, 0:HALF], 0.0, halves(rstd[:]),
                                             ALU.max, ALU.mult).then_inc(acc_free, 1)
                    split_ahead(g, j)
                    dve.wait_ge(f_hi, k + 1)
                    dve.tensor_tensor(mid_lo[:, bass.ds(4 * i + j, 1), :].rearrange("p a c -> p (a c)"), relu2[:, j % 2, :],
                                      mid_hi[:, bass.ds(4 * i + j, 1), :].rearrange("p a c -> p (a c)").bitcast(fp), ALU.subtract).then_inc(f_lo, 1)

            def down_tile(g, j, m, ahead=True):
                dve.wait_ge(mm_done, 4 * g + j + 1)
                y = y_ffn[:, bass.ds(m, 1), :].rearrange("p a (n c) -> p (a n) c", n=2)
                dve.tensor_tensor(y, y, acc[j % 2][:, :, 0:HALF], ALU.add).then_inc(acc_free, 1)
                if ahead:
                    split_ahead(g, j)

            dve.wait_ge(y_zero, 1)
            with dve.Fori(0, 3) as c:
                with dve.Fori(0, 2) as i:
                    up(c, i)
                with dve.Fori(0, 2) as i:
                    for j in range(4):
                        down_tile(G_FFN + 2 + 4 * c + i, j, 4 * i + j)
            with dve.Fori(0, 2) as i:
                up(3, i)
            for m in range(KT):
                down_tile(G_FFN + 14 + m // 4, m % 4, m, m < KT - 2)
            norm(3)

            def natural(m):
                dve.wait_ge(out_tr, m + 1)
                dve.tensor_copy(y_out[:, 0:4, P * m:P * m + P], out_psum(m)[:, 0:SEQ].rearrange("p (t c) -> p t c", t=4))
                dve.tensor_copy(y_out[0:DEC, 4, P * m:P * m + P], out_psum(m)[0:DEC, SEQ:5 * P]).then_inc(out_nat[0], 1)

            for m in range(KT):
                if m >= 2:
                    dve.wait_ge(outT_ready, m - 1)
                dve.scalar_tensor_tensor(scaled[:, m % 2, :], y_ffn[:, m, :], gains[:, 3, m:m + 1], rstd[:], ALU.mult, ALU.mult)\
                    .then_inc(scaled_ready, 1)
                if m % 2 == 1 and m > 1:
                    natural(m - 3)
            natural(KT - 2)


_INS = ['x_prompt', 'x_sample', 'cache_attn_k', 'cache_attn_v', 'state_retention', 'w_in', 'rel_bias_table',
        'w_attn_out', 'w_ret_out', 'w_o', 'w_ff_up', 'w_ff_down']
_GAINS = ['norm_mix_pre', 'norm_mix_post', 'norm_ffn_pre', 'norm_ffn_post']
_OUTS = [("y_prompt", (1, SEQ, D)), ("y_sample", (1, DEC, D)), ("new_k_prompt", (SEQ, AH * AD)), ("new_v_prompt", (SEQ, AH * AD)),
         ("new_state_prompt", (RH, RD, RD)), ("new_k_sample", (DEC, AH * AD)), ("new_v_sample", (DEC, AH * AD)),
         ("new_state_sample", (RH, RD, RD))]


def kernel(**inputs):
    import concourse.bacc as bacc
    from concourse.bass_utils import run_bass_kernel_spmd

    nc = bacc.Bacc("TRN2", target_bir_lowering=False, num_devices=1)
    arrays = {}
    for name in _INS:
        a = np.ascontiguousarray(inputs[name])
        if name.startswith("cache"):
            a = a.reshape(CACHE, AH * AD)
        elif name.startswith("state"):
            a = a.reshape(RH, RD, RD)
        elif not name.startswith("x_"):
            a = a[0]
        arrays[name] = a
    arrays["gains"] = np.ascontiguousarray(np.stack([np.asarray(inputs[n])[0].reshape(KT, P).T for n in _GAINS], axis=1))
    arrays.update(shape_constants())
    args = {n: nc.dram_tensor("in_" + n, a.shape, mybir.dt.from_np(a.dtype), kind="ExternalInput").ap() for n, a in arrays.items()}
    outs = {n: nc.dram_tensor("out_" + n, s, mybir.dt.float32, kind="ExternalOutput").ap() for n, s in _OUTS}
    build(nc, args, outs)
    r = run_bass_kernel_spmd(nc, [{"in_" + n: a for n, a in arrays.items()}], core_ids=[0]).results[0]
    y_p, y_s, k_p, v_p, s_p, k_s, v_s, s_s = (r["out_" + n] for n, _ in _OUTS)
    heads = (1, 1, -1, AH, AD)
    return (y_p, y_s, k_p.reshape(heads), v_p.reshape(heads), s_p.reshape(1, 1, RH, RD, RD),
            k_s.reshape(heads), v_s.reshape(heads), s_s.reshape(1, 1, RH, RD, RD))
```

```python
from contextlib import ExitStack

import concourse.bass as bass
import numpy as np
from concourse import mybir

D = 1024
P = 128
KT = D // P
SEQ, DEC = 512, 32
T = SEQ + DEC
HALF = T // 2
TILES = [(0, P), (P, P), (2 * P, P), (3 * P, P), (SEQ, DEC)]
AH, AD = 8, 64
PAIRS = AH // 2
CACHE = 512
RH, RD = 4, 128
CLIP = 128
TABLE = 2 * CLIP + 1
PAST = 1024
EPS = 1e-6
IN_COLS = 5632
D_FF = 4 * D
STAGE = 2 * P
RC = 136
NEG = -1.0e30
Z_AQ, Z_AK, Z_AV, Z_GATE, Z_SPARE, Z_RQ, Z_RK, Z_RV, Z_RG, Z_SLOTS = 0, 4, 8, 4, 12, 20, 24, 28, 32, 36


def shape_constants():
    f = np.float32
    ident = np.eye(P, dtype=f)
    flip = np.ascontiguousarray(ident[::-1])
    half = RD // 2
    inv = (f(10000.0) ** (-np.arange(half, dtype=f) / f(half))).astype(f)
    pos = np.concatenate([np.arange(SEQ), PAST + np.arange(DEC)]).astype(f)
    ang = (inv[:, None] * pos[None, :]).astype(f)
    cos = np.cos(ang.astype(np.float64)).astype(f)
    sin = np.sin(ang.astype(np.float64)).astype(f)
    rope = np.zeros((P, 2, T), f)
    rope[:half, 0] = rope[half:, 0] = cos
    rope[half:, 1] = -sin
    rope[:half, 1] = sin
    decay = np.zeros((P, RH, RC), f)
    t = np.arange(P)
    for h in range(RH):
        lg = np.log1p(-np.exp2(-5.0 - h))
        key = RD ** -0.5
        decay[:, h, :P] = np.where(t[None, :] >= t[:, None], key * np.exp(-(t[:, None] + 1.0) * lg), 0.0)
        decay[:, h, P] = np.exp((t + 1.0) * lg)
        decay[:, h, P + 1] = key * np.exp((P - 1.0 - t) * lg)
        decay[:DEC, h, P + 2] = key * np.exp((DEC - 1.0 - t[:DEC]) * lg)
        decay[:, h, P + 3] = np.exp(P * lg)
        decay[:, h, P + 4] = np.exp(DEC * lg)
    return {"ident": ident, "flip": flip, "ones": np.ones((P, P), f), "rope": rope, "decay": decay}


class Order:

    def __init__(self, eng, sem):
        self.eng, self.sem, self.base, self.n = eng, sem, 0, 0

    def after(self, ins):
        ins.then_inc(self.sem, 1)
        self.n += 1
        self.eng.wait_ge(self.sem, self.base + self.n)

    def flatten(self):
        self.base, self.n = self.base + self.n, 0

    def body(self, i, per):
        self.start = self.base
        self.base, self.n, self.per = self.start + i * per, 0, per

    def leave(self, count):
        assert self.n == self.per, (self.n, self.per)
        self.base, self.n = self.start + count * self.per, 0


def build(nc, a, outs):
    fp, fr = mybir.dt.float32, mybir.dt.float32r
    ALU, ACT, AX = mybir.AluOpType, mybir.ActivationFunctionType, mybir.AxisListType
    ctx = ExitStack()

    with ctx:
        def sem(name):
            return ctx.enter_context(nc.semaphore(name))

        arena_bytes = 212 * 1000
        arena = ctx.enter_context(nc.sbuf_tensor("arena", [P, arena_bytes // 4], fp))
        first = nc.sbuf_base - arena_bytes
        top = [first]

        def place(name, shape, dtype=fp, at=None):
            size = 4 * int(np.prod(shape[1:]))
            size += -size % 32
            where = top[0] if at is None else at
            if at is None:
                top[0] += size
                assert top[0] <= first + arena_bytes, (name, top[0] - first - arena_bytes)
            ends[name] = where + size
            return nc.alloc_sbuf_tensor_at(name, shape, dtype, offset=where)

        ends = {}
        xT = place("xT", [P, KT, T])
        act_hi = place("act_hi", [P, KT, T], fr)
        act_lo = place("act_lo", [P, KT, T], fr)
        w_raw = place("w_raw", [P, 2, KT, STAGE])
        w_hi = place("w_hi", [P, 2, KT, P], fr)
        w_lo = place("w_lo", [P, 2, KT, P], fr)
        rstd = place("rstd", [P, T])
        sqsum = place("sqsum", [P, T])
        ident = place("ident_sb", [P, P])
        ones = place("ones_sb", [P, P])
        gains = place("gains_sb", [P, 4, KT])
        tok_var = place("tok_var", [P, 8])
        tok_rstd = place("tok_rstd", [P, 8])
        tok_last = place("tok_last", [P, 8])
        rope = place("rope_sb", [P, 2, T])
        decay = place("decay_sb", [P, RH, RC])
        state_in = place("state_in", [P, RH, RD])
        w_hi_third = place("w_hi_third", [P, KT, P], fr, at=ends["state_in"] - 8 * KT * P)
        w_lo_third = place("w_lo_third", [P, KT, P], fr, at=ends["w_hi_third"])
        z_at = top[0]
        assert ends["w_lo_third"] == z_at and ends["ones_sb"] <= ends["w_hi_third"] - 4 * KT * P
        z = place("z", [P, Z_SLOTS, T])
        work_at = top[0]

        mid_hi = place("mid_hi", [P, KT, T], fr, at=z_at + 4 * T * Z_RQ)
        mid_lo = place("mid_lo", [P, KT, T], fr, at=z_at + 4 * T * (Z_RQ + KT))
        y_mix = place("y_mix", [P, KT, T], at=z_at + 4 * T * Z_GATE)
        y_ffn = place("y_ffn", [P, KT, T], at=z_at + 4 * T * (Z_GATE + KT))
        y_out = place("y_out", [P, 5, D], at=z_at + 4 * T * Z_RQ)
        x_nat = place("x_nat", [P, 5, D], at=z_at)
        hankel = place("hankel", [P, AH, 2 * P], at=z_at + 4 * T * Z_RQ)
        k_cache = place("k_cache", [P, 4, AH * AD], at=ends["hankel"])
        table_row = place("table_row", [AH, 3 * P], at=ends["k_cache"])
        flip = place("flip_sb", [P, P], at=ends["table_row"])
        x_waste = place("x_waste", [P, 2, D], at=ends["flip_sb"])
        assert ends["x_nat"] <= z_at + 4 * T * Z_SPARE and ends["x_waste"] <= work_at
        bias = place("bias", [P, AH, 2 * P], at=z_at + 4 * T * Z_SPARE)
        kcT = place("kcT", [P, PAIRS, CACHE], at=ends["bias"])
        assert ends["kcT"] <= z_at + 4 * T * Z_RQ

        v_cache = place("v_cache", [P, 4, P])
        q_pad = place("q_pad", [P, 2, T])
        k_pair = place("k_pair", [P, T])
        v_pair = place("v_pair", [P, T])
        probs = place("probs", [P, 4 * P + 3 * P + 2 * P + P + CACHE + DEC])
        probsT = place("probsT", [P, 1440])
        k_nat = place("k_nat", [P, 5, P])
        v_nat = place("v_nat", [P, 5, P])
        att_nat = place("att_nat", [P, 5, P])
        neg_max = place("neg_max", [P, 8])
        row_sum = place("row_sum", [P, 8])
        row_inv = place("row_inv", [P, 8])
        att_end = top[0]

        top[0] = work_at
        head_c = place("head_c", [P, RC])
        gate_sig = place("gate_sig", [P, T])
        rq = place("rq", [P, T])
        rk = place("rk", [P, T])
        rv = place("rv", [P, T])
        rope_q = place("rope_q", [P, T])
        rope_k = place("rope_k", [P, T])
        gate_row = place("gate_row", [P, T])
        rk_nat = place("rk_nat", [P, 5, P])
        rv_nat = place("rv_nat", [P, 5, P])
        ret_a = place("ret_a", [P, 4 * P + DEC])
        states = place("states", [P, 4, RD])
        state_new = place("state_new", [P, RD])
        ret_o = place("ret_o", [P, 5, RD])
        ret_n = place("ret_n", [P, 5, RD])
        gn_stats = place("gn_stats", [P, 5, 6])
        gn_mv = place("gn_mv", [P, 5, 2])
        gn_std = place("gn_std", [P, 5])
        gn_rstd = place("gn_rstd", [P, 5])

        top[0] = work_at
        part_a = place("part_a", [P, T])
        part_b = place("part_b", [P, T])
        merged = place("merged", [P, 2, T])
        sq = place("sq", [P, 2, T])
        scaled = place("scaled", [P, 2, T])
        relu = place("relu", [P, 2, T])
        relu2 = place("relu2", [P, 2, T])

        acc = [ctx.enter_context(nc.psum_tensor(f"acc{i}", [P, 2, 512], fp)) for i in range(2)]
        wk = ctx.enter_context(nc.psum_tensor("wk", [P, 2048], fp))
        wk_halves = [wk[:, 1024 * i:1024 * i + 1024].rearrange("p (n c) -> p n c", n=2) for i in range(2)]

        table_ext = nc.dram_tensor("table_ext", (AH, 3 * P), fp, kind="Internal").ap()

        ident_in, const_in = sem("ident_in"), sem("const_in")
        x_in = [sem(f"x_in{t}") for t in range(5)]
        w_in_sem = [sem("w_loaded0"), sem("w_loaded1")]
        cache_k_in, table_in, table_filled, table_out, hankel_in = (
            sem("cache_k_in"), sem("table_in"), sem("table_filled"), sem("table_out"), sem("hankel_in"))
        gains_in, x_tr, x_copied_act, x_copied_dve = sem("gains_in"), sem("x_tr"), sem("x_copied_act"), sem("x_copied_dve")
        x_hi, x_lo, x_sum_act, var_clear = sem("x_hi"), sem("x_lo"), sem("x_sum_act"), sem("var_clear")
        kc_tr, kc_ready, bias_mm, bias_ready = sem("kc_tr"), sem("kc_ready"), sem("bias_mm"), sem("bias_ready")
        sum_mm, var_ready, std_ready, tok_rstd_ready, spread_mm, rstd_ready = (
            sem("sum_mm"), sem("var_ready"), sem("std_ready"), sem("tok_rstd_ready"), sem("spread_mm"), sem("rstd_ready"))
        hi_ready, lo_ready, mm_done, acc_free = sem("hi_ready"), sem("lo_ready"), sem("mm_done"), sem("acc_free")
        dve_order, act_order, pool_order = sem("dve_order"), sem("act_order"), sem("pool_order")
        pair_ready, kv_tr, k_nat_ready, v_nat_ready = sem("pair_ready"), sem("kv_tr"), sem("k_nat_ready"), sem("v_nat_ready")
        scores_mm, max_ready, probs_ready = sem("scores_mm"), sem("max_ready"), sem("probs_ready")
        pT_mm, pT_a, pT_b, pT_c = sem("pT_mm"), sem("pT_a"), sem("pT_b"), sem("pT_c")
        pv_mm, att_nat_ready, att_tr, attT_ready = sem("pv_mm"), sem("att_nat_ready"), sem("att_tr"), sem("attT_ready")
        k_out, v_out, v_cache_in = sem("k_out"), sem("v_out"), sem("v_cache_in")
        ret_const_in, gate_sig_ready, swish_ready, q_rotated = sem("ret_const_in"), sem("gate_sig_ready"), sem("swish_ready"), sem("q_rotated")
        q_copied, gate_copied = sem("q_copied"), sem("gate_copied")
        ret_ready, rkv_tr, rk_nat_ready, rv_nat_ready = sem("ret_ready"), sem("rkv_tr"), sem("rk_nat_ready"), sem("rv_nat_ready")
        ret_s_mm, ret_a_ready, ret_o_mm, gn_var, gn_root = (
            sem("ret_s_mm"), sem("ret_a_ready"), sem("ret_o_mm"), sem("gn_var"), sem("gn_root"))
        ret_n_ready, ret_tr, retT_ready, state_out = sem("ret_n_ready"), sem("ret_tr"), sem("retT_ready"), sem("state_out")
        in_hi, in_lo, gates_ready, merge_ready, mid_hi_r, mid_lo_r = (
            sem("in_hi"), sem("in_lo"), sem("gates_ready"), sem("merge_ready"), sem("mid_hi_ready"), sem("mid_lo_ready"))
        sq_ready, sq_added = sem("sq_ready"), sem("sq_added")
        scaled_ready, x1_even, x1_odd = sem("scaled_ready"), sem("x1_even"), sem("x1_odd")
        h2_hi, h2_lo = sem("h2_hi"), sem("h2_lo")
        relu2_ready, f_hi, f_lo = sem("relu2_ready"), sem("f_hi"), sem("f_lo")
        y_zero, outT_even, outT_odd, out_tr = sem("y_zero"), sem("outT_even"), sem("outT_odd"), sem("out_tr")
        out_nat, y_stored = sem("out_nat"), sem("y_stored")

        block = ctx.enter_context(nc.Block())

        CREDITS = {k_out: 32, v_out: 32, state_out: 32, attT_ready: 1, retT_ready: 1, sq_added: 2, f_lo: 2, acc_free: 2}

        G_RET, G_GATE, G_MERGE, G_WO, G_FFN = 3, 7, 11, 13, 15

        def halves(ap):
            return ap.rearrange("p (n c) -> p n c", n=2)

        def evacuated(eng, g, j):
            eng.wait_ge(acc_free, 4 * g + j + 3)

        w_in_v = a["w_in"].rearrange("(k p) n -> p k n", p=P)
        w_ao_v = a["w_attn_out"].rearrange("(k p) n -> p k n", p=P)
        w_ro_v = a["w_ret_out"].rearrange("(k p) n -> p k n", p=P)
        w_o_v = a["w_o"].rearrange("(k p) n -> p k n", p=P)
        w_up_v = a["w_ff_up"].rearrange("(k p) n -> p k n", p=P)
        w_dn_v = a["w_ff_down"].rearrange("(k p) n -> p k n", p=P)

        S_COL = {3: 0, 2: 512, 0: 896, 1: 1024, 4: 1504}
        P_COL = {0: 0, 1: P, 2: 3 * P, 3: 6 * P, 4: 10 * P}
        WIDTH = {0: P, 1: 2 * P, 2: 3 * P, 3: 4 * P, 4: CACHE + DEC}
        NEAR = {0: (0, P), 1: (0, 2 * P), 2: (P, 2 * P), 3: (2 * P, 2 * P), 4: (3 * P, P + DEC)}
        PT_COL = {3: 0, 2: 512, 0: 896, 1: 1024, 4: 1280}
        ORDER = (3, 2, 0, 1, 4)
        SUM_COL = 1000

        def x_psum(t):
            n = TILES[t][1]
            if t in (0, 1):
                return acc[t][:].rearrange("p n (k c) -> p (n k) c", k=4)
            if t in (2, 3):
                return wk[:, 1024 * (t - 2):1024 * (t - 1)].rearrange("p (k c) -> p k c", k=KT)
            return acc[0][:, 0, 0:KT * n].rearrange("p (k c) -> p k c", k=KT)

        def out_psum(m):
            if m % 4 in (1, 2):
                return acc[m % 4 - 1][:].rearrange("p n c -> p (n c)")[:, 0:5 * P]
            return wk[:, 1024 * (m % 4 == 0):1024 * (m % 4 == 0) + 5 * P]

        def squares_added(norm, count):
            return 2 + (KT - 1) * (norm - 1) + count

        @block.sync
        def _(sp):
            for t, (s, n) in enumerate(TILES):
                src = a["x_prompt"][0, s:s + n, :] if t < 4 else a["x_sample"][0]
                sp.dma_start(x_nat[0:n, t, :], src).then_inc(x_in[t], 16)

            def load(buf, src_a, src_b, col):
                sp.dma_start(w_raw[:, buf, 0:4, :], src_a[:, :, bass.ds(col, STAGE)]).then_inc(w_in_sem[buf], 16)
                sp.dma_start(w_raw[:, buf, 4:8, :], src_b[:, :, bass.ds(col, STAGE)]).then_inc(w_in_sem[buf], 16)

            def load_body(g, src_a, src_b, col):
                for buf in range(2):
                    sp.wait_ge(lo_ready, 4 * g - 2 + 2 * buf)
                    load(buf, src_a, src_b, col + STAGE * buf)

            load(0, w_in_v[:, 0:4], w_in_v[:, 4:8], 0)
            sp.dma_start(k_cache[:], a["cache_attn_k"].rearrange("(t p) c -> p t c", p=P)).then_inc(cache_k_in, 16)
            load(1, w_in_v[:, 0:4], w_in_v[:, 4:8], STAGE)
            sp.dma_start(rope[:], a["rope"]).then_inc(ret_const_in, 16)
            sp.dma_start(decay[:], a["decay"]).then_inc(ret_const_in, 16)
            sp.dma_start(state_in[:], a["state_retention"].rearrange("h d e -> d h e")).then_inc(ret_const_in, 16)
            with sp.Fori(1, G_MERGE) as g:
                load_body(g, w_in_v[:, 0:4], w_in_v[:, 4:8], 512 * g)
            with sp.Fori(0, 2) as i:
                load_body(i + G_MERGE, w_ao_v, w_ro_v, 512 * i)
            with sp.Fori(0, 2) as i:
                load_body(i + G_WO, w_o_v[:, 0:4], w_o_v[:, 4:8], 512 * i)
            with sp.Fori(0, 4) as c:
                with sp.Fori(0, 2) as i:
                    load_body(G_FFN + 4 * c + i, w_up_v[:, 0:4], w_up_v[:, 4:8], 1024 * c + 512 * i)
                with sp.Fori(0, 2) as i:
                    load_body(G_FFN + 2 + 4 * c + i, w_dn_v[:, bass.ds(8 * c, 4)],
                              w_dn_v[:, bass.ds(8 * c + 4, 4)], 512 * i)
            for m in range(KT):
                sp.wait_ge(out_nat, m + 1)
                cols = slice(P * m, P * m + P)
                sp.dma_start(outs["y_prompt"][0].rearrange("(t p) c -> p t c", p=P)[:, :, cols], y_out[:, 0:4, cols]).then_inc(y_stored, 16)
                sp.dma_start(outs["y_sample"][0][:, cols], y_out[0:DEC, 4, cols]).then_inc(y_stored, 16)
            sp.wait_ge(y_stored, 32 * KT)

        @block.gpsimd
        def _(pool):
            order = Order(pool, pool_order)
            pool.dma_start(table_row[:, 0:TABLE], a["rel_bias_table"]).then_inc(table_in, 16)
            pool.wait_ge(table_in, 16)
            pool.tensor_copy(table_row[:, TABLE:3 * P],
                             table_row[:, TABLE - 1:TABLE].to_broadcast([AH, 3 * P - TABLE])).then_inc(table_filled, 1)
            pool.wait_ge(table_filled, 1)
            pool.dma_start(table_ext, table_row[:]).then_inc(table_out, 16)
            pool.wait_ge(table_out, 16)
            pool.dma_start(hankel[:], bass.AP(table_ext.tensor, 1, [[1, P], [3 * P, AH], [1, 2 * P]])).then_inc(hankel_in, 16)
            pool.wait_ge(ret_const_in, 48)
            pool.wait_ge(acc_free, 2 + 4 * G_GATE)
            pool.wait_ge(attT_ready, PAIRS + 1)
            pool.wait_ge(k_out, 32 * PAIRS + 32)
            pool.wait_ge(v_out, 32 * PAIRS + 32)

            with pool.Fori(0, RH) as i:
                order.body(i, 3)
                pool.wait_ge(q_copied, i + 1)
                for to, frm in ((0, RD // 2), (RD // 2, 0)):
                    order.after(pool.tensor_tensor(rope_q[to:to + RD // 2, :], rq[frm:frm + RD // 2, :], rope[frm:frm + RD // 2, 1, :], ALU.mult))
                order.after(pool.tensor_tensor(rq[:], rq[:], rope[:, 0, :], ALU.mult))
                pool.tensor_tensor(rq[:], rq[:], rope_q[:], ALU.add).then_inc(q_rotated, 1)
                pool.wait_ge(gate_sig_ready, i + 1)
                pool.tensor_tensor(gate_row[:], gate_row[:], gate_sig[:], ALU.mult).then_inc(swish_ready, 1)
            order.leave(RH)
            pool.wait_ge(state_out, 32 * RH + 32)

            def add_square(norm, m):
                pool.wait_ge(sq_ready, KT * (norm - 1) + m + 1)
                pool.tensor_tensor(sqsum[:], sqsum[:], sq[:, m % 2, :], ALU.add).then_inc(sq_added, 1)
                pool.wait_ge(sq_added, squares_added(norm, m + 1))

            pool.wait_ge(mid_lo_r, KT)
            pool.memset(y_ffn[:], 0.0).then_inc(y_zero, 1)
            order.after(pool.memset(sqsum[:], 0.0))
            for m in range(KT - 1):
                add_square(1, m)
            pool.wait_ge(sum_mm, 1)
            order.after(pool.memset(sqsum[:], 0.0))
            for m in range(KT):
                if m % 2:
                    pool.wait_ge(scaled_ready, m // 2 + 1)
                    pool.tensor_tensor(xT[:, m, :], xT[:, m, :], scaled[:, 1, :], ALU.add).then_inc(x1_odd, 1)
                if m > 1:
                    add_square(2, m - 2)
            add_square(2, KT - 2)
            pool.wait_ge(sum_mm, 2)
            order.after(pool.memset(sqsum[:], 0.0))
            for m in range(KT - 1):
                add_square(3, m)
            for p in range(KT // 2):
                pool.wait_ge(scaled_ready, KT // 2 + p + 1)
                pool.tensor_tensor(y_ffn[:, 2 * p + 1, :], xT[:, 2 * p + 1, :], scaled[:, 1, :], ALU.add).then_inc(outT_odd, 1)

        @block.scalar
        def _(act):
            order = Order(act, act_order)

            def split_hi(u, v, wait_load=None):
                if wait_load is not None:
                    act.wait_ge(w_in_sem[v // 2], wait_load)
                act.activation(w_hi[:, v % 2], w_raw[:, v // 2, :, P * (v % 2):P * (v % 2) + P], ACT.Copy).then_inc(hi_ready, 1)

            def split_ahead(g, j):
                act.wait_ge(mm_done, 4 * g + j + 1)
                v = (j + 2) % 4
                split_hi(4 * g + j + 2, v, {0: 32 * (g + 1), 2: 32 * (g + 2)}.get(j))

            act.dma_start(ident[:], a["ident"]).then_inc(ident_in, 16)
            act.dma_start(gains[:], a["gains"]).then_inc(gains_in, 16)
            act.dma_start(ones[:], a["ones"]).then_inc(const_in, 16)
            act.dma_start(flip[:], a["flip"]).then_inc(const_in, 16)
            for counter, n in CREDITS.items():
                act.sem_inc(counter, n)
            act.preload_act_table(ACT.Sqrt)

            def square_sum(t):
                n = TILES[t][1]
                act.wait_ge(x_in[t], 16)
                act.activation(x_waste[0:n, 0, :], x_nat[0:n, t, :], ACT.Square, accum_out=tok_var[0:n, t:t + 1]).then_inc(x_sum_act, 1)

            def copy_x(t):
                s, n = TILES[t]
                act.wait_ge(x_tr, t + 1)
                act.activation(xT[:, :, s:s + n], x_psum(t), ACT.Copy).then_inc(x_copied_act, 1)

            def root(norm):
                act.wait_ge(var_ready, norm + 1)
                act.activation(tok_rstd[:, 0:5], tok_var[:, 0:5], ACT.Sqrt).then_inc(std_ready, 1)

            act.wait_ge(var_clear, 1)
            square_sum(1)
            copy_x(0)
            act.wait_ge(x_sum_act, 1)
            square_sum(3)
            copy_x(2)
            copy_x(4)
            root(0)
            split_hi(0, 0, 32)
            act.wait_ge(gains_in, 16)
            act.wait_ge(x_copied_act, 3)
            act.wait_ge(x_copied_dve, 2)
            for k in range(KT):
                act.activation(act_hi[:, k, :], xT[:, k, :], ACT.Copy, scale=gains[:, 0, k:k + 1]).then_inc(x_hi, 1)
            split_hi(1, 1)

            split_ahead(0, 0)
            split_ahead(0, 1)
            act.wait_ge(kc_tr, 1)
            act.activation(kcT[:], wk[:].rearrange("p (a b) -> p a b", a=PAIRS), ACT.Copy).then_inc(kc_ready, 1)
            split_ahead(0, 2)
            split_ahead(0, 3)
            with act.Fori(1, G_RET) as g:
                for j in range(4):
                    split_ahead(g, j)

            def exps(i, e):
                for k, t in enumerate(ORDER):
                    n = TILES[t][1]
                    if k in (0, 1, 3):
                        act.wait_ge(max_ready, 6 * i + 3 * e + (1, 2, 2, 3, 3)[k])
                    act.activation(probs[0:n, P_COL[t]:P_COL[t] + WIDTH[t]], wk[0:n, S_COL[t]:S_COL[t] + WIDTH[t]],
                                   ACT.Exp, bias=neg_max[0:n, t:t + 1], accum_out=row_sum[0:n, t:t + 1]).then_inc(probs_ready, 1)

            def probsT_copy(i, e):
                act.wait_ge(pT_mm, 6 * i + 3 * e + 2)
                act.activation(probsT[:, 512:1024], wk[:, 512:1024], ACT.Copy).then_inc(pT_b, 1)

            def store_kv(i):
                for nat, ready, stored, name in ((k_nat, k_nat_ready, k_out, "new_k"), (v_nat, v_nat_ready, v_out, "new_v")):
                    act.wait_ge(ready, i + 1)
                    act.dma_start(outs[name + "_prompt"].rearrange("(t p) c -> p t c", p=P)[:, :, bass.ds(P * i, P)],
                                  nat[:, 0:4, :]).then_inc(stored, 16)
                    act.dma_start(outs[name + "_sample"][:, bass.ds(P * i, P)], nat[0:DEC, 4, :]).then_inc(stored, 16)

            with act.Fori(0, PAIRS) as i:
                g = i + G_RET
                act.wait_ge(attT_ready, i + 1)
                act.dma_start(v_cache[:], a["cache_attn_v"].rearrange("(t p) c -> p t c", p=P)[:, :, bass.ds(P * i, P)])\
                    .then_inc(v_cache_in, 16)
                split_ahead(g, 0)
                act.wait_ge(kv_tr, i + 1)
                act.wait_ge(v_out, 32 * i + 32)
                act.activation(v_nat[:, 0:4, :], wk[:, 1024:1536].rearrange("p (t c) -> p t c", t=4), ACT.Copy)
                act.activation(v_nat[0:DEC, 4, :], wk[0:DEC, 1536:1664], ACT.Copy).then_inc(v_nat_ready, 1)
                split_ahead(g, 1)
                store_kv(i)
                exps(i, 0)
                probsT_copy(i, 0)
                split_ahead(g, 2)
                exps(i, 1)
                probsT_copy(i, 1)
                split_ahead(g, 3)

            with act.Fori(0, RH) as i:
                g = i + G_GATE
                split_ahead(g, 0)
                act.wait_ge(gate_copied, i + 1)
                act.activation(gate_sig[:], gate_row[:], ACT.Sigmoid).then_inc(gate_sig_ready, 1)
                act.wait_ge(rkv_tr, i + 1)
                act.activation(rv_nat[:, 0:4, :], wk[:, 1024:1536].rearrange("p (t c) -> p t c", t=4), ACT.Copy)
                act.activation(rv_nat[0:DEC, 4, :], wk[0:DEC, 1536:1664], ACT.Copy).then_inc(rv_nat_ready, 1)
                split_ahead(g, 1)
                act.wait_ge(ret_a_ready, i + 1)
                act.dma_start(outs["new_state_prompt"][bass.ds(i, 1)].rearrange("h d e -> (h d) e"), states[:, 3, :]).then_inc(state_out, 16)
                act.dma_start(outs["new_state_sample"][bass.ds(i, 1)].rearrange("h d e -> (h d) e"), state_new[:]).then_inc(state_out, 16)
                split_ahead(g, 2)
                act.wait_ge(gn_var, i + 1)
                act.activation(gn_std[:, 0:4], gn_std[:, 0:4], ACT.Sqrt)
                act.activation(gn_std[0:DEC, 4:5], gn_std[0:DEC, 4:5], ACT.Sqrt).then_inc(gn_root, 1)
                split_ahead(g, 3)

            act.wait_ge(mm_done, 4 * G_MERGE)
            for k in range(KT):
                if k == 4:
                    act.wait_ge(retT_ready, RH + 1)
                if k == 0:
                    act.wait_ge(attT_ready, PAIRS + 1)
                act.activation(act_hi[:, k, :], z[:, k if k < 4 else Z_RQ + k - 4, :], ACT.Copy).then_inc(in_hi, 1)
            act.wait_ge(acc_free, 2 + 4 * G_MERGE)
            with act.Fori(0, 2) as i:
                for j in range(4):
                    m = 4 * i + j
                    act.activation(z[:, bass.ds(Z_GATE + m, 1), :], z[:, bass.ds(Z_GATE + m, 1), :], ACT.Sigmoid)
                    act.activation(z[:, bass.ds(Z_GATE + KT + m, 1), :], z[:, bass.ds(Z_GATE + KT + m, 1), :], ACT.Sigmoid)\
                        .then_inc(gates_ready, 1)
                    split_ahead(i + G_MERGE, j)
                    act.wait_ge(merge_ready, m + 1)
                    act.activation(mid_hi[:, m, :], merged[:, j % 2, :], ACT.Copy).then_inc(mid_hi_r, 1)

            act.preload_act_table(ACT.Sqrt)
            with act.Fori(0, 2) as i:
                for j in range(4):
                    split_ahead(i + G_WO, j)
                    evacuated(act, i + G_WO, j)
                    act.wait_ge(sq_added, 4 * i + j + 1)
                    act.activation(sq[:, j % 2, :], y_mix[:, 4 * i + j, :], ACT.Square).then_inc(sq_ready, 1)
            act.wait_ge(w_in_sem[1], 32 * (G_FFN + 1))
            act.activation(w_hi_third[:], w_raw[:, 1, :, 0:P], ACT.Copy).then_inc(hi_ready, 1)
            root(1)
            for m in range(KT):
                act.wait_ge((x1_even, x1_odd)[m % 2], m // 2 + 1)
                act.activation(act_hi[:, m, :], xT[:, m, :], ACT.Copy, scale=gains[:, 2, m:m + 1]).then_inc(h2_hi, 1)
                if m >= 2:
                    act.wait_ge(sq_added, squares_added(2, m - 1))
                act.activation(sq[:, m % 2, :], xT[:, m, :], ACT.Square).then_inc(sq_ready, 1)
            root(2)

            def up(c, i, first=False):
                for j in range(4):
                    g = G_FFN + 4 * c + i
                    if not (first and j < 2):
                        split_ahead(g, j)
                    k = 8 * c + 4 * i + j
                    evacuated(act, g, j)
                    act.wait_ge(f_lo, k + 1)
                    ins = act.activation(relu2[:, j % 2, :], relu[:, j % 2, :], ACT.Square)
                    ins.then_inc(relu2_ready, 1)
                    act.wait_ge(relu2_ready, k + 1)
                    act.activation(mid_hi[:, 4 * i + j, :], relu2[:, j % 2, :], ACT.Copy).then_inc(f_hi, 1)

            def down(c):
                with act.Fori(0, 2) as i:
                    for j in range(4):
                        split_ahead(G_FFN + 2 + 4 * c + i, j)

            split_ahead(G_FFN, 1)
            up(0, 0, first=True)
            up(0, 1)
            down(0)
            with act.Fori(1, 3) as c:
                with act.Fori(0, 2) as i:
                    up(c, i)
                down(c)
            with act.Fori(0, 2) as i:
                up(3, i)
            for m in range(KT):
                if m < KT - 2:
                    split_ahead(G_FFN + 14 + m // 4, m % 4)
                evacuated(act, G_FFN + 14 + m // 4, m % 4)
                if m >= 2:
                    act.wait_ge(sq_added, squares_added(3, m - 1))
                act.activation(sq[:, m % 2, :], y_ffn[:, m, :], ACT.Square).then_inc(sq_ready, 1)
            root(3)
            for m in range(KT):
                act.wait_ge(out_tr, m + 1)
                act.activation(y_out[:, 0:4, P * m:P * m + P], out_psum(m)[:, 0:SEQ].rearrange("p (t c) -> p t c", t=4), ACT.Copy)
                act.activation(y_out[0:DEC, 4, P * m:P * m + P], out_psum(m)[0:DEC, SEQ:5 * P], ACT.Copy).then_inc(out_nat, 1)

        @block.tensor
        def _(pe):
            def products(dst, whi, wlo, k, hi, lo, start, stop):
                for w, h, begin, end in ((whi, hi, start, False), (whi, lo, False, False), (wlo, hi, False, stop)):
                    for n in range(2):
                        ins = pe.matmul(dst[:, n, 0:HALF], w[:, k, :], h[:, k, HALF * n:HALF * n + HALF], start=begin, stop=end)
                return ins

            def column_tile(g, j, hi, lo, kt=range(KT), dst=None, first_=True, last=True, before=None):
                dst = acc[j % 2] if dst is None else dst
                if first_:
                    pe.wait_ge(lo_ready, 4 * g + j + 1)
                    pe.wait_ge(acc_free, 4 * g + j + 1)
                ks = list(kt)
                for k in ks:
                    if before:
                        before(k)
                    ins = products(dst, w_hi[:, j % 2], w_lo[:, j % 2], k, hi, lo, k == ks[0], k == ks[-1])
                if last:
                    ins.then_inc(mm_done, 1)

            def tr(out, in_):
                n = in_.shape[0]
                return pe.transpose(out, in_, ident[0:n, 0:n])

            pe.wait_ge(ident_in, 16)
            for t, (s, n) in enumerate(TILES):
                pe.wait_ge(x_in[t], 16)
                if t == 4:
                    pe.wait_ge(x_copied_act, 1)
                ps = x_psum(t)
                for k in range(KT):
                    ins = tr(ps[:, k, :], x_nat[0:n, t, P * k:P * k + P])
                ins.then_inc(x_tr, 1)
            def feature_sum(norm):
                for col, squares in ((SUM_COL, sqsum[:]), (SUM_COL + 5, sq[:, 1, :])):
                    if col == SUM_COL:
                        pe.wait_ge(sq_added, squares_added(norm, KT - 1))
                    else:
                        pe.wait_ge(sq_ready, KT * norm)
                    for t, (s, n) in enumerate(TILES):
                        ins = pe.matmul(wk[0:n, col + t:col + t + 1], squares[:, s:s + n], ones[:, 0:1], start=True, stop=True)
                ins.then_inc(sum_mm, 1)

            def spread(norm):
                pe.wait_ge(tok_rstd_ready, norm + 1)
                for t, (s, n) in enumerate(TILES):
                    ins = pe.matmul(wk[:, s:s + n], tok_rstd[0:n, t:t + 1].to_broadcast([n, P]), ident[0:n, 0:n], start=True, stop=True)
                ins.then_inc(spread_mm, 1)

            pe.wait_ge(x_copied_act, 2)
            spread(0)
            def x_split(k):
                pe.wait_ge(x_lo, k + 1)
            column_tile(0, 0, act_hi, act_lo, before=x_split)
            column_tile(0, 1, act_hi, act_lo)
            pe.wait_ge(cache_k_in, 16)
            pe.wait_ge(rstd_ready, 1)
            for p in range(PAIRS):
                for t in range(4):
                    ins = tr(wk[:, 512 * p + P * t:512 * p + P * t + P], k_cache[:, t, P * p:P * p + P])
            ins.then_inc(kc_tr, 1)
            column_tile(0, 2, act_hi, act_lo)
            column_tile(0, 3, act_hi, act_lo)
            with pe.Fori(1, G_RET) as g:
                for j in range(4):
                    column_tile(g, j, act_hi, act_lo)

            pe.wait_ge(hankel_in, 16)
            pe.wait_ge(const_in, 32)
            pe.wait_ge(kc_ready, 1)
            for h in range(AH):
                for b in range(2):
                    ins = pe.matmul(wk[:, 256 * h + P * b:256 * h + P * b + P], hankel[:, h, P * (1 - b):P * (1 - b) + P], flip[:],
                                    start=True, stop=True)
            ins.then_inc(bias_mm, 1)

            def scores(i, e):
                for t in ORDER:
                    s, n = TILES[t]
                    q = q_pad[:, e, s:s + n]
                    if t < 4:
                        ins = pe.matmul(wk[:, S_COL[t]:S_COL[t] + WIDTH[t]], q, k_pair[:, 0:WIDTH[t]], start=True, stop=True)
                    else:
                        pe.matmul(wk[0:n, 1504:1536], q, kcT[:, bass.ds(i, 1), 0:32].rearrange("p a c -> p (a c)"), start=True, stop=True)
                        pe.matmul(wk[0:n, 1536:2016], q, kcT[:, bass.ds(i, 1), 32:CACHE].rearrange("p a c -> p (a c)"), start=True, stop=True)
                        ins = pe.matmul(wk[0:n, 2016:2048], q, k_pair[:, SEQ:T], start=True, stop=True)
                ins.then_inc(scores_mm, 1)

            def probs_times_v(i, e):
                done = 0
                for k, t in enumerate(ORDER):
                    n = TILES[t][1]
                    if k in (0, 1, 3):
                        pe.wait_ge(probs_ready, 10 * i + 5 * e + (1, 3, 3, 5, 5)[k])
                    blocks = WIDTH[t] // P
                    for b in range(blocks):
                        ins = tr(wk[:, PT_COL[t] + n * b:PT_COL[t] + n * b + n], probs[0:n, P_COL[t] + P * b:P_COL[t] + P * b + P])
                    if t == 4:
                        ins = tr(wk[0:DEC, 1408:1440], probs[0:n, P_COL[t] + CACHE:P_COL[t] + CACHE + DEC])
                    if k in (0, 2, 4):
                        ins.then_inc(pT_mm, 1)
                for k, t in enumerate(ORDER):
                    n = TILES[t][1]
                    if k in (0, 1, 3):
                        pe.wait_ge((pT_a, pT_b, None, pT_c)[k], 2 * i + e + 1)
                    out = wk[0:n, 1536 + AD * t:1536 + AD * t + AD]
                    blocks = WIDTH[t] // P
                    for b in range(blocks):
                        v = v_nat[:, b, AD * e:AD * e + AD] if t < 4 else v_cache[:, b, AD * e:AD * e + AD]
                        ins = pe.matmul(out, probsT[:, PT_COL[t] + n * b:PT_COL[t] + n * b + n], v,
                                        start=(b == 0), stop=(t < 4 and b == blocks - 1))
                    if t == 4:
                        ins = pe.matmul(out, probsT[0:DEC, 1408:1440], v_nat[0:DEC, 4, AD * e:AD * e + AD], start=False, stop=True)
                ins.then_inc(pv_mm, 1)

            def to_natural(src, col):
                for t, (s, n) in enumerate(TILES):
                    ins = tr(wk[0:n, col + P * t:col + P * t + P], src[:, s:s + n])
                return ins

            with pe.Fori(0, PAIRS) as i:
                g = i + G_RET
                column_tile(g, 0, act_hi, act_lo)
                pe.wait_ge(pair_ready, i + 1)
                pe.wait_ge(bias_ready, 1)
                pe.wait_ge(attT_ready, i + 1)
                to_natural(k_pair, 0)
                to_natural(v_pair, 1024).then_inc(kv_tr, 1)
                column_tile(g, 1, act_hi, act_lo)
                pe.wait_ge(k_nat_ready, i + 1)
                pe.wait_ge(v_nat_ready, i + 1)
                scores(i, 0)
                column_tile(g, 2, act_hi, act_lo)
                pe.wait_ge(v_cache_in, 16 * i + 16)
                probs_times_v(i, 0)
                pe.wait_ge(att_nat_ready, 2 * i + 1)
                scores(i, 1)
                column_tile(g, 3, act_hi, act_lo)
                probs_times_v(i, 1)
                pe.wait_ge(att_nat_ready, 2 * i + 2)
                for t, (s, n) in enumerate(TILES):
                    ins = tr(wk[:, s:s + n], att_nat[0:n, t, :])
                ins.then_inc(att_tr, 1)

            with pe.Fori(0, RH) as i:
                g = i + G_GATE
                column_tile(g, 0, act_hi, act_lo)
                pe.wait_ge(ret_ready, i + 1)
                pe.wait_ge(retT_ready, i + 1)
                pe.wait_ge(attT_ready, PAIRS + 1)
                to_natural(rk, 0)
                to_natural(rv, 1024).then_inc(rkv_tr, 1)
                column_tile(g, 1, act_hi, act_lo)
                pe.wait_ge(q_rotated, i + 1)
                pe.wait_ge(rk_nat_ready, i + 1)
                pe.wait_ge(rv_nat_ready, i + 1)
                for t, (s, n) in enumerate(TILES):
                    pe.matmul(wk[0:n, s:s + n], rk[:, s:s + n], rq[:, s:s + n], start=True, stop=True)
                for t, (s, n) in enumerate(TILES):
                    ins = pe.matmul(wk[:, 1024 + RD * t:1024 + RD * t + RD], rk_nat[0:n, t, :], rv_nat[0:n, t, :], start=True, stop=True)
                ins.then_inc(ret_s_mm, 1)
                column_tile(g, 2, act_hi, act_lo)
                pe.wait_ge(ret_a_ready, i + 1)
                for t, (s, n) in enumerate(TILES):
                    out = wk[0:n, RD * t:RD * t + RD]
                    alone = t == 0
                    ins = pe.matmul(out, ret_a[0:n, s:s + n], rv_nat[0:n, t, :], start=True, stop=alone)
                    if t == 4:
                        ins = pe.matmul(out, rq[:, s:s + n], state_in[:, bass.ds(i, 1), :].rearrange("p a c -> p (a c)"), start=False, stop=True)
                    elif t:
                        ins = pe.matmul(out, rq[:, s:s + n], states[:, t - 1, :], start=False, stop=True)
                ins.then_inc(ret_o_mm, 1)
                column_tile(g, 3, act_hi, act_lo)
                pe.wait_ge(ret_n_ready, i + 1)
                for t, (s, n) in enumerate(TILES):
                    ins = tr(wk[:, 1024 + s:1024 + s + n], ret_n[0:n, t, :])
                ins.then_inc(ret_tr, 1)

            pe.wait_ge(retT_ready, RH + 1)
            with pe.Fori(0, 2) as i:
                for j in range(4):
                    def branch_ready(k):
                        pe.wait_ge(in_lo, k + 1)
                    column_tile(i + G_MERGE, j, act_hi, act_lo, range(4), last=False, before=branch_ready)
                    column_tile(i + G_MERGE, j, act_hi, act_lo, range(4, 8), dst=wk_halves[j % 2], first_=False, before=branch_ready)

            with pe.Fori(0, 2) as i:
                for j in range(4):
                    def merge_split(k):
                        pe.wait_ge(mid_lo_r, k + 1)
                    column_tile(i + G_WO, j, mid_hi, mid_lo, before=merge_split if j == 0 else None)
            feature_sum(1)
            spread(1)

            for k in range(KT):
                pe.wait_ge(h2_lo, k + 1)
                for j in range(2):
                    if k == 0:
                        pe.wait_ge(lo_ready, 4 * G_FFN + j + 1)
                        pe.wait_ge(acc_free, 4 * G_FFN + j + 1)
                    ins = products(acc[j], w_hi[:, j], w_lo[:, j], k, act_hi, act_lo, k == 0, k == KT - 1)
                    if k == KT - 1:
                        ins.then_inc(mm_done, 1)
            feature_sum(2)
            pe.wait_ge(lo_ready, 4 * G_FFN + 3)
            for k in range(KT):
                if k == 3:
                    spread(2)
                ins = products(wk_halves[1], w_hi_third, w_lo_third, k, act_hi, act_lo, k == 0, k == KT - 1)
            ins.then_inc(mm_done, 1)
            column_tile(G_FFN, 3, act_hi, act_lo)

            def up(g):
                for j in range(4):
                    column_tile(g, j, act_hi, act_lo)

            def down(c):
                def hidden_split(k):
                    pe.wait_ge(f_lo, 8 * c + k + 3)
                with pe.Fori(0, 2) as i:
                    for j in range(4):
                        column_tile(G_FFN + 2 + 4 * c + i, j, mid_hi, mid_lo, before=hidden_split if j == 0 else None)

            up(G_FFN + 1)
            down(0)
            with pe.Fori(1, 4) as c:
                with pe.Fori(0, 2) as i:
                    up(G_FFN + 4 * c + i)
                down(c)
            feature_sum(3)
            spread(3)
            for m in range(KT):
                pe.wait_ge((outT_even, outT_odd)[m % 2], m // 2 + 1)
                if m == 3:
                    pe.wait_ge(rstd_ready, 4)
                if m >= 4:
                    pe.wait_ge(out_nat, m - 3)
                for t, (s, n) in enumerate(TILES):
                    ins = tr(out_psum(m)[0:n, P * t:P * t + P], y_ffn[:, m, s:s + n])
                ins.then_inc(out_tr, 1)

        @block.vector
        def _(dve):
            order = Order(dve, dve_order)

            def copy(out, in_):
                return dve.tensor_scalar(out, in_, 1.0, None, ALU.mult)

            def split_lo(u, v):
                dve.wait_ge(hi_ready, u + 1)
                dve.tensor_tensor(w_lo[:, v % 2], w_raw[:, v // 2, :, P * (v % 2):P * (v % 2) + P],
                                  w_hi[:, v % 2].bitcast(fp), ALU.subtract).then_inc(lo_ready, 1)

            def split_ahead(g, j):
                split_lo(4 * g + j + 2, (j + 2) % 4)

            def to_z(g, j, slot):
                dve.wait_ge(mm_done, 4 * g + j + 1)
                dve.tensor_tensor(z[:, bass.ds(slot, 1), :].rearrange("p a (n c) -> p (a n) c", n=2),
                                  acc[j % 2][:, :, 0:HALF], halves(rstd[:]), ALU.mult).then_inc(acc_free, 1)

            dve.memset(tok_var[:], 1.0).then_inc(var_clear, 1)
            dve.memset(q_pad[:], 0.0)
            dve.wait_ge(var_clear, 1)

            def square_sum(t):
                n = TILES[t][1]
                dve.wait_ge(x_in[t], 16)
                order.after(dve.scalar_tensor_tensor(x_waste[0:n, 1, :], x_nat[0:n, t, :], 1.0, x_nat[0:n, t, :], ALU.mult, ALU.mult,
                                                     accum_out=tok_var[0:n, t:t + 1]))

            def copy_x(t):
                s, n = TILES[t]
                dve.wait_ge(x_tr, t + 1)
                dve.tensor_copy(xT[:, :, s:s + n], x_psum(t)).then_inc(x_copied_dve, 1)

            square_sum(0)
            square_sum(2)
            copy_x(1)
            square_sum(4)
            dve.wait_ge(x_sum_act, 2)
            dve.tensor_scalar(tok_var[:, 0:5], tok_var[:, 0:5], 1.0 / D, EPS, ALU.mult, ALU.add).then_inc(var_ready, 1)
            copy_x(3)
            dve.wait_ge(std_ready, 1)
            dve.reciprocal(tok_rstd[:, 0:5], tok_rstd[:, 0:5]).then_inc(tok_rstd_ready, 1)
            split_lo(0, 0)
            for k in range(KT):
                dve.wait_ge(x_hi, k + 1)
                dve.scalar_tensor_tensor(act_lo[:, k, :], xT[:, k, :], gains[:, 0, k:k + 1], act_hi[:, k, :].bitcast(fp),
                                         ALU.mult, ALU.subtract).then_inc(x_lo, 1)
            split_lo(1, 1)
            dve.wait_ge(spread_mm, 1)
            dve.tensor_copy(rstd[:], wk[:, 0:T]).then_inc(rstd_ready, 1)
            dve.wait_ge(rstd_ready, 1)

            def norm(n, between=None):
                dve.wait_ge(sum_mm, n)
                order.after(dve.tensor_scalar(tok_last[:, 0:5], wk[:, SUM_COL + 5:SUM_COL + 10], 1.0 / D, EPS, ALU.mult, ALU.add))
                dve.scalar_tensor_tensor(tok_var[:, 0:5], wk[:, SUM_COL:SUM_COL + 5], 1.0 / D, tok_last[:, 0:5], ALU.mult, ALU.add).then_inc(var_ready, 1)
                dve.wait_ge(std_ready, n + 1)
                dve.reciprocal(tok_rstd[:, 0:5], tok_rstd[:, 0:5]).then_inc(tok_rstd_ready, 1)
                if between:
                    between()
                dve.wait_ge(spread_mm, n + 1)
                dve.tensor_copy(rstd[:], wk[:, 0:T]).then_inc(rstd_ready, 1)
                dve.wait_ge(rstd_ready, n + 1)

            order.flatten()

            with dve.Fori(0, G_RET) as g:
                for j in range(4):
                    to_z(g, j, 4 * g + j)
                    split_ahead(g, j)

            dve.wait_ge(bias_mm, 1)
            order.after(dve.tensor_tensor(bias[:], wk[:].rearrange("p (h c) -> p h c", h=AH),
                                          hankel[:, :, 2 * P - 1:2 * P].to_broadcast([P, AH, 2 * P]), ALU.subtract))
            dve.memset(bias[0:AD, :, P + AD:2 * P], NEG).then_inc(bias_ready, 1)
            order.flatten()

            def masked_max(i, e):
                h = 2 * i + e
                dve.wait_ge(scores_mm, h + 1)
                for group, tiles in enumerate(((3,), (2, 0), (1, 4))):
                    for t in tiles:
                        n = TILES[t][1]
                        c, w = NEAR[t]
                        near = wk[0:n, S_COL[t] + c:S_COL[t] + c + w]
                        b = P if t == 0 else 0
                        ins = dve.tensor_tensor(near, near, bias[0:n, bass.ds(h, 1), b:b + w].rearrange("p a c -> p (a c)"), ALU.add)
                    order.after(ins)
                    for t in tiles:
                        n = TILES[t][1]
                        ins = dve.tensor_reduce(neg_max[0:n, t:t + 1], wk[0:n, S_COL[t]:S_COL[t] + WIDTH[t]], AX.X, ALU.max, negate=True)
                    ins.then_inc(max_ready, 1)

            def probsT_copies(i, e):
                dve.wait_ge(pT_mm, 6 * i + 3 * e + 1)
                dve.tensor_copy(probsT[:, 0:512], wk[:, 0:512]).then_inc(pT_a, 1)
                dve.wait_ge(pT_mm, 6 * i + 3 * e + 3)
                dve.tensor_copy(probsT[:, 1024:1408], wk[:, 1024:1408])
                dve.tensor_copy(probsT[0:DEC, 1408:1440], wk[0:DEC, 1408:1440]).then_inc(pT_c, 1)

            def att_to_natural(i, e):
                dve.wait_ge(probs_ready, 10 * i + 5 * e + 5)
                dve.reciprocal(row_inv[:, 0:4], row_sum[:, 0:4])
                order.after(dve.reciprocal(row_inv[0:DEC, 4:5], row_sum[0:DEC, 4:5]))
                dve.wait_ge(pv_mm, 2 * i + e + 1)
                dve.tensor_tensor(att_nat[:, 0:4, AD * e:AD * e + AD], wk[:, 1536:1792].rearrange("p (t c) -> p t c", t=4),
                                  row_inv[:, 0:4].unsqueeze(2).to_broadcast([P, 4, AD]), ALU.mult)
                dve.tensor_scalar(att_nat[0:DEC, 4, AD * e:AD * e + AD], wk[0:DEC, 1792:1856], row_inv[0:DEC, 4:5], None, ALU.mult)\
                    .then_inc(att_nat_ready, 1)

            with dve.Fori(0, PAIRS) as i:
                g = i + G_RET
                order.body(i, 8)
                for e in range(2):
                    rows = slice(AD * e, AD * e + AD)
                    dve.tensor_scalar(q_pad[rows, e, :], z[rows, bass.ds(i, 1), :].rearrange("p a c -> p (a c)"), AD ** -0.5, None, ALU.mult)
                copy(k_pair[:], z[:, bass.ds(Z_AK + i, 1), :].rearrange("p a c -> p (a c)"))
                copy(v_pair[:], z[:, bass.ds(Z_AV + i, 1), :].rearrange("p a c -> p (a c)")).then_inc(pair_ready, 1)
                to_z(g, 0, Z_RQ + 4 * i)
                split_ahead(g, 0)
                dve.wait_ge(kv_tr, i + 1)
                dve.wait_ge(k_out, 32 * i + 32)
                dve.tensor_copy(k_nat[:, 0:4, :], wk[:, 0:512].rearrange("p (t c) -> p t c", t=4))
                dve.tensor_copy(k_nat[0:DEC, 4, :], wk[0:DEC, 512:640]).then_inc(k_nat_ready, 1)
                to_z(g, 1, Z_RQ + 4 * i + 1)
                split_ahead(g, 1)
                masked_max(i, 0)
                probsT_copies(i, 0)
                att_to_natural(i, 0)
                to_z(g, 2, Z_RQ + 4 * i + 2)
                split_ahead(g, 2)
                masked_max(i, 1)
                probsT_copies(i, 1)
                att_to_natural(i, 1)
                dve.wait_ge(att_tr, i + 1)
                copy(z[:, bass.ds(i, 1), :].rearrange("p a c -> p (a c)"), wk[:, 0:T]).then_inc(attT_ready, 1)
                to_z(g, 3, Z_RQ + 4 * i + 3)
                split_ahead(g, 3)
            order.leave(PAIRS)

            dve.wait_ge(ret_const_in, 48)
            dve.wait_ge(k_out, 32 * PAIRS + 32)
            dve.wait_ge(v_out, 32 * PAIRS + 32)
            with dve.Fori(0, RH) as i:
                g = i + G_GATE
                order.body(i, 9)
                def row(slot, frm=0, to=P):
                    return z[frm:to, bass.ds(slot, 1), :].rearrange("p a c -> p (a c)")

                copy(rq[:], row(Z_RQ + i)).then_inc(q_copied, 1)
                copy(head_c[:], decay[:, bass.ds(i, 1), :].rearrange("p a c -> p (a c)"))
                for to, frm in ((0, RD // 2), (RD // 2, 0)):
                    dve.tensor_tensor(rope_k[to:to + RD // 2, :], row(Z_RK + i, frm, frm + RD // 2), rope[frm:frm + RD // 2, 1, :], ALU.mult)
                order.after(dve.tensor_tensor(rk[:], row(Z_RK + i), rope[:, 0, :], ALU.mult))
                dve.tensor_tensor(rk[:], rk[:], rope_k[:], ALU.add)
                copy(rv[:], row(Z_RV + i)).then_inc(ret_ready, 1)
                copy(gate_row[:], row(Z_RG + i)).then_inc(gate_copied, 1)
                to_z(g, 0, Z_GATE + 4 * i)
                split_ahead(g, 0)
                dve.wait_ge(rkv_tr, i + 1)
                dve.tensor_scalar(rk_nat[:, 0:4, :], wk[:, 0:512].rearrange("p (t c) -> p t c", t=4), head_c[:, P + 1:P + 2], None, ALU.mult)
                dve.tensor_scalar(rk_nat[0:DEC, 4, :], wk[0:DEC, 512:640], head_c[0:DEC, P + 2:P + 3], None, ALU.mult).then_inc(rk_nat_ready, 1)
                to_z(g, 1, Z_GATE + 4 * i + 1)
                split_ahead(g, 1)
                dve.wait_ge(ret_s_mm, i + 1)
                dve.wait_ge(state_out, 32 * i + 32)
                dve.tensor_tensor(ret_a[:, 0:SEQ].rearrange("p (t c) -> p t c", t=4), wk[:, 0:SEQ].rearrange("p (t c) -> p t c", t=4),
                                  head_c[:, 0:P].unsqueeze(1).to_broadcast([P, 4, P]), ALU.mult)
                dve.tensor_tensor(ret_a[0:DEC, SEQ:T], wk[0:DEC, SEQ:T], head_c[0:DEC, 0:DEC], ALU.mult)
                order.after(dve.tensor_copy(states[:, 0, :], wk[:, 1024:1024 + RD]))
                for t in range(1, 4):
                    order.after(dve.scalar_tensor_tensor(states[:, t, :], states[:, t - 1, :], head_c[:, P + 3:P + 4],
                                                         wk[:, 1024 + RD * t:1024 + RD * t + RD], ALU.mult, ALU.add))
                dve.scalar_tensor_tensor(state_new[:], state_in[:, bass.ds(i, 1), :].rearrange("p a c -> p (a c)"), head_c[:, P + 4:P + 5],
                                         wk[:, 1536:1536 + RD], ALU.mult, ALU.add).then_inc(ret_a_ready, 1)
                to_z(g, 2, Z_GATE + 4 * i + 2)
                dve.wait_ge(ret_o_mm, i + 1)
                dve.tensor_scalar(ret_o[:, 0:4, :], wk[:, 0:SEQ].rearrange("p (t c) -> p t c", t=4), head_c[:, P:P + 1], None, ALU.mult)
                order.after(dve.tensor_scalar(ret_o[0:DEC, 4, :], wk[0:DEC, SEQ:SEQ + RD], head_c[0:DEC, P:P + 1], None, ALU.mult))
                for t, (s, n) in enumerate(TILES):
                    ins = dve.bn_stats(gn_stats[0:n, t, :], ret_o[0:n, t, :])
                order.after(ins)
                split_ahead(g, 2)
                for t, (s, n) in enumerate(TILES):
                    ins = dve.bn_aggr(gn_mv[0:n, t, :], gn_stats[0:n, t, :])
                order.after(ins)
                dve.tensor_scalar(gn_std[:, 0:4], gn_mv[:, 0:4, 1], EPS, None, ALU.add)
                dve.tensor_scalar(gn_std[0:DEC, 4:5], gn_mv[0:DEC, 4, 1:2], EPS, None, ALU.add).then_inc(gn_var, 1)
                dve.wait_ge(gn_root, i + 1)
                dve.reciprocal(gn_rstd[:, 0:4], gn_std[:, 0:4])
                order.after(dve.reciprocal(gn_rstd[0:DEC, 4:5], gn_std[0:DEC, 4:5]))
                for t, (s, n) in enumerate(TILES):
                    ins = dve.tensor_scalar(ret_n[0:n, t, :], ret_o[0:n, t, :], gn_mv[0:n, t, 0:1], gn_rstd[0:n, t:t + 1],
                                            ALU.subtract, ALU.mult)
                ins.then_inc(ret_n_ready, 1)
                to_z(g, 3, Z_GATE + 4 * i + 3)
                split_ahead(g, 3)
                dve.wait_ge(ret_tr, i + 1)
                dve.wait_ge(swish_ready, i + 1)
                dve.tensor_tensor(z[:, bass.ds(Z_RQ + i, 1), :].rearrange("p a c -> p (a c)"), wk[:, 1024:1024 + T],
                                  gate_row[:], ALU.mult).then_inc(retT_ready, 1)
            order.leave(RH)

            for k in range(KT):
                dve.wait_ge(in_hi, k + 1)
                dve.tensor_tensor(act_lo[:, k, :], z[:, k if k < 4 else Z_RQ + k - 4, :], act_hi[:, k, :].bitcast(fp), ALU.subtract)\
                    .then_inc(in_lo, 1)
            with dve.Fori(0, 2) as i:
                for j in range(4):
                    m = 4 * i + j
                    dve.wait_ge(gates_ready, m + 1)
                    dve.wait_ge(mm_done, 4 * G_MERGE + m + 1)
                    dve.tensor_tensor(halves(part_a[:]), acc[j % 2][:, :, 0:HALF],
                                      z[:, bass.ds(Z_GATE + m, 1), :].rearrange("p a (n c) -> p (a n) c", n=2), ALU.mult)
                    ins = dve.tensor_tensor(halves(part_b[:]), wk_halves[j % 2][:, :, 0:HALF],
                                            z[:, bass.ds(Z_GATE + KT + m, 1), :].rearrange("p a (n c) -> p (a n) c", n=2), ALU.mult)
                    ins.then_inc(acc_free, 1)
                    evacuated(dve, i + G_MERGE, j)
                    dve.tensor_tensor(merged[:, j % 2, :], part_a[:], part_b[:], ALU.add).then_inc(merge_ready, 1)
                    split_ahead(i + G_MERGE, j)
                    dve.wait_ge(mid_hi_r, m + 1)
                    dve.tensor_tensor(mid_lo[:, bass.ds(m, 1), :].rearrange("p a c -> p (a c)"), merged[:, j % 2, :],
                                      mid_hi[:, bass.ds(m, 1), :].rearrange("p a c -> p (a c)").bitcast(fp), ALU.subtract).then_inc(mid_lo_r, 1)

            def third_low():
                dve.wait_ge(hi_ready, 4 * G_FFN + 3)
                dve.tensor_tensor(w_lo_third[:], w_raw[:, 1, :, 0:P], w_hi_third[:].bitcast(fp), ALU.subtract).then_inc(lo_ready, 1)

            with dve.Fori(0, 2) as i:
                for j in range(4):
                    dve.wait_ge(mm_done, 4 * (i + G_WO) + j + 1)
                    copy(y_mix[:, bass.ds(4 * i + j, 1), :].rearrange("p a (n c) -> p (a n) c", n=2),
                                    acc[j % 2][:, :, 0:HALF]).then_inc(acc_free, 1)
                    split_ahead(i + G_WO, j)
            norm(1, between=third_low)

            def add_normalised(out, y, gain, used, even):
                def scale(p, e):
                    return dve.scalar_tensor_tensor(scaled[:, e, :], y[:, 2 * p + e, :], gains[:, gain, 2 * p + e:2 * p + e + 1], rstd[:],
                                                    ALU.mult, ALU.mult)

                def pair(p, between=None):
                    if p:
                        dve.wait_ge(used, p)
                        dve.wait_ge(even, p)
                    scale(p, 1).then_inc(scaled_ready, 1)
                    if between:
                        between()
                    order.after(scale(p, 0))
                    dve.tensor_tensor(out[:, 2 * p, :], xT[:, 2 * p, :], scaled[:, 0, :], ALU.add).then_inc(even, 1)
                return pair

            def h2_low(m):
                dve.wait_ge(h2_hi, m + 1)
                dve.scalar_tensor_tensor(act_lo[:, m, :], xT[:, m, :], gains[:, 2, m:m + 1], act_hi[:, m, :].bitcast(fp),
                                         ALU.mult, ALU.subtract).then_inc(h2_lo, 1)

            pair = add_normalised(xT, y_mix, 1, x1_odd, x1_even)
            pair(0)
            for p in range(1, KT // 2):
                pair(p, between=lambda: h2_low(2 * p - 2))
                h2_low(2 * p - 1)
            h2_low(KT - 2)
            h2_low(KT - 1)
            norm(2, between=lambda: split_ahead(G_FFN, 1))

            def up(g, chunk, i, first=False):
                def evacuate(j):
                    dve.wait_ge(mm_done, 4 * g + j + 1)
                    src = wk_halves[1] if first and j == 2 else acc[j % 2]
                    dve.scalar_tensor_tensor(halves(relu[:, j % 2, :]), src[:, :, 0:HALF], 0.0, halves(rstd[:]),
                                             ALU.max, ALU.mult).then_inc(acc_free, 1)

                def hidden_low(j):
                    dve.wait_ge(f_hi, 8 * chunk + 4 * i + j + 1)
                    dve.tensor_tensor(mid_lo[:, bass.ds(4 * i + j, 1), :].rearrange("p a c -> p (a c)"), relu2[:, j % 2, :],
                                      mid_hi[:, bass.ds(4 * i + j, 1), :].rearrange("p a c -> p (a c)").bitcast(fp), ALU.subtract).then_inc(f_lo, 1)

                if first:
                    evacuate(0)
                    evacuate(1)
                    hidden_low(0)
                    hidden_low(1)
                for j in range(2 if first else 0, 4):
                    evacuate(j)
                    split_ahead(g, j)
                    hidden_low(j)

            def down_tile(g, j, m, ahead=True):
                dve.wait_ge(mm_done, 4 * g + j + 1)
                y = y_ffn[:, bass.ds(m, 1), :].rearrange("p a (n c) -> p (a n) c", n=2)
                dve.tensor_tensor(y, y, acc[j % 2][:, :, 0:HALF], ALU.add).then_inc(acc_free, 1)
                if ahead:
                    split_ahead(g, j)

            def down(g):
                with dve.Fori(0, 2) as i:
                    for j in range(4):
                        down_tile(g + i, j, 4 * i + j)

            dve.wait_ge(y_zero, 1)
            up(G_FFN, 0, 0, first=True)
            up(G_FFN + 1, 0, 1)
            down(G_FFN + 2)
            with dve.Fori(1, 3) as c:
                with dve.Fori(0, 2) as i:
                    up(G_FFN + 4 * c + i, c, i)
                down(G_FFN + 2 + 4 * c)
            with dve.Fori(0, 2) as i:
                up(G_FFN + 12 + i, 3, i)
            for m in range(KT):
                down_tile(G_FFN + 14 + m // 4, m % 4, m, m < KT - 2)
            norm(3)

            pair = add_normalised(y_ffn, y_ffn, 3, outT_odd, outT_even)
            for p in range(KT // 2):
                pair(p)


_INS = ['x_prompt', 'x_sample', 'cache_attn_k', 'cache_attn_v', 'state_retention', 'w_in', 'rel_bias_table',
        'w_attn_out', 'w_ret_out', 'w_o', 'w_ff_up', 'w_ff_down']
_GAINS = ['norm_mix_pre', 'norm_mix_post', 'norm_ffn_pre', 'norm_ffn_post']
_OUTS = [("y_prompt", (1, SEQ, D)), ("y_sample", (1, DEC, D)), ("new_k_prompt", (SEQ, AH * AD)), ("new_v_prompt", (SEQ, AH * AD)),
         ("new_state_prompt", (RH, RD, RD)), ("new_k_sample", (DEC, AH * AD)), ("new_v_sample", (DEC, AH * AD)),
         ("new_state_sample", (RH, RD, RD))]


def kernel(**inputs):
    import concourse.bacc as bacc
    from concourse.bass_utils import run_bass_kernel_spmd

    nc = bacc.Bacc("TRN2", target_bir_lowering=False, num_devices=1)
    arrays = {}
    for name in _INS:
        a = np.ascontiguousarray(inputs[name])
        if name.startswith("cache"):
            a = a.reshape(CACHE, AH * AD)
        elif name.startswith("state"):
            a = a.reshape(RH, RD, RD)
        elif not name.startswith("x_"):
            a = a[0]
        arrays[name] = a
    arrays["gains"] = np.ascontiguousarray(np.stack([np.asarray(inputs[n])[0].reshape(KT, P).T for n in _GAINS], axis=1))
    arrays.update(shape_constants())
    args = {n: nc.dram_tensor("in_" + n, a.shape, mybir.dt.from_np(a.dtype), kind="ExternalInput").ap() for n, a in arrays.items()}
    outs = {n: nc.dram_tensor("out_" + n, s, mybir.dt.float32, kind="ExternalOutput").ap() for n, s in _OUTS}
    build(nc, args, outs)
    r = run_bass_kernel_spmd(nc, [{"in_" + n: a for n, a in arrays.items()}], core_ids=[0]).results[0]
    y_p, y_s, k_p, v_p, s_p, k_s, v_s, s_s = (r["out_" + n] for n, _ in _OUTS)
    heads = (1, 1, -1, AH, AD)
    return (y_p, y_s, k_p.reshape(heads), v_p.reshape(heads), s_p.reshape(1, 1, RH, RD, RD),
            k_s.reshape(heads), v_s.reshape(heads), s_s.reshape(1, 1, RH, RD, RD))
```

```python
from contextlib import ExitStack

import concourse.bass as bass
import numpy as np
from concourse import mybir

D = 1024
P = 128
KT = D // P
SEQ, DEC = 512, 32
T = SEQ + DEC
HALF = T // 2
PARTS = [(0, 2 * P), (2 * P, T - 2 * P)]
TILES = [(0, P), (P, P), (2 * P, P), (3 * P, P), (SEQ, DEC)]
AH, AD = 8, 64
PAIRS = AH // 2
CACHE = 512
RH, RD = 4, 128
CLIP = 128
TABLE = 2 * CLIP + 1
PAST = 1024
EPS = 1e-6
STAGE = 2 * P
RC = 136
NEG = -1.0e30
Z_AQ, Z_AK, Z_AV, Z_GATE, Z_SPARE, Z_RQ, Z_RK, Z_RV, Z_RG, Z_SLOTS = 0, 4, 8, 4, 12, 20, 24, 28, 32, 36


def shape_constants():
    f = np.float32
    ident = np.eye(P, dtype=f)
    flip = np.ascontiguousarray(ident[::-1])
    half = RD // 2
    inv = (f(10000.0) ** (-np.arange(half, dtype=f) / f(half))).astype(f)
    pos = np.concatenate([np.arange(SEQ), PAST + np.arange(DEC)]).astype(f)
    ang = (inv[:, None] * pos[None, :]).astype(f)
    cos = np.cos(ang.astype(np.float64)).astype(f)
    sin = np.sin(ang.astype(np.float64)).astype(f)
    rope = np.zeros((P, 2, T), f)
    rope[:half, 0] = rope[half:, 0] = cos
    rope[half:, 1] = -sin
    rope[:half, 1] = sin
    decay = np.zeros((P, RH, RC), f)
    t = np.arange(P)
    for h in range(RH):
        lg = np.log1p(-np.exp2(-5.0 - h))
        key = RD ** -0.5
        decay[:, h, :P] = np.where(t[None, :] >= t[:, None], key * np.exp(-(t[:, None] + 1.0) * lg), 0.0)
        decay[:, h, P] = np.exp((t + 1.0) * lg)
        decay[:, h, P + 1] = key * np.exp((P - 1.0 - t) * lg)
        decay[:DEC, h, P + 2] = key * np.exp((DEC - 1.0 - t[:DEC]) * lg)
        decay[:, h, P + 3] = np.exp(P * lg)
        decay[:, h, P + 4] = np.exp(DEC * lg)
    return {"ident": ident, "flip": flip, "ones": np.ones((P, P), f), "rope": rope, "decay": decay}


class Order:

    def __init__(self, eng, sem):
        self.eng, self.sem, self.base, self.n = eng, sem, 0, 0

    def after(self, ins):
        ins.then_inc(self.sem, 1)
        self.n += 1
        self.eng.wait_ge(self.sem, self.base + self.n)

    def flatten(self):
        self.base, self.n = self.base + self.n, 0

    def body(self, i, per):
        self.start = self.base
        self.base, self.n, self.per = self.start + i * per, 0, per

    def leave(self, count):
        assert self.n == self.per, (self.n, self.per)
        self.base, self.n = self.start + count * self.per, 0


def build(nc, a, outs):
    fp, fr = mybir.dt.float32, mybir.dt.float32r
    ALU, ACT, AX = mybir.AluOpType, mybir.ActivationFunctionType, mybir.AxisListType
    ctx = ExitStack()

    with ctx:
        def sem(name):
            return ctx.enter_context(nc.semaphore(name))

        arena_bytes = 212 * 1000
        arena = ctx.enter_context(nc.sbuf_tensor("arena", [P, arena_bytes // 4], fp))
        first = nc.sbuf_base - arena_bytes
        top = [first]

        def place(name, shape, dtype=fp, at=None):
            size = 4 * int(np.prod(shape[1:]))
            size += -size % 32
            where = top[0] if at is None else at
            if at is None:
                top[0] += size
                assert top[0] <= first + arena_bytes, (name, top[0] - first - arena_bytes)
            ends[name] = where + size
            return nc.alloc_sbuf_tensor_at(name, shape, dtype, offset=where)

        ends = {}
        xT = place("xT", [P, KT, T])
        act_hi = place("act_hi", [P, KT, T], fr)
        act_lo = place("act_lo", [P, KT, T], fr)
        w_raw = place("w_raw", [P, 2, KT, STAGE])
        w_hi = place("w_hi", [P, 2, KT, P], fr)
        w_lo = place("w_lo", [P, 2, KT, P], fr)
        rstd = place("rstd", [P, T])
        sqsum = place("sqsum", [P, T])
        ident = place("ident_sb", [P, P])
        ones = place("ones_sb", [P, P])
        gains = place("gains_sb", [P, 4, KT])
        tok_var = place("tok_var", [P, 8])
        tok_rstd = place("tok_rstd", [P, 8])
        tok_last = place("tok_last", [P, 8])
        rope = place("rope_sb", [P, 2, T])
        decay = place("decay_sb", [P, RH, RC])
        state_in = place("state_in", [P, RH, RD])
        k_stack_hi = place("k_stack_hi", [P, CACHE + T], fr, at=ends["decay_sb"] - 4 * RH * RC - 8 * T)
        k_stack_lo = place("k_stack_lo", [P, CACHE + T], fr, at=ends["k_stack_hi"])
        assert ends["k_stack_lo"] <= ends["state_in"]
        w_hi_third = place("w_hi_third", [P, KT, P], fr, at=ends["state_in"] - 8 * KT * P)
        w_lo_third = place("w_lo_third", [P, KT, P], fr, at=ends["w_hi_third"])
        z_at = top[0]
        assert ends["w_lo_third"] == z_at and ends["ones_sb"] <= ends["w_hi_third"] - 4 * KT * P
        z = place("z", [P, Z_SLOTS, T])
        work_at = top[0]

        mid_hi = place("mid_hi", [P, KT, T], fr, at=z_at + 4 * T * Z_RQ)
        mid_lo = place("mid_lo", [P, KT, T], fr, at=z_at + 4 * T * (Z_RQ + KT))
        y_mix = place("y_mix", [P, KT, T], at=z_at + 4 * T * Z_GATE)
        y_ffn = place("y_ffn", [P, KT, T], at=z_at + 4 * T * (Z_GATE + KT))
        y_out = place("y_out", [P, 5, D], at=z_at + 4 * T * Z_RQ)
        x_nat = place("x_nat", [P, 5, D], at=z_at)
        hankel = place("hankel", [P, AH, 2 * P], at=z_at + 4 * T * Z_RQ)
        k_cache = place("k_cache", [P, 4, AH * AD], at=ends["hankel"])
        table_row = place("table_row", [AH, 3 * P], at=ends["k_cache"])
        flip = place("flip_sb", [P, P], at=ends["table_row"])
        x_waste = place("x_waste", [P, 2, D], at=ends["flip_sb"])
        assert ends["x_nat"] <= z_at + 4 * T * Z_SPARE and ends["x_waste"] <= work_at
        bias = place("bias", [P, AH, 2 * P], at=z_at + 4 * T * Z_SPARE)
        kcT = place("kcT", [P, PAIRS, CACHE], at=ends["bias"])
        assert ends["kcT"] <= z_at + 4 * T * Z_RQ

        v_cache = place("v_cache", [P, 4, P])
        q_stack = place("q_stack", [P, 2, T], fr)
        k_pair = place("k_pair", [P, T])
        v_pair = place("v_pair", [P, T])
        probs = place("probs", [P, 4 * P + 3 * P + 2 * P + P + CACHE + DEC])
        probsT = place("probsT", [P, 1440])
        k_nat = place("k_nat", [P, 5, P])
        v_nat = place("v_nat", [P, 5, P])
        att_nat = place("att_nat", [P, 5, P])
        neg_max = place("neg_max", [P, 8])
        row_sum = place("row_sum", [P, 8])
        row_inv = place("row_inv", [P, 8])

        top[0] = work_at
        head_c = place("head_c", [P, RC])
        gate_sig = place("gate_sig", [P, T])
        rq = place("rq", [P, T])
        rk = place("rk", [P, T])
        rv = place("rv", [P, T])
        rope_q = place("rope_q", [P, T])
        rope_k = place("rope_k", [P, T])
        gate_row = place("gate_row", [P, T])
        rk_nat = place("rk_nat", [P, 5, P])
        rv_nat = place("rv_nat", [P, 5, P])
        ret_a = place("ret_a", [P, 4 * P + DEC])
        states = place("states", [P, 4, RD])
        state_new = place("state_new", [P, RD])
        ret_o = place("ret_o", [P, 5, RD])
        ret_n = place("ret_n", [P, 5, RD])
        gn_stats = place("gn_stats", [P, 5, 6])
        gn_mv = place("gn_mv", [P, 5, 2])
        gn_std = place("gn_std", [P, 5])
        gn_rstd = place("gn_rstd", [P, 5])

        top[0] = work_at
        part_a = place("part_a", [P, T])
        part_b = place("part_b", [P, T])
        merged = place("merged", [P, 2, T])
        sq = place("sq", [P, 2, T])
        scaled = place("scaled", [P, 4, T])
        relu = place("relu", [P, 2, T])
        relu2 = place("relu2", [P, 2, T])

        acc = [ctx.enter_context(nc.psum_tensor(f"acc{i}", [P, 2, 512], fp)) for i in range(2)]
        wk = ctx.enter_context(nc.psum_tensor("wk", [P, 2048], fp))
        wk_halves = [wk[:, 1024 * i:1024 * i + 1024].rearrange("p (n c) -> p n c", n=2) for i in range(2)]

        table_ext = nc.dram_tensor("table_ext", (AH, 3 * P), fp, kind="Internal").ap()

        ident_in, const_in = sem("ident_in"), sem("const_in")
        x_in = [sem(f"x_in{t}") for t in range(5)]
        w_first, w_in_sem = sem("w_first"), [sem("w_loaded0"), sem("w_loaded1")]
        cache_k_in, table_in, table_filled, table_out, hankel_in = (
            sem("cache_k_in"), sem("table_in"), sem("table_filled"), sem("table_out"), sem("hankel_in"))
        gains_in, x_tr, x_copied_act, x_copied_dve = sem("gains_in"), sem("x_tr"), sem("x_copied_act"), sem("x_copied_dve")
        x_hi, x_lo, x_sum_act, var_clear = sem("x_hi"), sem("x_lo"), sem("x_sum_act"), sem("var_clear")
        kc_tr, kc_ready, bias_mm, bias_ready = sem("kc_tr"), sem("kc_ready"), sem("bias_mm"), sem("bias_ready")
        sum_mm, var_ready, std_ready, tok_rstd_ready, spread_mm, rstd_ready = (
            sem("sum_mm"), sem("var_ready"), sem("std_ready"), sem("tok_rstd_ready"), sem("spread_mm"), sem("rstd_ready"))
        hi_ready, lo_ready, mm_done, acc_free = sem("hi_ready"), sem("lo_ready"), sem("mm_done"), sem("acc_free")
        dve_order, pool_order = sem("dve_order"), sem("pool_order")
        q_hi_ready, q_lo_ready, k_hi_ready, k_lo_ready, k_stacked = (
            sem("q_hi_ready"), sem("q_lo_ready"), sem("k_hi_ready"), sem("k_lo_ready"), sem("k_stacked"))
        pair_ready, kv_tr, k_nat_ready, v_nat_ready = sem("pair_ready"), sem("kv_tr"), sem("k_nat_ready"), sem("v_nat_ready")
        scores_mm, max_ready, probs_ready = sem("scores_mm"), sem("max_ready"), sem("probs_ready")
        pT_mm, pT_a, pT_b, pT_c = sem("pT_mm"), sem("pT_a"), sem("pT_b"), sem("pT_c")
        pv_mm, att_nat_ready, att_tr, attT_ready = sem("pv_mm"), sem("att_nat_ready"), sem("att_tr"), sem("attT_ready")
        k_out, v_out, v_cache_in = sem("k_out"), sem("v_out"), sem("v_cache_in")
        ret_const_in, gate_sig_ready, swish_ready, q_rotated = sem("ret_const_in"), sem("gate_sig_ready"), sem("swish_ready"), sem("q_rotated")
        q_copied, gate_copied = sem("q_copied"), sem("gate_copied")
        ret_ready, rkv_tr, rk_nat_ready, rv_nat_ready = sem("ret_ready"), sem("rkv_tr"), sem("rk_nat_ready"), sem("rv_nat_ready")
        ret_s_mm, ret_a_ready, ret_o_mm, gn_var, gn_root = (
            sem("ret_s_mm"), sem("ret_a_ready"), sem("ret_o_mm"), sem("gn_var"), sem("gn_root"))
        ret_n_ready, ret_tr, retT_ready, state_out = sem("ret_n_ready"), sem("ret_tr"), sem("retT_ready"), sem("state_out")
        h_half_used, in_lo_pool = sem("h_half_used"), sem("in_lo_pool")
        in_hi, in_lo, gates_ready, merge_ready, mid_hi_r, mid_lo_r = (
            sem("in_hi"), sem("in_lo"), sem("gates_ready"), sem("merge_ready"), sem("mid_hi_ready"), sem("mid_lo_ready"))
        sq_ready, sq_added = sem("sq_ready"), sem("sq_added")
        scaled_ready, x1_even, x1_odd = sem("scaled_ready"), sem("x1_even"), sem("x1_odd")
        h2_hi, h2_lo = sem("h2_hi"), sem("h2_lo")
        relu2_ready, f_hi, f_lo = sem("relu2_ready"), sem("f_hi"), sem("f_lo")
        y_zero, outT_even, outT_odd, out_tr = sem("y_zero"), sem("outT_even"), sem("outT_odd"), sem("out_tr")
        part_mm, part_read = sem("part_mm"), sem("part_read")
        out_nat, sample_nat, y_stored = sem("out_nat"), sem("sample_nat"), sem("y_stored")

        block = ctx.enter_context(nc.Block())

        CREDITS = {w_in_sem[0]: 16, k_out: 32, v_out: 32, state_out: 32, attT_ready: 1, retT_ready: 1, sq_added: 2, f_lo: 2, acc_free: 2}

        G_RET, G_GATE, G_MERGE, G_WO, G_FFN = 3, 7, 11, 13, 15

        def halves(ap):
            return ap.rearrange("p (n c) -> p n c", n=2)

        def evacuated(eng, g, j):
            eng.wait_ge(acc_free, 4 * g + j + 3)

        w_in_v = a["w_in"].rearrange("(k p) n -> p k n", p=P)
        w_ao_v = a["w_attn_out"].rearrange("(k p) n -> p k n", p=P)
        w_ro_v = a["w_ret_out"].rearrange("(k p) n -> p k n", p=P)
        w_o_v = a["w_o"].rearrange("(k p) n -> p k n", p=P)
        w_up_v = a["w_ff_up"].rearrange("(k p) n -> p k n", p=P)
        w_dn_v = a["w_ff_down"].rearrange("(k p) n -> p k n", p=P)

        S_COL = {3: 0, 2: 512, 0: 896, 1: 1024, 4: 1504}
        P_COL = {0: 0, 1: P, 2: 3 * P, 3: 6 * P, 4: 10 * P}
        WIDTH = {0: P, 1: 2 * P, 2: 3 * P, 3: 4 * P, 4: CACHE + DEC}
        NEAR = {0: (0, P), 1: (0, 2 * P), 2: (P, 2 * P), 3: (2 * P, 2 * P)}
        PT_COL = {3: 0, 2: 512, 0: 896, 1: 1024, 4: 1280}
        ORDER = (3, 2, 0, 1, 4)
        SUM_COL = 1000

        def x_psum(t):
            n = TILES[t][1]
            if t in (0, 1):
                return acc[t][:].rearrange("p n (k c) -> p (n k) c", k=4)
            if t in (2, 3):
                return wk[:, 1024 * (t - 2):1024 * (t - 1)].rearrange("p (k c) -> p k c", k=KT)
            return acc[0][:, 0, 0:KT * n].rearrange("p (k c) -> p k c", k=KT)

        PART_TILES = (range(0, 2), range(2, 5))
        PART_RSTD = (0, 512)

        def out_psum(part, p):
            banks = [wk[:, 1024:1536], wk[:, 1536:2048], acc[0][:, 0, :], acc[1][:, 0, :], acc[0][:, 1, :], acc[1][:, 1, :]]
            return banks[(p, (4, 5, 0, 1)[p])[part]]

        def sample_psum(q):
            return acc[q][0:DEC, 0, :]

        def squares_added(norm, count):
            return 2 + (KT - 1) * (norm - 1) + count

        @block.sync
        def _(sp):
            for t, (s, n) in enumerate(TILES):
                src = a["x_prompt"][0, s:s + n, :] if t < 4 else a["x_sample"][0]
                sp.dma_start(x_nat[0:n, t, :], src).then_inc(x_in[t], 16)

            def load(buf, src_a, src_b, col):
                sp.dma_start(w_raw[:, buf, 0:4, :], src_a[:, :, bass.ds(col, STAGE)]).then_inc(w_in_sem[buf], 16)
                sp.dma_start(w_raw[:, buf, 4:8, :], src_b[:, :, bass.ds(col, STAGE)]).then_inc(w_in_sem[buf], 16)

            def load_body(g, src_a, src_b, col):
                for buf in range(2):
                    sp.wait_ge(lo_ready, 4 * g - 2 + 2 * buf)
                    load(buf, src_a, src_b, col + STAGE * buf)

            sp.dma_start(w_raw[:, 0, :, 0:P], w_in_v[:, :, 0:P]).then_inc(w_first, 16)
            sp.dma_start(w_raw[:, 0, :, P:STAGE], w_in_v[:, :, P:STAGE]).then_inc(w_in_sem[0], 16)
            sp.dma_start(k_cache[:], a["cache_attn_k"].rearrange("(t p) c -> p t c", p=P)).then_inc(cache_k_in, 16)
            load(1, w_in_v[:, 0:4], w_in_v[:, 4:8], STAGE)
            with sp.Fori(1, G_MERGE) as g:
                load_body(g, w_in_v[:, 0:4], w_in_v[:, 4:8], 512 * g)
            with sp.Fori(0, 2) as i:
                load_body(i + G_MERGE, w_ao_v, w_ro_v, 512 * i)
            with sp.Fori(0, 2) as i:
                load_body(i + G_WO, w_o_v[:, 0:4], w_o_v[:, 4:8], 512 * i)
            with sp.Fori(0, 4) as c:
                with sp.Fori(0, 2) as i:
                    load_body(G_FFN + 4 * c + i, w_up_v[:, 0:4], w_up_v[:, 4:8], 1024 * c + 512 * i)
                with sp.Fori(0, 2) as i:
                    load_body(G_FFN + 2 + 4 * c + i, w_dn_v[:, bass.ds(8 * c, 4)],
                              w_dn_v[:, bass.ds(8 * c + 4, 4)], 512 * i)

            def store(tiles, cols):
                sp.dma_start(outs["y_prompt"][0].rearrange("(t p) c -> p t c", p=P)[:, tiles, cols], y_out[:, tiles, cols]).then_inc(y_stored, 16)

            for q in range(2):
                sp.wait_ge(out_nat, 2 * q + 2)
                store(slice(0, 2), slice(512 * q, 512 * q + 512))
            for p in range(KT // 2):
                sp.wait_ge(out_nat, 5 + p)
                store(slice(2, 4), slice(256 * p, 256 * p + 256))
            sp.wait_ge(sample_nat, 2)
            sp.dma_start(outs["y_sample"][0], y_out[0:DEC, 4, :]).then_inc(y_stored, 16)
            sp.wait_ge(y_stored, 16 * 7)

        @block.gpsimd
        def _(pool):
            order = Order(pool, pool_order)
            pool.dma_start(table_row[:, 0:TABLE], a["rel_bias_table"]).then_inc(table_in, 16)
            pool.wait_ge(table_in, 16)
            pool.tensor_copy(table_row[:, TABLE:3 * P],
                             table_row[:, TABLE - 1:TABLE].to_broadcast([AH, 3 * P - TABLE])).then_inc(table_filled, 1)
            pool.wait_ge(table_filled, 1)
            pool.dma_start(table_ext, table_row[:]).then_inc(table_out, 16)
            pool.wait_ge(table_out, 16)
            pool.dma_start(hankel[:], bass.AP(table_ext.tensor, 1, [[1, P], [3 * P, AH], [1, 2 * P]])).then_inc(hankel_in, 16)
            pool.wait_ge(scores_mm, 2 * PAIRS)
            pool.dma_start(rope[:], a["rope"]).then_inc(ret_const_in, 16)
            pool.dma_start(decay[:], a["decay"]).then_inc(ret_const_in, 16)
            pool.dma_start(state_in[:], a["state_retention"].rearrange("h d e -> d h e")).then_inc(ret_const_in, 16)
            pool.wait_ge(ret_const_in, 48)
            pool.wait_ge(acc_free, 2 + 4 * G_GATE)
            pool.wait_ge(attT_ready, PAIRS + 1)
            pool.wait_ge(k_out, 32 * PAIRS + 32)
            pool.wait_ge(v_out, 32 * PAIRS + 32)

            with pool.Fori(0, RH) as i:
                order.body(i, 3)
                pool.wait_ge(q_copied, i + 1)
                for to, frm in ((0, RD // 2), (RD // 2, 0)):
                    order.after(pool.tensor_tensor(rope_q[to:to + RD // 2, :], rq[frm:frm + RD // 2, :], rope[frm:frm + RD // 2, 1, :], ALU.mult))
                order.after(pool.tensor_tensor(rq[:], rq[:], rope[:, 0, :], ALU.mult))
                pool.tensor_tensor(rq[:], rq[:], rope_q[:], ALU.add).then_inc(q_rotated, 1)
                pool.wait_ge(gate_sig_ready, i + 1)
                pool.tensor_tensor(gate_row[:], gate_row[:], gate_sig[:], ALU.mult).then_inc(swish_ready, 1)
            order.leave(RH)
            for k in (2, 3):
                pool.wait_ge(in_hi, k + 1)
                pool.tensor_tensor(act_lo[:, k, :], z[:, k, :], act_hi[:, k, :].bitcast(fp), ALU.subtract).then_inc(in_lo_pool, 1)
            pool.wait_ge(state_out, 32 * RH + 32)

            def add_square(norm, m):
                pool.wait_ge(sq_ready, KT * (norm - 1) + m + 1)
                pool.tensor_tensor(sqsum[:], sqsum[:], sq[:, m % 2, :], ALU.add).then_inc(sq_added, 1)
                pool.wait_ge(sq_added, squares_added(norm, m + 1))

            pool.wait_ge(mid_lo_r, KT)
            pool.memset(y_ffn[:], 0.0).then_inc(y_zero, 1)
            order.after(pool.memset(sqsum[:], 0.0))
            for m in range(KT - 1):
                add_square(1, m)
            pool.wait_ge(sum_mm, 1)
            order.after(pool.memset(sqsum[:], 0.0))
            for m in range(KT):
                if m % 2:
                    pool.wait_ge(scaled_ready, m // 2 + 1)
                    pool.tensor_tensor(xT[:, m, :], xT[:, m, :], scaled[:, m % 4, :], ALU.add).then_inc(x1_odd, 1)
                if m > 1:
                    add_square(2, m - 2)
            add_square(2, KT - 2)
            pool.wait_ge(sum_mm, 2)
            order.after(pool.memset(sqsum[:], 0.0))
            for m in range(KT - 2):
                add_square(3, m)

            def add_last_square(part):
                s, n = PARTS[part]
                pool.wait_ge(sq_ready, 3 * KT - 1 + 2 * part)
                pool.tensor_tensor(sqsum[:, s:s + n], sqsum[:, s:s + n], sq[:, 0, s:s + n], ALU.add).then_inc(sq_added, 1)

            def add_odd(part, p):
                s, n = PARTS[part]
                pool.wait_ge(scaled_ready, KT // 2 * (1 + part) + p + 1)
                pool.tensor_tensor(y_ffn[:, 2 * p + 1, s:s + n], xT[:, 2 * p + 1, s:s + n], scaled[:, (2 * p + 1) % 4, s:s + n], ALU.add)\
                    .then_inc(outT_odd, 1)

            add_last_square(0)
            add_odd(0, 0)
            add_odd(0, 1)
            add_last_square(1)
            add_odd(0, 2)
            add_odd(0, 3)
            for p in range(KT // 2):
                add_odd(1, p)

        @block.scalar
        def _(act):
            def split_hi(u, v, wait_load=None):
                if wait_load is not None:
                    act.wait_ge(w_in_sem[v // 2], wait_load)
                act.activation(w_hi[:, v % 2], w_raw[:, v // 2, :, P * (v % 2):P * (v % 2) + P], ACT.Copy).then_inc(hi_ready, 1)

            def split_ahead(g, j):
                act.wait_ge(mm_done, 4 * g + j + 1)
                v = (j + 2) % 4
                split_hi(4 * g + j + 2, v, {0: 32 * (g + 1), 2: 32 * (g + 2)}.get(j))

            act.dma_start(ident[:], a["ident"]).then_inc(ident_in, 16)
            act.dma_start(gains[:], a["gains"]).then_inc(gains_in, 16)
            act.dma_start(ones[:], a["ones"]).then_inc(const_in, 16)
            act.dma_start(flip[:], a["flip"]).then_inc(const_in, 16)
            for counter, n in CREDITS.items():
                act.sem_inc(counter, n)
            act.preload_act_table(ACT.Sqrt)

            def square_sum(t):
                n = TILES[t][1]
                act.wait_ge(x_in[t], 16)
                act.activation(x_waste[0:n, 0, :], x_nat[0:n, t, :], ACT.Square, accum_out=tok_var[0:n, t:t + 1]).then_inc(x_sum_act, 1)

            def copy_x(t):
                s, n = TILES[t]
                act.wait_ge(x_tr, t + 1)
                act.activation(xT[:, :, s:s + n], x_psum(t), ACT.Copy).then_inc(x_copied_act, 1)

            def root(norm, tiles=range(5)):
                act.wait_ge(var_ready, norm + 1)
                cols = slice(tiles[0], tiles[-1] + 1)
                act.activation(tok_rstd[:, cols], tok_var[:, cols], ACT.Sqrt).then_inc(std_ready, 1)

            act.wait_ge(var_clear, 1)
            square_sum(1)
            copy_x(0)
            act.wait_ge(x_sum_act, 1)
            square_sum(3)
            copy_x(2)
            copy_x(4)
            root(0)
            act.wait_ge(w_first, 16)
            split_hi(0, 0)
            act.wait_ge(gains_in, 16)
            act.wait_ge(x_copied_act, 3)
            act.wait_ge(x_copied_dve, 2)
            for k in range(KT):
                act.activation(act_hi[:, k, :], xT[:, k, :], ACT.Copy, scale=gains[:, 0, k:k + 1]).then_inc(x_hi, 1)
            split_hi(1, 1, 32)

            split_ahead(0, 0)
            split_ahead(0, 1)
            act.wait_ge(kc_tr, 1)
            act.activation(kcT[:], wk[:].rearrange("p (a b) -> p a b", a=PAIRS), ACT.Copy).then_inc(kc_ready, 1)
            split_ahead(0, 2)
            split_ahead(0, 3)
            with act.Fori(1, G_RET) as g:
                for j in range(4):
                    split_ahead(g, j)

            def exps(i, e):
                for k, t in enumerate(ORDER):
                    n = TILES[t][1]
                    if k in (0, 1, 3):
                        act.wait_ge(max_ready, 6 * i + 3 * e + (1, 2, 2, 3, 3)[k])
                    act.activation(probs[0:n, P_COL[t]:P_COL[t] + WIDTH[t]], wk[0:n, S_COL[t]:S_COL[t] + WIDTH[t]],
                                   ACT.Exp, bias=neg_max[0:n, t:t + 1], accum_out=row_sum[0:n, t:t + 1]).then_inc(probs_ready, 1)

            def probsT_copy(i, e):
                act.wait_ge(pT_mm, 6 * i + 3 * e + 2)
                act.activation(probsT[:, 512:1024], wk[:, 512:1024], ACT.Copy).then_inc(pT_b, 1)

            def store_kv(i):
                for nat, ready, stored, name in ((k_nat, k_nat_ready, k_out, "new_k"), (v_nat, v_nat_ready, v_out, "new_v")):
                    act.wait_ge(ready, i + 1)
                    act.dma_start(outs[name + "_prompt"].rearrange("(t p) c -> p t c", p=P)[:, :, bass.ds(P * i, P)],
                                  nat[:, 0:4, :]).then_inc(stored, 16)
                    act.dma_start(outs[name + "_sample"][:, bass.ds(P * i, P)], nat[0:DEC, 4, :]).then_inc(stored, 16)

            def keys_high(i, e):
                rows = slice(AD * e, AD * e + AD)
                act.activation(k_stack_hi[rows, CACHE:], k_pair[rows, :], ACT.Copy)
                act.activation(k_stack_hi[rows, 0:CACHE], kcT[rows, bass.ds(i, 1), :].rearrange("p a c -> p (a c)"), ACT.Copy)\
                    .then_inc(k_hi_ready, 1)

            def stack_keys(i, e):
                rows, others = slice(AD * e, AD * e + AD), slice(AD - AD * e, 2 * AD - AD * e)
                act.wait_ge(k_hi_ready, 2 * i + e + 1)
                act.activation(k_stack_hi[others, :], k_stack_hi[rows, :].bitcast(fp), ACT.Copy)
                act.wait_ge(k_lo_ready, 2 * i + e + 1)
                act.activation(k_stack_lo[others, :], k_stack_lo[rows, :].bitcast(fp), ACT.Copy).then_inc(k_stacked, 1)

            act.preload_act_table(ACT.Exp)
            with act.Fori(0, PAIRS) as i:
                g = i + G_RET
                act.wait_ge(attT_ready, i + 1)
                act.dma_start(v_cache[:], a["cache_attn_v"].rearrange("(t p) c -> p t c", p=P)[:, :, bass.ds(P * i, P)])\
                    .then_inc(v_cache_in, 16)
                for e in range(2):
                    rows = slice(AD * e, AD * e + AD)
                    act.activation(q_stack[rows, e, :], z[rows, bass.ds(i, 1), :].rearrange("p a c -> p (a c)"), ACT.Copy, scale=AD ** -0.5)\
                        .then_inc(q_hi_ready, 1)
                act.wait_ge(pair_ready, i + 1)
                keys_high(i, 0)
                stack_keys(i, 0)
                split_ahead(g, 0)
                act.wait_ge(kv_tr, i + 1)
                act.wait_ge(v_out, 32 * i + 32)
                act.activation(v_nat[:, 0:4, :], wk[:, 1024:1536].rearrange("p (t c) -> p t c", t=4), ACT.Copy)
                act.activation(v_nat[0:DEC, 4, :], wk[0:DEC, 1536:1664], ACT.Copy).then_inc(v_nat_ready, 1)
                split_ahead(g, 1)
                store_kv(i)
                act.wait_ge(scores_mm, 2 * i + 1)
                keys_high(i, 1)
                exps(i, 0)
                probsT_copy(i, 0)
                stack_keys(i, 1)
                split_ahead(g, 2)
                exps(i, 1)
                probsT_copy(i, 1)
                split_ahead(g, 3)

            def branch_high(k):
                act.activation(act_hi[:, k, :], z[:, k if k < 4 else Z_RQ + k - 4, :], ACT.Copy).then_inc(in_hi, 1)

            def retention(i, last=False):
                g = i + G_GATE
                split_ahead(g, 0)
                act.wait_ge(gate_copied, i + 1)
                act.activation(gate_sig[:], gate_row[:], ACT.Sigmoid).then_inc(gate_sig_ready, 1)
                act.wait_ge(rkv_tr, i + 1)
                act.activation(rv_nat[:, 0:4, :], wk[:, 1024:1536].rearrange("p (t c) -> p t c", t=4), ACT.Copy)
                act.activation(rv_nat[0:DEC, 4, :], wk[0:DEC, 1536:1664], ACT.Copy).then_inc(rv_nat_ready, 1)
                split_ahead(g, 1)
                act.wait_ge(ret_a_ready, i + 1)
                act.dma_start(outs["new_state_prompt"][bass.ds(i, 1)].rearrange("h d e -> (h d) e"), states[:, 3, :]).then_inc(state_out, 16)
                act.dma_start(outs["new_state_sample"][bass.ds(i, 1)].rearrange("h d e -> (h d) e"), state_new[:]).then_inc(state_out, 16)
                split_ahead(g, 2)
                act.wait_ge(gn_var, i + 1)
                act.activation(gn_std[:, 0:4], gn_std[:, 0:4], ACT.Sqrt)
                act.activation(gn_std[0:DEC, 4:5], gn_std[0:DEC, 4:5], ACT.Sqrt).then_inc(gn_root, 1)
                if last:
                    act.wait_ge(h_half_used, RH)
                    act.wait_ge(attT_ready, PAIRS + 1)
                    for k in range(4):
                        branch_high(k)
                    act.wait_ge(mm_done, 4 * G_MERGE)
                    branch_high(4)
                    branch_high(5)
                split_ahead(g, 3)

            with act.Fori(0, RH - 1) as i:
                retention(i)
            retention(RH - 1, last=True)
            branch_high(6)
            act.wait_ge(retT_ready, RH + 1)
            branch_high(7)
            act.wait_ge(acc_free, 2 + 4 * G_MERGE)
            with act.Fori(0, 2) as i:
                for j in range(4):
                    m = 4 * i + j
                    act.activation(z[:, bass.ds(Z_GATE + m, 1), :], z[:, bass.ds(Z_GATE + m, 1), :], ACT.Sigmoid)
                    act.activation(z[:, bass.ds(Z_GATE + KT + m, 1), :], z[:, bass.ds(Z_GATE + KT + m, 1), :], ACT.Sigmoid)\
                        .then_inc(gates_ready, 1)
                    split_ahead(i + G_MERGE, j)
                    act.wait_ge(merge_ready, m + 1)
                    act.activation(mid_hi[:, m, :], merged[:, j % 2, :], ACT.Copy).then_inc(mid_hi_r, 1)

            act.preload_act_table(ACT.Sqrt)
            with act.Fori(0, 2) as i:
                for j in range(4):
                    split_ahead(i + G_WO, j)
                    evacuated(act, i + G_WO, j)
                    act.wait_ge(sq_added, 4 * i + j + 1)
                    act.activation(sq[:, j % 2, :], y_mix[:, 4 * i + j, :], ACT.Square).then_inc(sq_ready, 1)
            act.wait_ge(w_in_sem[1], 32 * (G_FFN + 1))
            act.activation(w_hi_third[:], w_raw[:, 1, :, 0:P], ACT.Copy).then_inc(hi_ready, 1)
            root(1)
            for m in range(KT):
                act.wait_ge((x1_even, x1_odd)[m % 2], m // 2 + 1)
                act.activation(act_hi[:, m, :], xT[:, m, :], ACT.Copy, scale=gains[:, 2, m:m + 1]).then_inc(h2_hi, 1)
                if m >= 2:
                    act.wait_ge(sq_added, squares_added(2, m - 1))
                act.activation(sq[:, m % 2, :], xT[:, m, :], ACT.Square).then_inc(sq_ready, 1)
            root(2)

            def up(c, i, first=False):
                for j in range(4):
                    g = G_FFN + 4 * c + i
                    if not (first and j < 2):
                        split_ahead(g, j)
                    k = 8 * c + 4 * i + j
                    evacuated(act, g, j)
                    act.wait_ge(f_lo, k + 1)
                    act.activation(relu2[:, j % 2, :], relu[:, j % 2, :], ACT.Square).then_inc(relu2_ready, 1)
                    act.wait_ge(relu2_ready, k + 1)
                    act.activation(mid_hi[:, 4 * i + j, :], relu2[:, j % 2, :], ACT.Copy).then_inc(f_hi, 1)

            def down(c):
                with act.Fori(0, 2) as i:
                    for j in range(4):
                        split_ahead(G_FFN + 2 + 4 * c + i, j)

            split_ahead(G_FFN, 1)
            up(0, 0, first=True)
            up(0, 1)
            down(0)
            with act.Fori(1, 3) as c:
                with act.Fori(0, 2) as i:
                    up(c, i)
                down(c)
            with act.Fori(0, 2) as i:
                up(3, i)
            for m in range(KT - 2):
                split_ahead(G_FFN + 14 + m // 4, m % 4)
                evacuated(act, G_FFN + 14 + m // 4, m % 4)
                if m >= 2:
                    act.wait_ge(sq_added, squares_added(3, m - 1))
                act.activation(sq[:, m % 2, :], y_ffn[:, m, :], ACT.Square).then_inc(sq_ready, 1)

            def part_squares(part):
                s, n = PARTS[part]
                for j in range(2):
                    act.wait_ge(part_read, 2 * part + j + 1)
                    if part == 0:
                        act.wait_ge(sq_added, squares_added(3, 5 + j))
                    act.activation(sq[:, j, s:s + n], y_ffn[:, 6 + j, s:s + n], ACT.Square).then_inc(sq_ready, 1)

            part_squares(0)
            root(3, PART_TILES[0])
            part_squares(1)
            root(4, PART_TILES[1])

            def natural(part, p):
                act.wait_ge(out_tr, 4 * part + p + 1)
                act.activation(y_out[:, 2 * part:2 * part + 2, 2 * P * p:2 * P * p + 2 * P],
                               out_psum(part, p).rearrange("p (t c) -> p t c", t=2), ACT.Copy).then_inc(out_nat, 1)

            for p in range(4):
                natural(0, p)
            for p in range(4):
                natural(1, p)
                if p % 2:
                    act.activation(y_out[0:DEC, 4, 2 * P * (p - 1):2 * P * (p + 1)], sample_psum(p // 2), ACT.Copy).then_inc(sample_nat, 1)

        @block.tensor
        def _(pe):
            def products(dst, whi, wlo, k, hi, lo, start, stop):
                for w, h, begin, end in ((whi, hi, start, False), (whi, lo, False, False), (wlo, hi, False, stop)):
                    for n in range(2):
                        ins = pe.matmul(dst[:, n, 0:HALF], w[:, k, :], h[:, k, HALF * n:HALF * n + HALF], start=begin, stop=end)
                return ins

            def column_tile(g, j, hi, lo, kt=range(KT), dst=None, opens=True, closes=True, before=None, half_used=None):
                dst = acc[j % 2] if dst is None else dst
                if opens:
                    pe.wait_ge(lo_ready, 4 * g + j + 1)
                ks = list(kt)
                for k in ks:
                    if before:
                        before(k)
                    ins = products(dst, w_hi[:, j % 2], w_lo[:, j % 2], k, hi, lo, k == ks[0], k == ks[-1])
                    if half_used is not None and k == KT // 2 - 1:
                        ins.then_inc(half_used, 1)
                if closes:
                    ins.then_inc(mm_done, 1)

            def tr(out, in_):
                n = in_.shape[0]
                return pe.transpose(out, in_, ident[0:n, 0:n])

            pe.wait_ge(ident_in, 16)
            for t, (s, n) in enumerate(TILES):
                pe.wait_ge(x_in[t], 16)
                if t == 4:
                    pe.wait_ge(x_copied_act, 1)
                ps = x_psum(t)
                for k in range(KT):
                    ins = tr(ps[:, k, :], x_nat[0:n, t, P * k:P * k + P])
                ins.then_inc(x_tr, 1)

            def feature_sum(norm, added, squares, tiles=range(5)):
                for col, src in ((SUM_COL, sqsum[:]), (SUM_COL + 5, sq[:, 1, :])):
                    if col == SUM_COL:
                        pe.wait_ge(sq_added, added)
                    else:
                        pe.wait_ge(sq_ready, squares)
                    for t in tiles:
                        s, n = TILES[t]
                        ins = pe.matmul(wk[0:n, col + t:col + t + 1], src[:, s:s + n], ones[:, 0:1], start=True, stop=True)
                ins.then_inc(sum_mm, 1)

            def spread(norm, tiles=range(5), at=0):
                pe.wait_ge(tok_rstd_ready, norm + 1)
                for t in tiles:
                    s, n = TILES[t]
                    col = at + s - TILES[tiles[0]][0]
                    ins = pe.matmul(wk[:, col:col + n], tok_rstd[0:n, t:t + 1].to_broadcast([n, P]), ident[0:n, 0:n], start=True, stop=True)
                ins.then_inc(spread_mm, 1)

            pe.wait_ge(x_copied_act, 2)
            spread(0)

            def x_split(k):
                pe.wait_ge(x_lo, k + 1)

            column_tile(0, 0, act_hi, act_lo, before=x_split)
            column_tile(0, 1, act_hi, act_lo)
            pe.wait_ge(cache_k_in, 16)
            pe.wait_ge(rstd_ready, 1)
            for p in range(PAIRS):
                for t in range(4):
                    ins = tr(wk[:, 512 * p + P * t:512 * p + P * t + P], k_cache[:, t, P * p:P * p + P])
            ins.then_inc(kc_tr, 1)
            column_tile(0, 2, act_hi, act_lo)
            column_tile(0, 3, act_hi, act_lo)
            with pe.Fori(1, G_RET) as g:
                for j in range(4):
                    column_tile(g, j, act_hi, act_lo)

            pe.wait_ge(hankel_in, 16)
            pe.wait_ge(const_in, 32)
            pe.wait_ge(kc_ready, 1)
            for h in range(AH):
                for b in range(2):
                    ins = pe.matmul(wk[:, 256 * h + P * b:256 * h + P * b + P], hankel[:, h, P * (1 - b):P * (1 - b) + P], flip[:],
                                    start=True, stop=True)
            ins.then_inc(bias_mm, 1)

            def scores(i, e):
                def product(t, out, col, count):
                    s, n = TILES[t]
                    pe.matmul(wk[0:n, out:out + count], q_stack[:, e, s:s + n], k_stack_hi[:, col:col + count], start=True, stop=False)
                    return pe.matmul(wk[0:n, out:out + count], q_stack[:, e, s:s + n], k_stack_lo[:, col:col + count], start=False, stop=True)

                product(3, S_COL[3], CACHE, 4 * P)
                product(0, S_COL[0] - P, CACHE - P, 2 * P)
                product(2, S_COL[2], CACHE, 3 * P)
                if e:
                    pe.wait_ge(att_nat_ready, 2 * i + 1)
                product(1, S_COL[1], CACHE, 2 * P)
                product(4, S_COL[4], CACHE + SEQ, DEC)
                ins = product(4, S_COL[4] + DEC, 0, CACHE)
                ins.then_inc(scores_mm, 1)

            def probs_transposes(i, e, group):
                pe.wait_ge(probs_ready, 10 * i + 5 * e + (1, 3, 5)[group])
                for t in ((3,), (2, 0), (1, 4))[group]:
                    n = TILES[t][1]
                    for b in range(WIDTH[t] // P):
                        col = P_COL[t] + P * b + (DEC if t == 4 else 0)
                        ins = tr(wk[:, PT_COL[t] + n * b:PT_COL[t] + n * b + n], probs[0:n, col:col + P])
                    if t == 4:
                        ins = tr(wk[0:DEC, 1408:1440], probs[0:n, P_COL[t]:P_COL[t] + DEC])
                ins.then_inc(pT_mm, 1)

            def probs_times_v(i, e):
                for k, t in enumerate(ORDER):
                    n = TILES[t][1]
                    if k in (0, 1, 3):
                        pe.wait_ge((pT_a, pT_b, None, pT_c)[k], 2 * i + e + 1)
                    out = wk[0:n, 1536 + AD * t:1536 + AD * t + AD]
                    blocks = WIDTH[t] // P
                    for b in range(blocks):
                        v = v_nat[:, b, AD * e:AD * e + AD] if t < 4 else v_cache[:, b, AD * e:AD * e + AD]
                        ins = pe.matmul(out, probsT[:, PT_COL[t] + n * b:PT_COL[t] + n * b + n], v,
                                        start=(b == 0), stop=(t < 4 and b == blocks - 1))
                    if t == 4:
                        ins = pe.matmul(out, probsT[0:DEC, 1408:1440], v_nat[0:DEC, 4, AD * e:AD * e + AD], start=False, stop=True)
                ins.then_inc(pv_mm, 1)

            def to_natural(src, col):
                for t, (s, n) in enumerate(TILES):
                    ins = tr(wk[0:n, col + P * t:col + P * t + P], src[:, s:s + n])
                return ins

            with pe.Fori(0, PAIRS) as i:
                g = i + G_RET
                column_tile(g, 0, act_hi, act_lo)
                pe.wait_ge(pair_ready, i + 1)
                pe.wait_ge(bias_ready, 1)
                pe.wait_ge(attT_ready, i + 1)
                to_natural(k_pair, 0)
                to_natural(v_pair, 1024).then_inc(kv_tr, 1)
                column_tile(g, 1, act_hi, act_lo)
                pe.wait_ge(k_nat_ready, i + 1)
                pe.wait_ge(v_nat_ready, i + 1)
                pe.wait_ge(q_lo_ready, 2 * i + 2)
                pe.wait_ge(k_stacked, 2 * i + 1)
                scores(i, 0)

                def attend(e):
                    def before(k):
                        if k == KT - 2:
                            probs_transposes(i, e, 0)
                            probs_transposes(i, e, 1)
                        if k == KT - 1:
                            probs_transposes(i, e, 2)
                            probs_times_v(i, e)
                    return before

                pe.wait_ge(v_cache_in, 16 * i + 16)
                column_tile(g, 2, act_hi, act_lo, before=attend(0))
                pe.wait_ge(k_stacked, 2 * i + 2)
                scores(i, 1)
                column_tile(g, 3, act_hi, act_lo, before=attend(1))
                pe.wait_ge(att_nat_ready, 2 * i + 2)
                for t, (s, n) in enumerate(TILES):
                    ins = tr(wk[:, s:s + n], att_nat[0:n, t, :])
                ins.then_inc(att_tr, 1)

            with pe.Fori(0, RH) as i:
                g = i + G_GATE
                column_tile(g, 0, act_hi, act_lo)
                pe.wait_ge(ret_ready, i + 1)
                pe.wait_ge(retT_ready, i + 1)
                pe.wait_ge(attT_ready, PAIRS + 1)
                to_natural(rk, 0)
                to_natural(rv, 1024).then_inc(rkv_tr, 1)
                column_tile(g, 1, act_hi, act_lo)
                pe.wait_ge(q_rotated, i + 1)
                pe.wait_ge(rk_nat_ready, i + 1)
                pe.wait_ge(rv_nat_ready, i + 1)
                for t, (s, n) in enumerate(TILES):
                    pe.matmul(wk[0:n, s:s + n], rk[:, s:s + n], rq[:, s:s + n], start=True, stop=True)
                for t, (s, n) in enumerate(TILES):
                    ins = pe.matmul(wk[:, 1024 + RD * t:1024 + RD * t + RD], rk_nat[0:n, t, :], rv_nat[0:n, t, :], start=True, stop=True)
                ins.then_inc(ret_s_mm, 1)
                column_tile(g, 2, act_hi, act_lo)
                pe.wait_ge(ret_a_ready, i + 1)
                for t, (s, n) in enumerate(TILES):
                    out = wk[0:n, RD * t:RD * t + RD]
                    alone = t == 0
                    ins = pe.matmul(out, ret_a[0:n, s:s + n], rv_nat[0:n, t, :], start=True, stop=alone)
                    if t == 4:
                        ins = pe.matmul(out, rq[:, s:s + n], state_in[:, bass.ds(i, 1), :].rearrange("p a c -> p (a c)"), start=False, stop=True)
                    elif t:
                        ins = pe.matmul(out, rq[:, s:s + n], states[:, t - 1, :], start=False, stop=True)
                ins.then_inc(ret_o_mm, 1)
                column_tile(g, 3, act_hi, act_lo, half_used=h_half_used)
                for t, (s, n) in enumerate(TILES):
                    if t < 4:
                        pe.wait_ge(ret_n_ready, 5 * i + (1, 2, 3, 5)[t])
                    ins = tr(wk[:, 1024 + s:1024 + s + n], ret_n[0:n, t, :])
                ins.then_inc(ret_tr, 1)

            with pe.Fori(0, 2) as i:
                for j in range(4):
                    def branch_ready(k):
                        if k in (2, 3):
                            pe.wait_ge(in_lo_pool, k - 1)
                        else:
                            pe.wait_ge(in_lo, k + 1 if k < 2 else k - 1)
                    column_tile(i + G_MERGE, j, act_hi, act_lo, range(4), closes=False, before=branch_ready)
                    column_tile(i + G_MERGE, j, act_hi, act_lo, range(4, 8), dst=wk_halves[j % 2], opens=False, before=branch_ready)

            with pe.Fori(0, 2) as i:
                for j in range(4):
                    def merge_split(k):
                        pe.wait_ge(mid_lo_r, k + 1)
                    column_tile(i + G_WO, j, mid_hi, mid_lo, before=merge_split if j == 0 else None)
            feature_sum(1, squares_added(1, KT - 1), KT)
            spread(1)

            for k in range(KT):
                pe.wait_ge(h2_lo, k + 1)
                for j in range(2):
                    if k == 0:
                        pe.wait_ge(lo_ready, 4 * G_FFN + j + 1)
                        pe.wait_ge(acc_free, 4 * G_FFN + j + 1)
                    ins = products(acc[j], w_hi[:, j], w_lo[:, j], k, act_hi, act_lo, k == 0, k == KT - 1)
                    if k == KT - 1:
                        ins.then_inc(mm_done, 1)
            feature_sum(2, squares_added(2, KT - 1), 2 * KT)
            pe.wait_ge(lo_ready, 4 * G_FFN + 3)
            for k in range(KT):
                if k == 3:
                    spread(2)
                ins = products(wk_halves[1], w_hi_third, w_lo_third, k, act_hi, act_lo, k == 0, k == KT - 1)
            ins.then_inc(mm_done, 1)
            pe.wait_ge(acc_free, 4 * G_FFN + 4)
            column_tile(G_FFN, 3, act_hi, act_lo)

            def up(g):
                for j in range(4):
                    column_tile(g, j, act_hi, act_lo)

            def hidden_split(c):
                def before(k):
                    pe.wait_ge(f_lo, 8 * c + k + 3)
                return before

            def down(c):
                with pe.Fori(0, 2) as i:
                    for j in range(4):
                        column_tile(G_FFN + 2 + 4 * c + i, j, mid_hi, mid_lo, before=hidden_split(c) if j == 0 else None)

            up(G_FFN + 1)
            down(0)
            with pe.Fori(1, 3) as c:
                with pe.Fori(0, 2) as i:
                    up(G_FFN + 4 * c + i)
                down(c)
            with pe.Fori(0, 2) as i:
                up(G_FFN + 12 + i)
            for m in range(KT - 2):
                column_tile(G_FFN + 14 + m // 4, m % 4, mid_hi, mid_lo, before=hidden_split(3) if m == 0 else None)

            for part, (s, n) in enumerate(PARTS):
                for j in range(2):
                    if part == 0:
                        pe.wait_ge(lo_ready, 4 * (G_FFN + 15) + 3 + j)
                    for k in range(KT):
                        if part and j == 0 and k == 3:
                            feature_sum(3, squares_added(3, KT - 1), 3 * KT, PART_TILES[0])
                        if part and j == 0 and k == 6:
                            spread(3, PART_TILES[0], PART_RSTD[0])
                        dst = acc[j][:, part, 0:n]
                        pe.matmul(dst, w_hi[:, j, k, :], mid_hi[:, k, s:s + n], start=(k == 0), stop=False)
                        pe.matmul(dst, w_hi[:, j, k, :], mid_lo[:, k, s:s + n], start=False, stop=False)
                        ins = pe.matmul(dst, w_lo[:, j, k, :], mid_hi[:, k, s:s + n], start=False, stop=(k == KT - 1))
                    ins.then_inc(part_mm, 1)

            def transpose_out(part, p):
                for e, ready in enumerate((outT_even, outT_odd)):
                    pe.wait_ge(ready, 4 * part + p + 1)
                    if part and e == 0:
                        pe.wait_ge(out_nat, (3, 4, 4, 4)[p])
                    m = 2 * p + e
                    for t in PART_TILES[part]:
                        s, n = TILES[t]
                        if t < 4:
                            col = 2 * P * (t % 2) + P * e
                            ins = tr(out_psum(part, p)[:, col:col + P], y_ffn[:, m, s:s + n])
                        else:
                            col = P * (m % 4)
                            ins = tr(sample_psum(m // 4)[:, col:col + P], y_ffn[:, m, s:s + n])
                ins.then_inc(out_tr, 1)

            transpose_out(0, 0)
            feature_sum(4, squares_added(3, KT), 3 * KT + 2, PART_TILES[1])
            transpose_out(0, 1)
            transpose_out(0, 2)
            spread(4, PART_TILES[1], PART_RSTD[1])
            transpose_out(0, 3)
            for p in range(4):
                transpose_out(1, p)

        @block.vector
        def _(dve):
            order = Order(dve, dve_order)

            def copy(out, in_):
                return dve.tensor_scalar(out, in_, 1.0, None, ALU.mult)

            def split_lo(u, v):
                dve.wait_ge(hi_ready, u + 1)
                dve.tensor_tensor(w_lo[:, v % 2], w_raw[:, v // 2, :, P * (v % 2):P * (v % 2) + P],
                                  w_hi[:, v % 2].bitcast(fp), ALU.subtract).then_inc(lo_ready, 1)

            def split_ahead(g, j):
                split_lo(4 * g + j + 2, (j + 2) % 4)

            def to_z(g, j, slot):
                dve.wait_ge(mm_done, 4 * g + j + 1)
                dve.tensor_tensor(z[:, bass.ds(slot, 1), :].rearrange("p a (n c) -> p (a n) c", n=2),
                                  acc[j % 2][:, :, 0:HALF], halves(rstd[:]), ALU.mult).then_inc(acc_free, 1)

            dve.memset(tok_var[:], 1.0).then_inc(var_clear, 1)
            dve.wait_ge(var_clear, 1)

            def square_sum(t):
                n = TILES[t][1]
                dve.wait_ge(x_in[t], 16)
                order.after(dve.scalar_tensor_tensor(x_waste[0:n, 1, :], x_nat[0:n, t, :], 1.0, x_nat[0:n, t, :], ALU.mult, ALU.mult,
                                                     accum_out=tok_var[0:n, t:t + 1]))

            def copy_x(t):
                s, n = TILES[t]
                dve.wait_ge(x_tr, t + 1)
                dve.tensor_copy(xT[:, :, s:s + n], x_psum(t)).then_inc(x_copied_dve, 1)

            square_sum(0)
            square_sum(2)
            copy_x(1)
            square_sum(4)
            dve.wait_ge(x_sum_act, 2)
            dve.tensor_scalar(tok_var[:, 0:5], tok_var[:, 0:5], 1.0 / D, EPS, ALU.mult, ALU.add).then_inc(var_ready, 1)
            copy_x(3)
            dve.wait_ge(std_ready, 1)
            dve.reciprocal(tok_rstd[:, 0:5], tok_rstd[:, 0:5]).then_inc(tok_rstd_ready, 1)
            split_lo(0, 0)
            for k in range(KT):
                dve.wait_ge(x_hi, k + 1)
                dve.scalar_tensor_tensor(act_lo[:, k, :], xT[:, k, :], gains[:, 0, k:k + 1], act_hi[:, k, :].bitcast(fp),
                                         ALU.mult, ALU.subtract).then_inc(x_lo, 1)
            split_lo(1, 1)
            dve.wait_ge(spread_mm, 1)
            dve.tensor_copy(rstd[:], wk[:, 0:T]).then_inc(rstd_ready, 1)
            dve.wait_ge(rstd_ready, 1)

            def norm(n, between=None, keep=False, tiles=range(5)):
                cols, (a, b) = slice(tiles[0], tiles[-1] + 1), (SUM_COL + tiles[0], SUM_COL + tiles[-1] + 1)
                dve.wait_ge(sum_mm, n)
                order.after(dve.tensor_scalar(tok_last[:, cols], wk[:, a + 5:b + 5], 1.0 / D, EPS, ALU.mult, ALU.add))
                dve.scalar_tensor_tensor(tok_var[:, cols], wk[:, a:b], 1.0 / D, tok_last[:, cols], ALU.mult, ALU.add).then_inc(var_ready, 1)
                dve.wait_ge(std_ready, n + 1)
                dve.reciprocal(tok_rstd[:, cols], tok_rstd[:, cols]).then_inc(tok_rstd_ready, 1)
                if between:
                    between()
                dve.wait_ge(spread_mm, n + 1)
                if keep:
                    order.after(dve.tensor_copy(rstd[:], wk[:, 0:T]))

            order.flatten()

            with dve.Fori(0, G_RET) as g:
                for j in range(4):
                    to_z(g, j, 4 * g + j)
                    split_ahead(g, j)

            dve.wait_ge(bias_mm, 1)
            order.after(dve.tensor_tensor(bias[:], wk[:].rearrange("p (h c) -> p h c", h=AH),
                                          hankel[:, :, 2 * P - 1:2 * P].to_broadcast([P, AH, 2 * P]), ALU.subtract))
            dve.memset(bias[0:AD, :, P + AD:2 * P], NEG).then_inc(bias_ready, 1)
            order.flatten()

            def keys_low(i, e):
                rows = slice(AD * e, AD * e + AD)
                dve.wait_ge(k_hi_ready, 2 * i + e + 1)
                dve.tensor_tensor(k_stack_lo[rows, CACHE:], k_pair[rows, :], k_stack_hi[rows, CACHE:].bitcast(fp), ALU.subtract)
                dve.tensor_tensor(k_stack_lo[rows, 0:CACHE], kcT[rows, bass.ds(i, 1), :].rearrange("p a c -> p (a c)"),
                                  k_stack_hi[rows, 0:CACHE].bitcast(fp), ALU.subtract).then_inc(k_lo_ready, 1)

            def masked_max(i, e):
                h = 2 * i + e
                dve.wait_ge(scores_mm, h + 1)
                for group, tiles in enumerate(((3,), (2, 0), (1, 4))):
                    for t in tiles:
                        n = TILES[t][1]
                        spans = [(*NEAR[t], P if t == 0 else 0)] if t < 4 else [(CACHE + DEC - P, P, 0), (0, DEC, P)]
                        for c, w, b in spans:
                            near = wk[0:n, S_COL[t] + c:S_COL[t] + c + w]
                            ins = dve.tensor_tensor(near, near, bias[0:n, bass.ds(h, 1), b:b + w].rearrange("p a c -> p (a c)"), ALU.add)
                    order.after(ins)
                    for t in tiles:
                        n = TILES[t][1]
                        ins = dve.tensor_reduce(neg_max[0:n, t:t + 1], wk[0:n, S_COL[t]:S_COL[t] + WIDTH[t]], AX.X, ALU.max, negate=True)
                    ins.then_inc(max_ready, 1)

            def probsT_copies(i, e):
                dve.wait_ge(pT_mm, 6 * i + 3 * e + 1)
                dve.tensor_copy(probsT[:, 0:512], wk[:, 0:512]).then_inc(pT_a, 1)
                if e == 0:
                    keys_low(i, 1)
                dve.wait_ge(pT_mm, 6 * i + 3 * e + 3)
                dve.tensor_copy(probsT[:, 1024:1408], wk[:, 1024:1408])
                dve.tensor_copy(probsT[0:DEC, 1408:1440], wk[0:DEC, 1408:1440]).then_inc(pT_c, 1)

            def att_to_natural(i, e):
                dve.wait_ge(probs_ready, 10 * i + 5 * e + 5)
                dve.reciprocal(row_inv[:, 0:4], row_sum[:, 0:4])
                order.after(dve.reciprocal(row_inv[0:DEC, 4:5], row_sum[0:DEC, 4:5]))
                dve.wait_ge(pv_mm, 2 * i + e + 1)
                dve.tensor_tensor(att_nat[:, 0:4, AD * e:AD * e + AD], wk[:, 1536:1792].rearrange("p (t c) -> p t c", t=4),
                                  row_inv[:, 0:4].unsqueeze(2).to_broadcast([P, 4, AD]), ALU.mult)
                dve.tensor_scalar(att_nat[0:DEC, 4, AD * e:AD * e + AD], wk[0:DEC, 1792:1856], row_inv[0:DEC, 4:5], None, ALU.mult)\
                    .then_inc(att_nat_ready, 1)

            with dve.Fori(0, PAIRS) as i:
                g = i + G_RET
                order.body(i, 8)
                copy(k_pair[:], z[:, bass.ds(Z_AK + i, 1), :].rearrange("p a c -> p (a c)"))
                copy(v_pair[:], z[:, bass.ds(Z_AV + i, 1), :].rearrange("p a c -> p (a c)")).then_inc(pair_ready, 1)
                for e in range(2):
                    rows, others = slice(AD * e, AD * e + AD), slice(AD - AD * e, 2 * AD - AD * e)
                    dve.wait_ge(q_hi_ready, 2 * i + e + 1)
                    dve.scalar_tensor_tensor(q_stack[others, e, :], z[rows, bass.ds(i, 1), :].rearrange("p a c -> p (a c)"), AD ** -0.5,
                                             q_stack[rows, e, :].bitcast(fp), ALU.mult, ALU.subtract).then_inc(q_lo_ready, 1)
                keys_low(i, 0)
                to_z(g, 0, Z_RQ + 4 * i)
                split_ahead(g, 0)
                dve.wait_ge(kv_tr, i + 1)
                dve.wait_ge(k_out, 32 * i + 32)
                dve.tensor_copy(k_nat[:, 0:4, :], wk[:, 0:512].rearrange("p (t c) -> p t c", t=4))
                dve.tensor_copy(k_nat[0:DEC, 4, :], wk[0:DEC, 512:640]).then_inc(k_nat_ready, 1)
                to_z(g, 1, Z_RQ + 4 * i + 1)
                masked_max(i, 0)
                probsT_copies(i, 0)
                split_ahead(g, 1)
                att_to_natural(i, 0)
                to_z(g, 2, Z_RQ + 4 * i + 2)
                masked_max(i, 1)
                split_ahead(g, 2)
                probsT_copies(i, 1)
                att_to_natural(i, 1)
                dve.wait_ge(att_tr, i + 1)
                copy(z[:, bass.ds(i, 1), :].rearrange("p a c -> p (a c)"), wk[:, 0:T]).then_inc(attT_ready, 1)
                to_z(g, 3, Z_RQ + 4 * i + 3)
                split_ahead(g, 3)
            order.leave(PAIRS)

            dve.wait_ge(ret_const_in, 48)
            dve.wait_ge(k_out, 32 * PAIRS + 32)
            dve.wait_ge(v_out, 32 * PAIRS + 32)

            def branch_low(k):
                dve.wait_ge(in_hi, k + 1)
                dve.tensor_tensor(act_lo[:, k, :], z[:, k if k < 4 else Z_RQ + k - 4, :], act_hi[:, k, :].bitcast(fp), ALU.subtract)\
                    .then_inc(in_lo, 1)

            def retention(i, last=False):
                g = i + G_GATE

                def row(slot, frm=0, to=P):
                    return z[frm:to, bass.ds(slot, 1), :].rearrange("p a c -> p (a c)")

                copy(rq[:], row(Z_RQ + i)).then_inc(q_copied, 1)
                copy(head_c[:], decay[:, bass.ds(i, 1), :].rearrange("p a c -> p (a c)"))
                for to, frm in ((0, RD // 2), (RD // 2, 0)):
                    dve.tensor_tensor(rope_k[to:to + RD // 2, :], row(Z_RK + i, frm, frm + RD // 2), rope[frm:frm + RD // 2, 1, :], ALU.mult)
                order.after(dve.tensor_tensor(rk[:], row(Z_RK + i), rope[:, 0, :], ALU.mult))
                dve.tensor_tensor(rk[:], rk[:], rope_k[:], ALU.add)
                copy(rv[:], row(Z_RV + i)).then_inc(ret_ready, 1)
                copy(gate_row[:], row(Z_RG + i)).then_inc(gate_copied, 1)
                to_z(g, 0, Z_GATE + 4 * i)
                split_ahead(g, 0)
                dve.wait_ge(rkv_tr, i + 1)
                dve.tensor_scalar(rk_nat[:, 0:4, :], wk[:, 0:512].rearrange("p (t c) -> p t c", t=4), head_c[:, P + 1:P + 2], None, ALU.mult)
                dve.tensor_scalar(rk_nat[0:DEC, 4, :], wk[0:DEC, 512:640], head_c[0:DEC, P + 2:P + 3], None, ALU.mult).then_inc(rk_nat_ready, 1)
                to_z(g, 1, Z_GATE + 4 * i + 1)
                split_ahead(g, 1)
                dve.wait_ge(ret_s_mm, i + 1)
                dve.wait_ge(state_out, 32 * i + 32)
                dve.tensor_tensor(ret_a[:, 0:SEQ].rearrange("p (t c) -> p t c", t=4), wk[:, 0:SEQ].rearrange("p (t c) -> p t c", t=4),
                                  head_c[:, 0:P].unsqueeze(1).to_broadcast([P, 4, P]), ALU.mult)
                dve.tensor_tensor(ret_a[0:DEC, SEQ:T], wk[0:DEC, SEQ:T], head_c[0:DEC, 0:DEC], ALU.mult)
                order.after(dve.tensor_copy(states[:, 0, :], wk[:, 1024:1024 + RD]))
                for t in range(1, 4):
                    order.after(dve.scalar_tensor_tensor(states[:, t, :], states[:, t - 1, :], head_c[:, P + 3:P + 4],
                                                         wk[:, 1024 + RD * t:1024 + RD * t + RD], ALU.mult, ALU.add))
                dve.scalar_tensor_tensor(state_new[:], state_in[:, bass.ds(i, 1), :].rearrange("p a c -> p (a c)"), head_c[:, P + 4:P + 5],
                                         wk[:, 1536:1536 + RD], ALU.mult, ALU.add).then_inc(ret_a_ready, 1)
                to_z(g, 2, Z_GATE + 4 * i + 2)
                dve.wait_ge(ret_o_mm, i + 1)
                dve.tensor_scalar(ret_o[:, 0:4, :], wk[:, 0:SEQ].rearrange("p (t c) -> p t c", t=4), head_c[:, P:P + 1], None, ALU.mult)
                order.after(dve.tensor_scalar(ret_o[0:DEC, 4, :], wk[0:DEC, SEQ:SEQ + RD], head_c[0:DEC, P:P + 1], None, ALU.mult))
                for t in range(4):
                    ins = dve.bn_stats(gn_stats[:, t, :], ret_o[:, t, :])
                order.after(ins)
                dve.bn_stats(gn_stats[0:DEC, 4, :], ret_o[0:DEC, 4, :])
                for t in range(4):
                    ins = dve.bn_aggr(gn_mv[:, t, :], gn_stats[:, t, :])
                order.after(ins)
                dve.tensor_scalar(gn_std[:, 0:4], gn_mv[:, 0:4, 1], EPS, None, ALU.add)
                order.after(dve.bn_aggr(gn_mv[0:DEC, 4, :], gn_stats[0:DEC, 4, :]))
                dve.tensor_scalar(gn_std[0:DEC, 4:5], gn_mv[0:DEC, 4, 1:2], EPS, None, ALU.add).then_inc(gn_var, 1)
                dve.wait_ge(gn_root, i + 1)
                dve.reciprocal(gn_rstd[:, 0:4], gn_std[:, 0:4])
                order.after(dve.reciprocal(gn_rstd[0:DEC, 4:5], gn_std[0:DEC, 4:5]))
                for t, (s, n) in enumerate(TILES):
                    dve.tensor_scalar(ret_n[0:n, t, :], ret_o[0:n, t, :], gn_mv[0:n, t, 0:1], gn_rstd[0:n, t:t + 1],
                                      ALU.subtract, ALU.mult).then_inc(ret_n_ready, 1)
                split_ahead(g, 2)
                if last:
                    for k in (0, 1, 4, 5):
                        branch_low(k)
                else:
                    to_z(g, 3, Z_GATE + 4 * i + 3)
                    split_ahead(g, 3)
                dve.wait_ge(ret_tr, i + 1)
                dve.wait_ge(swish_ready, i + 1)
                dve.tensor_tensor(z[:, bass.ds(Z_RQ + i, 1), :].rearrange("p a c -> p (a c)"), wk[:, 1024:1024 + T],
                                  gate_row[:], ALU.mult).then_inc(retT_ready, 1)
                if last:
                    branch_low(6)
                    branch_low(7)
                    to_z(g, 3, Z_GATE + 4 * i + 3)
                    split_ahead(g, 3)

            with dve.Fori(0, RH - 1) as i:
                order.body(i, 10)
                retention(i)
            order.leave(RH - 1)
            retention(RH - 1, last=True)

            with dve.Fori(0, 2) as i:
                for j in range(4):
                    m = 4 * i + j
                    dve.wait_ge(gates_ready, m + 1)
                    dve.wait_ge(mm_done, 4 * G_MERGE + m + 1)
                    dve.tensor_tensor(halves(part_a[:]), acc[j % 2][:, :, 0:HALF],
                                      z[:, bass.ds(Z_GATE + m, 1), :].rearrange("p a (n c) -> p (a n) c", n=2), ALU.mult)
                    ins = dve.tensor_tensor(halves(part_b[:]), wk_halves[j % 2][:, :, 0:HALF],
                                            z[:, bass.ds(Z_GATE + KT + m, 1), :].rearrange("p a (n c) -> p (a n) c", n=2), ALU.mult)
                    ins.then_inc(acc_free, 1)
                    evacuated(dve, i + G_MERGE, j)
                    dve.tensor_tensor(merged[:, j % 2, :], part_a[:], part_b[:], ALU.add).then_inc(merge_ready, 1)
                    split_ahead(i + G_MERGE, j)
                    dve.wait_ge(mid_hi_r, m + 1)
                    dve.tensor_tensor(mid_lo[:, bass.ds(m, 1), :].rearrange("p a c -> p (a c)"), merged[:, j % 2, :],
                                      mid_hi[:, bass.ds(m, 1), :].rearrange("p a c -> p (a c)").bitcast(fp), ALU.subtract).then_inc(mid_lo_r, 1)

            def third_low():
                dve.wait_ge(hi_ready, 4 * G_FFN + 3)
                dve.tensor_tensor(w_lo_third[:], w_raw[:, 1, :, 0:P], w_hi_third[:].bitcast(fp), ALU.subtract).then_inc(lo_ready, 1)

            with dve.Fori(0, 2) as i:
                for j in range(4):
                    dve.wait_ge(mm_done, 4 * (i + G_WO) + j + 1)
                    copy(y_mix[:, bass.ds(4 * i + j, 1), :].rearrange("p a (n c) -> p (a n) c", n=2), acc[j % 2][:, :, 0:HALF])\
                        .then_inc(acc_free, 1)
                    split_ahead(i + G_WO, j)
            norm(1, between=third_low)

            def add_normalised(out, y, gain, used, even, tokens=(0, T), at=0, done=0):
                s, n = tokens

                def scale(p, e):
                    return dve.scalar_tensor_tensor(scaled[:, 2 * (p % 2) + e, s:s + n], y[:, 2 * p + e, s:s + n],
                                                    gains[:, gain, 2 * p + e:2 * p + e + 1], wk[:, at:at + n], ALU.mult, ALU.mult)

                def pair(p, between=None):
                    if done + p >= 2:
                        dve.wait_ge(used, done + p - 1)
                        dve.wait_ge(even, done + p - 1)
                    if p:
                        scale(p, 1).then_inc(scaled_ready, 1)
                    if between:
                        between()
                    order.after(scale(p, 0))
                    dve.tensor_tensor(out[:, 2 * p, s:s + n], xT[:, 2 * p, s:s + n], scaled[:, 2 * (p % 2), s:s + n], ALU.add).then_inc(even, 1)
                    if p == 0:
                        scale(p, 1).then_inc(scaled_ready, 1)
                return pair

            def h2_low(m):
                dve.wait_ge(h2_hi, m + 1)
                dve.scalar_tensor_tensor(act_lo[:, m, :], xT[:, m, :], gains[:, 2, m:m + 1], act_hi[:, m, :].bitcast(fp),
                                         ALU.mult, ALU.subtract).then_inc(h2_lo, 1)

            pair = add_normalised(xT, y_mix, 1, x1_odd, x1_even)
            pair(0)
            h2_low(0)
            for p in range(1, KT // 2):
                pair(p, between=(lambda: h2_low(2 * p - 2)) if p > 1 else None)
                h2_low(2 * p - 1)
            h2_low(KT - 2)
            h2_low(KT - 1)
            norm(2, between=lambda: split_ahead(G_FFN, 1), keep=True)

            def up(g, chunk, i, first=False):
                def evacuate(j):
                    dve.wait_ge(mm_done, 4 * g + j + 1)
                    src = wk_halves[1] if first and j == 2 else acc[j % 2]
                    dve.scalar_tensor_tensor(halves(relu[:, j % 2, :]), src[:, :, 0:HALF], 0.0, halves(rstd[:]),
                                             ALU.max, ALU.mult).then_inc(acc_free, 1)

                def hidden_low(j):
                    dve.wait_ge(f_hi, 8 * chunk + 4 * i + j + 1)
                    dve.tensor_tensor(mid_lo[:, bass.ds(4 * i + j, 1), :].rearrange("p a c -> p (a c)"), relu2[:, j % 2, :],
                                      mid_hi[:, bass.ds(4 * i + j, 1), :].rearrange("p a c -> p (a c)").bitcast(fp), ALU.subtract).then_inc(f_lo, 1)

                if first:
                    evacuate(0)
                    evacuate(1)
                    hidden_low(0)
                    hidden_low(1)
                for j in range(2 if first else 0, 4):
                    evacuate(j)
                    split_ahead(g, j)
                    hidden_low(j)

            def down_tile(g, j, m):
                dve.wait_ge(mm_done, 4 * g + j + 1)
                y = y_ffn[:, bass.ds(m, 1), :].rearrange("p a (n c) -> p (a n) c", n=2)
                dve.tensor_tensor(y, y, acc[j % 2][:, :, 0:HALF], ALU.add).then_inc(acc_free, 1)
                split_ahead(g, j)

            def down(g):
                with dve.Fori(0, 2) as i:
                    for j in range(4):
                        down_tile(g + i, j, 4 * i + j)

            dve.wait_ge(y_zero, 1)
            up(G_FFN, 0, 0, first=True)
            up(G_FFN + 1, 0, 1)
            down(G_FFN + 2)
            with dve.Fori(1, 3) as c:
                with dve.Fori(0, 2) as i:
                    up(G_FFN + 4 * c + i, c, i)
                down(G_FFN + 2 + 4 * c)
            with dve.Fori(0, 2) as i:
                up(G_FFN + 12 + i, 3, i)
            for m in range(KT - 2):
                down_tile(G_FFN + 14 + m // 4, m % 4, m)

            def down_part(part, j):
                s, n = PARTS[part]
                dve.wait_ge(part_mm, 2 * part + j + 1)
                dve.tensor_tensor(y_ffn[:, 6 + j, s:s + n], y_ffn[:, 6 + j, s:s + n], acc[j][:, part, 0:n], ALU.add).then_inc(part_read, 1)

            first_pair, second_pair = (add_normalised(y_ffn, y_ffn, 3, outT_odd, outT_even, PARTS[part], PART_RSTD[part], 4 * part)
                                       for part in range(2))
            down_part(0, 0)
            down_part(0, 1)
            norm(3, tiles=PART_TILES[0])
            first_pair(0)
            first_pair(1)
            down_part(1, 0)
            first_pair(2)
            down_part(1, 1)
            first_pair(3)
            norm(4, tiles=PART_TILES[1])
            for p in range(KT // 2):
                second_pair(p)


_INS = ['x_prompt', 'x_sample', 'cache_attn_k', 'cache_attn_v', 'state_retention', 'w_in', 'rel_bias_table',
        'w_attn_out', 'w_ret_out', 'w_o', 'w_ff_up', 'w_ff_down']
_GAINS = ['norm_mix_pre', 'norm_mix_post', 'norm_ffn_pre', 'norm_ffn_post']
_OUTS = [("y_prompt", (1, SEQ, D)), ("y_sample", (1, DEC, D)), ("new_k_prompt", (SEQ, AH * AD)), ("new_v_prompt", (SEQ, AH * AD)),
         ("new_state_prompt", (RH, RD, RD)), ("new_k_sample", (DEC, AH * AD)), ("new_v_sample", (DEC, AH * AD)),
         ("new_state_sample", (RH, RD, RD))]


def kernel(**inputs):
    import concourse.bacc as bacc
    from concourse.bass_utils import run_bass_kernel_spmd

    nc = bacc.Bacc("TRN2", target_bir_lowering=False, num_devices=1)
    arrays = {}
    for name in _INS:
        a = np.ascontiguousarray(inputs[name])
        if name.startswith("cache"):
            a = a.reshape(CACHE, AH * AD)
        elif name.startswith("state"):
            a = a.reshape(RH, RD, RD)
        elif not name.startswith("x_"):
            a = a[0]
        arrays[name] = a
    arrays["gains"] = np.ascontiguousarray(np.stack([np.asarray(inputs[n])[0].reshape(KT, P).T for n in _GAINS], axis=1))
    arrays.update(shape_constants())
    args = {n: nc.dram_tensor("in_" + n, a.shape, mybir.dt.from_np(a.dtype), kind="ExternalInput").ap() for n, a in arrays.items()}
    outs = {n: nc.dram_tensor("out_" + n, s, mybir.dt.float32, kind="ExternalOutput").ap() for n, s in _OUTS}
    build(nc, args, outs)
    r = run_bass_kernel_spmd(nc, [{"in_" + n: a for n, a in arrays.items()}], core_ids=[0]).results[0]
    y_p, y_s, k_p, v_p, s_p, k_s, v_s, s_s = (r["out_" + n] for n, _ in _OUTS)
    heads = (1, 1, -1, AH, AD)
    return (y_p, y_s, k_p.reshape(heads), v_p.reshape(heads), s_p.reshape(1, 1, RH, RD, RD),
            k_s.reshape(heads), v_s.reshape(heads), s_s.reshape(1, 1, RH, RD, RD))
```
